# Optimizing a Trainium2 kernel written in Bass

```python
import jax, jax.numpy as jnp
from jax import lax
import numpy as np

D_MODEL = 1024
BATCH = 1
SEQ = 512
DEPTH = 2

HEAD_DIM = 64
BLK = 128
NEG = -1e30
RMS_EPS = 1e-6
FOX_HEADS = 8
DIL_HEADS = 8
DIL_BRANCHES = ((128, 1), (512, 4), (2048, 16))
MLA_HEADS = 8
MLA_Q_RANK = 384
MLA_KV_RANK = 256
MLA_NOPE = 64
MLA_ROPE = 32
MLA_V = 64
ROPE_THETA = 10000.0
SWA_Q_HEADS = 8
SWA_KV_HEADS = 2
SWA_WINDOW = 128
N_GROUPS = 4
EXPERTS_PER_GROUP = 8
N_EXPERTS = N_GROUPS * EXPERTS_PER_GROUP
EXPERT_TOPK = 2
D_EXPERT = 256

EVEN_SPLIT = [FOX_HEADS * HEAD_DIM] * 3 + [FOX_HEADS] + [DIL_HEADS * HEAD_DIM] * 3
EVEN_IN = sum(EVEN_SPLIT)
EVEN_MIX = (FOX_HEADS + DIL_HEADS) * HEAD_DIM
ODD_SPLIT = [MLA_Q_RANK, MLA_KV_RANK, MLA_ROPE, SWA_Q_HEADS * HEAD_DIM, SWA_KV_HEADS * HEAD_DIM, SWA_KV_HEADS * HEAD_DIM]
ODD_IN = sum(ODD_SPLIT)
ODD_MIX = MLA_HEADS * MLA_V + SWA_Q_HEADS * HEAD_DIM
N_EVEN = (DEPTH + 1) // 2
N_ODD = DEPTH // 2

kernel_name = "hybrid_fox_dilated_mla_swa_hmoe"

F32 = jnp.float32

def rmsnorm(x, g):
    xf = x.astype(F32)
    y = xf * lax.rsqrt(jnp.mean(xf * xf, axis=-1, keepdims=True) + RMS_EPS)
    return (y * g.astype(F32)).astype(x.dtype)

def split_cols(z, sizes):
    idx = [int(v) for v in np.cumsum(sizes)[:-1]]
    return jnp.split(z, idx, axis=-1)

def to_heads(t, n):
    b, s, _ = t.shape
    return t.reshape(b, s, n, -1).transpose(0, 2, 1, 3)

def from_heads(o):
    b, h, s, e = o.shape
    return o.transpose(0, 2, 1, 3).reshape(b, s, h * e)

def alibi_slopes(n):
    return jnp.exp2(-8.0 * jnp.arange(1, n + 1, dtype=F32) / n)

def rope_tables(s):
    inv = ROPE_THETA ** (-jnp.arange(0, MLA_ROPE, 2, dtype=F32) / MLA_ROPE)
    ang = jnp.arange(s, dtype=F32)[:, None] * inv[None, :]
    return jnp.cos(ang), jnp.sin(ang)

def apply_rope(t, cos, sin):
    half = t.shape[-1] // 2
    t1, t2 = t[..., :half].astype(F32), t[..., half:].astype(F32)
    return jnp.concatenate([t1 * cos - t2 * sin, t1 * sin + t2 * cos], axis=-1).astype(t.dtype)

def causal_block_sweep(block_scores, v):
    b, h, s, e = v.shape
    kpos = jnp.arange(s)
    vf = v.astype(F32)

    def one(i):
        sc = block_scores(i)
        qpos = i * BLK + jnp.arange(BLK)
        sc = jnp.where(kpos[None, :] <= qpos[:, None], sc, NEG)
        p = jax.nn.softmax(sc, axis=-1)
        return jnp.einsum("bhqk,bhke->bhqe", p, vf)

    out = lax.map(one, jnp.arange(s // BLK))
    return out.transpose(1, 2, 0, 3, 4).reshape(b, h, s, e).astype(v.dtype)

def banded_attention(q, k, v, max_steps, step_dist, slopes, sinks=None):
    n, hk, g, L, e = q.shape
    nb = L // BLK
    qb = q.reshape(n, hk, g, nb, BLK, e)

    def with_prev(t):
        t = t.reshape(n, hk, nb, BLK, e)
        prev = jnp.concatenate([jnp.zeros_like(t[:, :, :1]), t[:, :, :-1]], axis=2)
        return jnp.concatenate([prev, t], axis=3)

    kc, vc = with_prev(k), with_prev(v)
    s = jnp.einsum("nhgbqe,nhbke->nhgbqk", qb, kc, preferred_element_type=F32) * (e ** -0.5)
    steps = (jnp.arange(BLK)[:, None] + BLK) - jnp.arange(2 * BLK)[None, :]
    in_band = (steps >= 0) & (steps <= max_steps)
    has_prev = (jnp.arange(nb)[:, None, None] > 0) | (jnp.arange(2 * BLK)[None, None, :] >= BLK)
    mask = in_band[None] & has_prev
    dist = (steps * step_dist).astype(F32)
    s = s - slopes.astype(F32)[None, :, :, None, None, None] * dist
    s = jnp.where(mask, s, NEG)
    m = s.max(axis=-1)
    if sinks is not None:
        sk = sinks.astype(F32)[None, :, :, None, None]
        m = jnp.maximum(m, sk)
    p = jnp.exp(s - m[..., None])
    den = p.sum(axis=-1)
    if sinks is not None:
        den = den + jnp.exp(sk - m)
    o = jnp.einsum("nhgbqk,nhbke->nhgbqe", p, vc.astype(F32)) / den[..., None]
    lse = m + jnp.log(den)
    return o.reshape(n, hk, g, L, e).astype(q.dtype), lse.reshape(n, hk, g, L)

def forgetting_attention(q, k, v, log_f):
    c = jnp.cumsum(log_f, axis=-1)
    scale = q.shape[-1] ** -0.5

    def scores(i):
        qi = lax.dynamic_slice_in_dim(q, i * BLK, BLK, axis=2)
        ci = lax.dynamic_slice_in_dim(c, i * BLK, BLK, axis=2)
        sc = jnp.einsum("bhqe,bhke->bhqk", qi, k, preferred_element_type=F32) * scale
        return sc + ci[..., None] - c[:, :, None, :]

    return causal_block_sweep(scores, v)

def dilated_branch(q, k, v, window, dil, slopes):
    b, h, s, e = q.shape
    L = s // dil
    Lp = -(-L // BLK) * BLK

    def split(t):
        t = t.reshape(b, h, L, dil, e).transpose(0, 3, 1, 2, 4).reshape(b * dil, h, L, e)
        return jnp.pad(t, ((0, 0), (0, 0), (0, Lp - L), (0, 0)))

    o, lse = banded_attention(split(q)[:, :, None], split(k), split(v), window // dil, dil, slopes[:, None])
    o = o[:, :, 0, :L].reshape(b, dil, h, L, e).transpose(0, 2, 3, 1, 4).reshape(b, h, s, e)
    lse = lse[:, :, 0, :L].reshape(b, dil, h, L).transpose(0, 2, 3, 1).reshape(b, h, s)
    return o, lse

def dilated_attention(q, k, v, slopes):
    res = [dilated_branch(q, k, v, w, d, slopes) for (w, d) in DIL_BRANCHES]
    outs = jnp.stack([r[0] for r in res]).astype(F32)
    wts = jax.nn.softmax(jnp.stack([r[1] for r in res]), axis=0)
    return jnp.einsum("rbhs,rbhse->bhse", wts, outs).astype(q.dtype)

def even_mixer(hn, w_in, b_f, w_out, dil_slopes):
    zq, zk, zv, zf, dq, dk, dv = split_cols(hn @ w_in, EVEN_SPLIT)
    log_f = jax.nn.log_sigmoid((zf + b_f).astype(F32)).transpose(0, 2, 1)
    o_a = forgetting_attention(to_heads(zq, FOX_HEADS), to_heads(zk, FOX_HEADS), to_heads(zv, FOX_HEADS), log_f)
    o_b = dilated_attention(to_heads(dq, DIL_HEADS), to_heads(dk, DIL_HEADS), to_heads(dv, DIL_HEADS), dil_slopes)
    o = jnp.concatenate([o_a, o_b.astype(o_a.dtype)], axis=1)
    return from_heads(o) @ w_out

def odd_mixer(hn, w_in, q_norm, kv_norm, w_uq, w_ukv, sinks, w_out, cos, sin, swa_slopes):
    b, s, _ = hn.shape
    c_q, c_kv, k_pe, q_s, k_s, v_s = split_cols(hn @ w_in, ODD_SPLIT)
    q = to_heads(rmsnorm(c_q, q_norm) @ w_uq, MLA_HEADS)
    q_nope, q_pe = q[..., :MLA_NOPE], apply_rope(q[..., MLA_NOPE:], cos, sin)
    kv = to_heads(rmsnorm(c_kv, kv_norm) @ w_ukv, MLA_HEADS)
    k_nope, v_c = kv[..., :MLA_NOPE], kv[..., MLA_NOPE:]
    k_pe = apply_rope(k_pe, cos, sin)
    scale = (MLA_NOPE + MLA_ROPE) ** -0.5

    def mla_scores(i):
        qn = lax.dynamic_slice_in_dim(q_nope, i * BLK, BLK, axis=2)
        qp = lax.dynamic_slice_in_dim(q_pe, i * BLK, BLK, axis=2)
        sc = jnp.einsum("bhqe,bhke->bhqk", qn, k_nope, preferred_element_type=F32)
        sc = sc + jnp.einsum("bhqr,bkr->bhqk", qp, k_pe, preferred_element_type=F32)
        return sc * scale

    o_c = causal_block_sweep(mla_scores, v_c)
    grp = SWA_Q_HEADS // SWA_KV_HEADS
    qd = to_heads(q_s, SWA_Q_HEADS).reshape(b, SWA_KV_HEADS, grp, s, HEAD_DIM)
    o_d, _ = banded_attention(qd, to_heads(k_s, SWA_KV_HEADS), to_heads(v_s, SWA_KV_HEADS),
                              SWA_WINDOW - 1, 1, swa_slopes, sinks.reshape(SWA_KV_HEADS, grp))
    o_d = o_d.reshape(b, SWA_Q_HEADS, s, HEAD_DIM)
    o = jnp.concatenate([o_c, o_d.astype(o_c.dtype)], axis=1)
    return from_heads(o) @ w_out

def hierarchical_moe(hn, w_group, b_group, w_router, b_router, w_gate, w_up, w_down):
    b, s, d = hn.shape
    t = hn.reshape(-1, d)
    g_logits = (t @ w_group + b_group).astype(F32)
    g_prob = jax.nn.softmax(g_logits, axis=-1)
    g_idx = jnp.argmax(g_logits, axis=-1)
    g_w = jnp.take_along_axis(g_prob, g_idx[:, None], axis=-1)[:, 0]
    e_logits = (t @ w_router + b_router).astype(F32).reshape(-1, N_GROUPS, EXPERTS_PER_GROUP)
    e_sel = jnp.take_along_axis(e_logits, g_idx[:, None, None], axis=1)[:, 0]
    top_v, top_i = lax.top_k(e_sel, EXPERT_TOPK)
    top_w = jax.nn.softmax(top_v, axis=-1) * g_w[:, None]
    expert_id = g_idx[:, None] * EXPERTS_PER_GROUP + top_i
    gates = jnp.sum(jax.nn.one_hot(expert_id, N_EXPERTS, dtype=F32) * top_w[..., None], axis=1)
    gates = gates.reshape(-1, N_GROUPS, EXPERTS_PER_GROUP)
    y = jnp.zeros((t.shape[0], d), F32)
    for grp in range(N_GROUPS):
        a = jnp.einsum("nd,edf->nef", t, w_gate[grp])
        u = jnp.einsum("nd,edf->nef", t, w_up[grp])
        act = jax.nn.silu(a) * u * gates[:, grp, :, None]
        y = y + jnp.einsum("nef,efd->nd", act, w_down[grp])
    return y.reshape(b, s, d).astype(hn.dtype)

def setup_inputs(seed: int = 0) -> dict:
    key = jax.random.key(seed)
    ks = jax.random.split(key, 24)

    def nrm(k, shape, scale):
        return scale * jax.random.normal(k, shape, F32)

    def gain(k, shape):
        return 1.0 + 0.01 * jax.random.normal(k, shape, F32)

    return {
        "x": nrm(ks[0], (BATCH, SEQ, D_MODEL), 1.0),
        "attn_norm": gain(ks[1], (DEPTH, D_MODEL)),
        "ffn_norm": gain(ks[2], (DEPTH, D_MODEL)),
        "final_norm": gain(ks[3], (D_MODEL,)),
        "e_w_in": nrm(ks[4], (N_EVEN, D_MODEL, EVEN_IN), D_MODEL ** -0.5),
        "e_b_f": jax.random.uniform(ks[5], (N_EVEN, FOX_HEADS), F32, 1.0, 4.0),
        "e_w_out": nrm(ks[6], (N_EVEN, EVEN_MIX, D_MODEL), EVEN_MIX ** -0.5),
        "o_w_in": nrm(ks[7], (N_ODD, D_MODEL, ODD_IN), D_MODEL ** -0.5),
        "o_q_norm": gain(ks[8], (N_ODD, MLA_Q_RANK)),
        "o_kv_norm": gain(ks[9], (N_ODD, MLA_KV_RANK)),
        "o_w_uq": nrm(ks[10], (N_ODD, MLA_Q_RANK, MLA_HEADS * (MLA_NOPE + MLA_ROPE)), MLA_Q_RANK ** -0.5),
        "o_w_ukv": nrm(ks[11], (N_ODD, MLA_KV_RANK, MLA_HEADS * (MLA_NOPE + MLA_V)), MLA_KV_RANK ** -0.5),
        "o_sinks": nrm(ks[12], (N_ODD, SWA_Q_HEADS), 1.0),
        "o_w_out": nrm(ks[13], (N_ODD, ODD_MIX, D_MODEL), ODD_MIX ** -0.5),
        "moe_w_group": nrm(ks[14], (DEPTH, D_MODEL, N_GROUPS), D_MODEL ** -0.5),
        "moe_b_group": nrm(ks[15], (DEPTH, N_GROUPS), 0.01),
        "moe_w_router": nrm(ks[16], (DEPTH, D_MODEL, N_EXPERTS), D_MODEL ** -0.5),
        "moe_b_router": nrm(ks[17], (DEPTH, N_EXPERTS), 0.01),
        "moe_w_gate": nrm(ks[18], (DEPTH, N_GROUPS, EXPERTS_PER_GROUP, D_MODEL, D_EXPERT), D_MODEL ** -0.5),
        "moe_w_up": nrm(ks[19], (DEPTH, N_GROUPS, EXPERTS_PER_GROUP, D_MODEL, D_EXPERT), D_MODEL ** -0.5),
        "moe_w_down": nrm(ks[20], (DEPTH, N_GROUPS, EXPERTS_PER_GROUP, D_EXPERT, D_MODEL), D_EXPERT ** -0.5),
    }

def reference(x, attn_norm, ffn_norm, final_norm, e_w_in, e_b_f, e_w_out, o_w_in, o_q_norm, o_kv_norm,
              o_w_uq, o_w_ukv, o_sinks, o_w_out, moe_w_group, moe_b_group, moe_w_router, moe_b_router,
              moe_w_gate, moe_w_up, moe_w_down):
    s = x.shape[1]
    cos, sin = rope_tables(s)
    dil_slopes = alibi_slopes(DIL_HEADS)
    swa_slopes = alibi_slopes(SWA_Q_HEADS).reshape(SWA_KV_HEADS, SWA_Q_HEADS // SWA_KV_HEADS)
    h = x
    for layer in range(DEPTH):
        hn = rmsnorm(h, attn_norm[layer])
        if layer % 2 == 0:
            i = layer // 2
            h = h + even_mixer(hn, e_w_in[i], e_b_f[i], e_w_out[i], dil_slopes)
        else:
            i = layer // 2
            h = h + odd_mixer(hn, o_w_in[i], o_q_norm[i], o_kv_norm[i], o_w_uq[i], o_w_ukv[i], o_sinks[i],
                              o_w_out[i], cos, sin, swa_slopes)
        h = h + hierarchical_moe(rmsnorm(h, ffn_norm[layer]), moe_w_group[layer], moe_b_group[layer],
                                 moe_w_router[layer], moe_b_router[layer], moe_w_gate[layer],
                                 moe_w_up[layer], moe_w_down[layer])
    return rmsnorm(h, final_norm)


_drawn_inputs = setup_inputs


def setup_inputs(seed=0):
    import zlib

    import numpy as np

    out = dict(_drawn_inputs(seed))
    spreads = {}
    factors = {'final_norm': 36.074,
     'o_q_norm': 5.558,
     'o_kv_norm': 4.512,
     'moe_b_group': 3.225,
     'o_sinks': 8.0}
    for name, (base, spread) in spreads.items():
        noise = np.random.default_rng([zlib.crc32(name.encode()), seed]).standard_normal(out[name].shape)
        drawn = base * np.exp(spread * noise) if base else spread * noise
        out[name] = __import__('jax').numpy.asarray(drawn.astype(out[name].dtype))
    for name, factor in factors.items():
        out[name] = (out[name] * factor).astype(out[name].dtype)
    return out
```

```python
import concourse.bass as bass
from concourse import mybir
from contextlib import ExitStack
import numpy as np

DM, S, C = 1024, 512, 4
KD = DM // 128
H, HD = 8, 64
NE, DE, SLOTS = 32, 256, 64
QR, KVR, NOPE, ROPE = 384, 256, 64, 32
OOB = 1 << 20
BIG = 1e30
MAXOV = (2 * S - 1) // SLOTS

C_ID, C_TRI, C_ONE, C_CAUSAL, C_DIL, C_SWA = 0, 128, 256, 384, 896, 1408
C_IOTA, C_TOK, C_HALF, C_THR = 1664, 1696, 1712, 1713
C_END = 1720


def shape_constants():
    p = np.arange(128)[:, None]
    t = np.zeros((128, C_END), np.float32)
    t[:, C_ID:C_ID + 128] = np.eye(128)
    t[:, C_TRI:C_TRI + 128] = p < np.arange(128)[None, :]
    t[:, C_ONE:C_ONE + 128] = 1.0
    d = p - np.arange(512)[None, :] + 384
    t[:, C_CAUSAL:C_CAUSAL + 512] = np.where(d >= 0, 0.0, BIG)
    count = (d >= 0) * ((d <= 128) * 1 + (d % 4 == 0) * 1 + (d % 16 == 0) * 1)
    t[:, C_DIL:C_DIL + 512] = np.where(count > 0, -np.log(np.maximum(count, 1)), BIG)
    d = 128 + p - np.arange(256)[None, :]
    t[:, C_SWA:C_SWA + 256] = np.where((d >= 0) & (d <= 127), 0.0, BIG)
    t[:, C_IOTA:C_IOTA + 32] = np.arange(32)
    tok = np.arange(C)[None, :] * 128 + p
    for k in range(2):
        t[:, C_TOK + 4 * k:C_TOK + 4 * k + 4] = 2 * tok
        t[:, C_TOK + 8 + 4 * k:C_TOK + 12 + 4 * k] = 2 * (2 * tok + k)
    t[:, C_HALF:C_HALF + 1] = p >= 64
    t[:, C_THR:C_THR + 7] = SLOTS * np.arange(1, 8)
    slope = 2.0 ** -np.arange(1, H + 1)
    pos = np.arange(S) - 256.0
    aug = np.zeros((4, H, S), np.float32)
    aug[0] = slope[:, None] * pos[None, :]
    aug[1] = -slope[:, None]
    aug[2] = 1.0
    aug[3] = pos[None, :]
    inv = np.float32(10000.0) ** (-np.arange(0, ROPE, 2, dtype=np.float32) / np.float32(ROPE))
    ang = (np.arange(S, dtype=np.float32)[:, None] * inv[None, :]).astype(np.float64)
    cos, sin = np.cos(ang), np.sin(ang)
    sc = -((NOPE + ROPE) ** -0.5)
    qrot = np.zeros((128, S), np.float32)
    qrot[64:80] = qrot[80:96] = sc * cos.T
    qrot[96:112] = -sc * sin.T
    qrot[112:128] = sc * sin.T
    krot = np.zeros((128, 2, C, 16), np.float32)
    krot[:, 0] = cos.reshape(C, 128, 16).transpose(1, 0, 2)
    krot[:, 1] = sin.reshape(C, 128, 16).transpose(1, 0, 2)
    return {"const_table": t, "const_aug": aug.reshape(4, H * S), "const_qrot": qrot,
            "const_krot": krot.reshape(128, 128)}


def trunk(nc, x, attn_norm, ffn_norm, final_norm, e_w_in, e_b_f, e_w_out, o_w_in, o_q_norm, o_kv_norm,
          o_w_uq, o_w_ukv, o_sinks, o_w_out, moe_w_group, moe_b_group, moe_w_router, moe_b_router,
          moe_w_gate, moe_w_up, moe_w_down, const_table, const_aug, const_qrot, const_krot, out):
    f32, i32 = mybir.dt.float32, mybir.dt.int32
    ALU, ACT = mybir.AluOpType, mybir.ActivationFunctionType
    X = mybir.AxisListType.X

    hn_dram = [nc.dram_tensor(f"hn_rows{l}", (2 * S, DM // 2), f32, kind="Internal").ap() for l in range(2)]
    tab_dram = [nc.dram_tensor(f"expert_table{l}", (S * NE, 4), i32, kind="Internal").ap() for l in range(2)]
    c_dram = nc.dram_tensor("forget_sums", (2, H * S), f32, kind="Internal").ap()
    y_dram = [nc.dram_tensor(f"expert_rows{l}", (2 * 2 * S, DM // 2), f32, kind="Internal").ap() for l in range(2)]

    wg_v = [moe_w_gate[l].rearrange("g e (h p k) f -> (g e) p h (k f)", h=2, p=128) for l in range(2)]
    wu_v = [moe_w_up[l].rearrange("g e (h p k) f -> (g e) p h (k f)", h=2, p=128) for l in range(2)]
    wd_v = [moe_w_down[l].rearrange("g e (p c) d -> (g e) p (c d)", p=128) for l in range(2)]
    ewin_v = e_w_in.rearrange("a (k p) n -> p (a k) n", p=128)
    owin_v = o_w_in.rearrange("a (k p) n -> p (a k) n", p=128)
    ewout_v = e_w_out.rearrange("a (k p) n -> p (a k) n", p=128)
    owout_v = o_w_out.rearrange("a (k p) n -> p (a k) n", p=128)

    fw = H * HD
    FOX0, ZF0, DIL0 = 0, 3 * fw, 3 * fw + H
    EVEN_COLS = [DIL0, DIL0 + fw, DIL0 + 2 * fw, FOX0, FOX0 + fw, FOX0 + 2 * fw]
    QS0 = QR + KVR + ROPE
    KS0 = QS0 + fw
    T_MOE = [8, 48]
    T_ODD = 40

    DIL, FOX, SWA, MLA = range(4)
    LEN = {f: [128 * (i + 1) for i in range(4)] for f in (DIL, FOX, MLA)}
    LEN[SWA] = [128, 256, 256, 256]
    FIRST_KEY = {f: [0] * 4 for f in (DIL, FOX, MLA)}
    FIRST_KEY[SWA] = [0, 0, 1, 2]
    MASK = {DIL: (C_DIL, 512), FOX: (C_CAUSAL, 512), MLA: (C_CAUSAL, 512), SWA: (C_SWA, 256)}

    def p_col(f, i):
        return sum(LEN[f][:i])

    def q_chunks(f, j):
        return [i for i in range(4) if FIRST_KEY[f][i] <= j <= i]

    def pt_col(f, j):
        return sum(128 * len(q_chunks(f, jj)) for jj in range(j))

    ctx = ExitStack()
    with ctx:
        def sb(name, shape, dt=f32):
            return ctx.enter_context(nc.sbuf_tensor(name, shape, dt))

        def sem(name):
            return ctx.enter_context(nc.semaphore(name))

        h = sb("h", [128, C, DM])
        hnT = sb("hnT", [128, KD, S])
        Q = sb("Q", [128, H, S])
        K = sb("K", [128, H, S])
        oT = sb("oT", [128, KD, S])
        V = sb("V", [128, C, 512])
        W = [sb(f"W{i}", [128, 4096]) for i in range(4)]
        D = [sb(f"D{i}", [128, 2048]) for i in range(4)]
        P = sb("P", [128, 2, 1280])
        PT = sb("PT", [128, 1280])
        cst = sb("cst", [128, C_END])
        nm = sb("nm", [128, 8])
        den = sb("den", [128, 8])
        rden = sb("rden", [128, 8])
        esink = sb("esink", [128, 8])
        sinks = sb("sinks", [128, 2 * H])
        ssq = sb("ssq", [128, 8])
        rstd = sb("rstd", [128, 8])
        ncells = sb("ncells", [1, 32], i32)
        turn = sb("turn", [1, 4])
        bf_sb = sb("bf_sb", [8, 1])
        bank = [ctx.enter_context(nc.psum_tensor(f"bank{i}", [128, 512], f32)) for i in range(8)]

        ident = cst[:, C_ID:C_ID + 128]
        ones = cst[:, C_ONE:C_ONE + 128]
        tri = cst[:, C_TRI:C_TRI + 128]
        iota = cst[:, C_IOTA:C_IOTA + 32]

        hn_row = Q[:, :, :].rearrange("p h s -> p (h s)").rearrange("p (c d) -> p c d", c=C)
        flatQ = Q[:, :, :].rearrange("p h s -> p (h s)")
        flatK = K[:, :, :].rearrange("p h s -> p (h s)")
        flatV = V[:, :, :].rearrange("p c s -> p (c s)")
        gain = P[:, 0, 0:DM]
        Xg = [flatK[:, 512 * i:512 * i + 512] for i in range(4)]
        XT = [flatK[:, 2048 + 512 * i:2560 + 512 * i] for i in range(2)]
        sil = [PT[:, 256 * i:256 * i + 256] for i in range(2)]
        hid = [PT[:, 512 + 256 * i:768 + 256 * i] for i in range(2)]
        hT = [PT[:, 1024 + 128 * i:1152 + 128 * i] for i in range(2)]
        Y = [flatV[:, 512 * i:512 * i + 512] for i in range(2)]
        wr = flatV[:, 1024:1312].rearrange("p (k n) -> p k n", k=KD)
        rbias = flatV[:, 1312:1348]
        rec = flatV[:, 1348:1380].bitcast(i32)
        recs = flatV[:, 1380:1508].bitcast(i32)
        gidx = flatV[:, 1508:1540].bitcast(i32)
        sidx = flatV[:, 1540:1572].bitcast(i32)
        slot = flatV[:, 1572:1580].bitcast(i32)
        ibuf = flatV[:, 1580:1588].bitcast(i32)
        orec = flatV[:, 1588:1592].bitcast(i32)
        oidx = flatV[:, 1592:1594].bitcast(i32)
        zf_w = D[2][:, 0:64].rearrange("p (k n) -> p k n", k=KD)
        zf = [D[3][0:8, 512 * i:512 * i + 512] for i in range(4)]
        junk = flatV[:, 0:1024]
        cq_row = flatQ[:, 0:2688].rearrange("p (c n) -> p c n", c=C)
        kpe_pad = PT[:, 0:512].rearrange("p (c n) -> p c n", c=C)
        ktmp = PT[:, 512:768].rearrange("p (a c n) -> p a c n", a=4, c=C)
        qkv_gain = P[:, 0, 0:QR + KVR]
        qrot = P[:, 0, 640:1152]
        krot = P[:, 0, 1152:1280].rearrange("p (a c n) -> p a c n", a=2, c=C)
        y_in = [flatQ[:, 2048 * i:2048 * i + 2048] for i in range(2)]
        tab_init = P[:, 0, 0:512].bitcast(i32)

        R = P[:, 1, :]

        def r(at, *dims):
            n = int(np.prod(dims))
            v = R[:, at:at + n]
            if len(dims) == 2:
                v = v.rearrange("p (a b) -> p a b", a=dims[0])
            if len(dims) == 3:
                v = v.rearrange("p (a b c) -> p a b c", a=dims[0], b=dims[1])
            return v

        lg, gmax, gexp, gsum = r(0, 4, 36), r(144, 4), r(148, 4, 4), r(164, 4)
        gw, gpick, gmin, goh, gpen = r(168, 4), r(172, 4, 4), r(188, 4), r(192, 4, 4), r(208, 4, 4)
        em = [r(224, 4, 32), r(352, 4, 32)]
        pick = [r(480, 4, 32), r(608, 4, 32)]
        oh = [r(736, 4, 32), r(864, 4, 32)]
        ohs = r(992, 4, 32)
        emax = [r(1120, 4), r(1124, 4)]
        emin = [r(1128, 4), r(1132, 4)]
        ed, esum, einv, wgt = r(1136, 4), r(1140, 4), r(1144, 4), r(1148, 2, 4)
        rpos = [r(1156, 4), r(1160, 4)]
        extra, ends = R[0:1, 1164:1196], R[0:1, 1196:1228]
        oe, ostart = R[0:1, 1228:1243], R[0:1, 1243:1258]
        ovbig = [P[0:1, 0, 0:480], P[0:1, 0, 480:960]]

        s_const = sem("const_loaded")
        s_heads = sem("head_constants_loaded")
        s_x = [sem(f"x_loaded{c}") for c in range(C)]
        s_small = sem("small_loaded")
        s_tabinit = sem("table_init")
        s_ld = [sem(f"tile_loaded{i}") for i in range(4)]
        s_gain = sem("gain_loaded")
        s_sq = sem("squares_summed")
        s_ms = sem("mean_square")
        s_sqrt = sem("root_taken")
        s_hn = sem("normed_rows")
        s_nt = sem("norm_transposed")
        s_ntA = sem("norm_t_out_act")
        s_ntV = sem("norm_t_out_dve")
        s_pj = sem("projected")
        s_pjA = sem("proj_out_act")
        s_pjV = sem("proj_out_dve")
        s_aug = sem("position_rows")
        s_zf = sem("forget_logits")
        s_cst = sem("forget_sums_stored")
        s_zfa = sem("forget_act")
        s_zfv = sem("forget_dve")
        s_qk = sem("scores_ready")
        s_msk = sem("scores_masked")
        s_exp = sem("probs_ready")
        s_rd = sem("denominator_inverted")
        s_nrm = sem("probs_normalised")
        s_tr = sem("probs_transposed")
        s_teA = sem("probs_t_out_act")
        s_teV = sem("probs_t_out_dve")
        s_pv = sem("head_output")
        s_oev = sem("head_pair_out")
        s_og = sem("mixer_projected")
        s_oga = sem("mixer_added")
        s_lrow = sem("latent_rows_normed")
        s_lt = sem("latent_transposed")
        s_ltA = sem("latent_out_act")
        s_ltV = sem("latent_out_dve")
        s_lsq = sem("latent_squares")
        s_lms = sem("latent_mean_square")
        s_lrt = sem("latent_root")
        s_perm = sem("rotary_columns")
        s_hnst = sem("normed_rows_stored")
        s_lg = sem("router_logits")
        s_rsub = sem("router_differences")
        s_rexp = sem("router_exps")
        s_oh = sem("expert_one_hots")
        s_rank = sem("expert_ranks")
        s_slot = sem("table_slots")
        s_tab = sem("table_written")
        s_recs = sem("records_loaded")
        s_idx = sem("expert_indices")
        s_ncell = sem("further_tiles_listed")
        s_ib = sem("index_column")
        s_g = [sem(f"rows_gathered{i}") for i in range(4)]
        s_xt = sem("rows_transposed")
        s_xte = sem("rows_t_out")
        s_gu = sem("gate_up_done")
        s_sil = sem("silu_done")
        s_hid = sem("hidden_done")
        s_ht = sem("hidden_transposed")
        s_hte = sem("hidden_t_out")
        s_y = sem("down_done")
        s_ye = sem("down_out")
        s_sc = [sem(f"rows_scattered{i}") for i in range(2)]
        ov = [{n: sem(f"further{l}_{n}") for n in
               ("loaded", "records", "indices", "gathered", "xt", "xte", "gu", "sil", "hid", "ht", "hte",
                "y", "ye", "scattered", "out")} for l in range(2)]
        s_yld = [sem(f"expert_rows_loaded{i}") for i in range(2)]
        s_yadd = sem("expert_rows_added")
        s_out = sem("output_stored")
        s_dv = sem("dve_order")
        s_av = sem("act_order")
        s_pl = sem("pool_order")

        block = ctx.enter_context(nc.Block())

        def tile_ready(n):
            return 48 * (n // 4 + 1)

        def last_read(n):
            if n < 6:
                return s_pj, 4 * (n + 1)
            if n < 8:
                return s_og, 4 * (n - 5)
            if n < T_ODD:
                return s_y, n - T_MOE[0] + 1
            if n < T_ODD + 6:
                return s_pj, (28, 30, 34, 36, 44, 52)[n - T_ODD]
            return s_og, 8 + 4 * (n - T_ODD - 5)

        @block.sync
        def _(sp):
            sp.dma_start(cst[:, :], const_table).then_inc(s_const, 16)
            for c in range(C):
                sp.dma_start(h[:, c, :], x[0, 128 * c:128 * c + 128, :]).then_inc(s_x[c], 16)

            def slot_free(n):
                if n >= 4:
                    sp.wait_ge(*last_read(n - 4))

            def load_cols(n, src, c0, width):
                slot_free(n)
                dst = W[n % 4][:, :].rearrange("p (k n) -> p k n", k=KD)
                sp.dma_start(dst[:, :, 0:width], src[:, :, c0:c0 + width]).then_inc(s_ld[n % 4], 48)

            def load_expert(lay, w, s, done):
                for v, at in ((wg_v[lay], 0), (wu_v[lay], 2048)):
                    dst = W[s][:, at:at + 2048].rearrange("p (h x) -> p h x", h=2)
                    sp.dma_start(dst, v[bass.ds(w, 1), :, :, :].rearrange("a p h x -> (a p) h x"))\
                      .then_inc(done, 16)
                sp.dma_start(D[s][:, :], wd_v[lay][bass.ds(w, 1), :, :].rearrange("a p x -> (a p) x"))\
                  .then_inc(done, 16)

            def experts(lay):
                for s in range(4):
                    slot_free(T_MOE[lay] + s)
                    load_expert(lay, s, s, s_ld[s])
                with sp.Fori(4, NE - 3, 4) as e:
                    for s in range(4):
                        w = sp.snap(e + s)
                        sp.wait_ge(s_y, e + (NE * lay + s - 3))
                        load_expert(lay, w, s, s_ld[s])

            def further_tiles(lay):
                o_ = ov[lay]
                sp.wait_ge(s_ncell, lay + 1)
                n_over = sp.value_load(ncells[0:1, 0:1], min_val=0, max_val=MAXOV)
                with sp.If(n_over > 0):
                    sp.wait_ge(s_y, NE * (lay + 1))
                    with sp.Fori(0, n_over) as o:
                        ex = sp.value_load(ncells[0:1, bass.ds(o + 1, 1)], min_val=0, max_val=NE - 1)
                        rk = sp.value_load(ncells[0:1, bass.ds(o + (1 + MAXOV), 1)], min_val=1, max_val=7)
                        sp.wait_ge(o_["out"], o + 1)
                        load_expert(lay, ex, 0, o_["loaded"])
                        tv = tab_dram[lay].rearrange("(r e) w -> r (e w)", e=NE)
                        for half in range(2):
                            sp.dma_start(orec[64 * half:64 * half + 64, :],
                                         tv[bass.ds(sp.snap(rk * SLOTS), SLOTS), bass.ds(sp.snap(ex * 4), 4)])\
                              .then_inc(o_["records"], 16)

            for n, c0 in enumerate(EVEN_COLS):
                load_cols(n, ewin_v, c0, 512)
            for half in range(2):
                load_cols(6 + half, ewout_v, 512 * half, 512)
            experts(0)
            further_tiles(0)
            load_cols(T_ODD, owin_v, QS0, 512)
            load_cols(T_ODD + 1, owin_v, KS0, 256)
            load_cols(T_ODD + 2, owin_v, 0, 512)
            load_cols(T_ODD + 3, owin_v, 512, 160)
            slot_free(T_ODD + 4)
            for k in range(3):
                dst = W[(T_ODD + 4) % 4][:, 0:3072].rearrange("p (k h n) -> p k h n", k=3, h=H)
                sp.dma_start(dst[:, k, :, 0:96],
                             o_w_uq[0, 128 * k:128 * k + 128, :].rearrange("p (h n) -> p h n", h=H))\
                  .then_inc(s_ld[(T_ODD + 4) % 4], 16)
            slot_free(T_ODD + 5)
            sp.dma_start(W[(T_ODD + 5) % 4][:, 0:2048].rearrange("p (k n) -> p k n", k=2),
                         o_w_ukv.rearrange("a (k p) n -> p (a k) n", p=128)).then_inc(s_ld[(T_ODD + 5) % 4], 48)
            for half in range(2):
                load_cols(T_ODD + 6 + half, owout_v, 512 * half, 512)
            experts(1)
            further_tiles(1)
            for c in range(C):
                sp.wait_ge(s_hn, 16 + c + 1)
                sp.dma_start(out[0, 128 * c:128 * c + 128, :], hn_row[:, c, :]).then_inc(s_out, 16)
            sp.wait_ge(s_out, 16 * C)

        @block.gpsimd
        def _(pool):
            order = [0]
            last_half_row = pool.to_reg(2 * S - 1)
            last_result = pool.to_reg(4 * S - 1)

            def then(ins):
                order[0] += 1
                ins.then_inc(s_pl, 1)
                pool.wait_ge(s_pl, order[0])

            def hold(at=1):
                return nc.gpsimd.tensor_tensor(turn[:, at:at + 1], turn[:, 0:1], turn[:, 0:1], ALU.add)

            then(nc.gpsimd.memset(turn[:, :], 0.0))
            then(nc.gpsimd.memset(tab_init, OOB))
            for l in range(2):
                pool.dma_start(tab_dram[l].rearrange("(p r) w -> p (r w)", p=128), tab_init).then_inc(s_tabinit, 16)
            pool.dma_start(sinks[:, 0:H], o_sinks[0:1, :].partition_broadcast(128).rearrange("a b n -> a (b n)")
                           ).then_inc(s_heads, 16)
            pool.dma_start(bf_sb[:, :], e_b_f.rearrange("a n -> n a")).then_inc(s_heads, 16)
            pool.wait_ge(s_tabinit, 32)

            def load_gain(v):
                src = (attn_norm[0:1, :], ffn_norm[0:1, :], attn_norm[1:2, :], ffn_norm[1:2, :],
                       final_norm.rearrange("(a n) -> a n", a=1))[v]
                pool.dma_start(gain, src.partition_broadcast(128).rearrange("a b n -> a (b n)")).then_inc(s_gain, 16)

            def normalise(f):
                for u in range(H):
                    for i in range(4):
                        b = 4 * (H * f + u) + i
                        pool.wait_ge(s_rd, b + 1)
                        blk = P[:, u % 2, p_col(f, i):p_col(f, i) + LEN[f][i]]
                        nc.gpsimd.tensor_scalar(blk, blk, rden[:, b % 8:b % 8 + 1], None, ALU.mult)\
                          .then_inc(s_nrm, 1)

            def alibi_rows(kv_heads):
                pool.dma_start(Q[64:66, :, :].rearrange("p h s -> p (h s)"), const_aug[0:2, :]).then_inc(s_aug, 16)
                pool.dma_start(K[64:66, 0:kv_heads, :].rearrange("p h s -> p (h s)"),
                               const_aug[2:4, 0:kv_heads * S]).then_inc(s_aug, 16)

            def routing(lay):
                pool.wait_ge(s_oga, 8 * lay + 1)
                pool.dma_start(wr[:, :, 0:4], moe_w_group[lay].rearrange("(k p) n -> p k n", p=128)).then_inc(s_small, 16)
                pool.dma_start(wr[:, :, 4:36], moe_w_router[lay].rearrange("(k p) n -> p k n", p=128)).then_inc(s_small, 16)
                pool.dma_start(rbias[:, 0:4], moe_b_group[lay:lay + 1, :].partition_broadcast(128)
                               .rearrange("a b n -> a (b n)")).then_inc(s_small, 16)
                pool.dma_start(rbias[:, 4:36], moe_b_router[lay:lay + 1, :].partition_broadcast(128)
                               .rearrange("a b n -> a (b n)")).then_inc(s_small, 16)
                for c in range(C):
                    pool.wait_ge(s_hn, 4 * (2 * lay + 1) + c + 1)
                    pool.dma_start(hn_dram[lay].rearrange("(s h) d -> s (h d)", h=2)[128 * c:128 * c + 128, :],
                                   hn_row[:, c, :]).then_inc(s_hnst, 16)
                pool.wait_ge(s_slot, lay + 1)
                for kc in range(8):
                    pool.indirect_dma_start(out=tab_dram[lay],
                                            out_offset=bass.IndirectOffsetOnAxis(ap=slot[:, kc:kc + 1], axis=0),
                                            in_=rec[:, 4 * kc:4 * kc + 4], in_offset=None,
                                            bounds_check=S * NE - 1, oob_is_err=False).then_inc(s_tab, 16)
                pool.wait_ge(s_tab, 128 * (lay + 1))
                for half in range(2):
                    pool.dma_start(recs[64 * half:64 * half + 64, :],
                                   tab_dram[lay].rearrange("(r e) w -> r (e w)", e=NE)[0:SLOTS, :]).then_inc(s_recs, 16)

            def gather(lay, dst, idx_col, done):
                pool.indirect_dma_start(out=dst, out_offset=None, in_=hn_dram[lay],
                                        in_offset=bass.IndirectOffsetOnAxis(ap=idx_col, axis=0),
                                        bounds_check=last_half_row, oob_is_err=False).then_inc(done, 16)

            def scatter(lay, src, idx_col, done):
                pool.indirect_dma_start(out=y_dram[lay],
                                        out_offset=bass.IndirectOffsetOnAxis(ap=idx_col, axis=0),
                                        in_=src, in_offset=None,
                                        bounds_check=last_result, oob_is_err=False).then_inc(done, 16)

            def expert_rows(lay):
                base = NE * lay
                pool.wait_ge(s_idx, lay + 1)
                pool.wait_ge(s_hnst, 64 * (lay + 1))

                for s in range(4):
                    nc.gpsimd.tensor_copy(ibuf[:, s:s + 1], gidx[:, s:s + 1]).then_inc(s_ib, 1)
                    pool.wait_ge(s_ib, 64 * lay + s + 1)
                    gather(lay, Xg[s], ibuf[:, s:s + 1], s_g[s])

                def scatter_first(e, s, col):
                    pool.wait_ge(s_ye, e + (base + 1))
                    nc.gpsimd.tensor_copy(ibuf[:, 4 + s:5 + s], sidx[:, col]).then_inc(s_ib, 1)

                with pool.Fori(0, NE - 7, 4) as e0:
                    for s in range(4):
                        e = e0 + s
                        ahead = pool.snap(e0 + (s + 4))
                        scatter_first(e, s, bass.ds(pool.snap(e), 1))
                        pool.wait_ge(s_xt, e + (base + 1))
                        nc.gpsimd.tensor_copy(ibuf[:, s:s + 1], gidx[:, bass.ds(ahead, 1)]).then_inc(s_ib, 1)
                        pool.wait_ge(s_ib, e0 * 2 + (64 * lay + 2 * s + 6))
                        hold()
                        scatter(lay, Y[s % 2], ibuf[:, 4 + s:5 + s], s_sc[s % 2])
                        gather(lay, Xg[s], ibuf[:, s:s + 1], s_g[s])
                for s in range(4):
                    e = NE - 4 + s
                    scatter_first(e, s, slice(e, e + 1))
                    pool.wait_ge(s_ib, 64 * lay + 4 + 2 * (NE - 4) + s + 1)
                    scatter(lay, Y[s % 2], ibuf[:, 4 + s:5 + s], s_sc[s % 2])
                for s in range(2):
                    pool.wait_ge(s_sc[s], 16 * 16 * (lay + 1))

            def further_tiles(lay):
                o_ = ov[lay]
                pool.wait_ge(s_ncell, lay + 1)
                n_over = pool.value_load(ncells[0:1, 0:1], min_val=0, max_val=MAXOV)
                with pool.If(n_over > 0):
                    hold(3).then_inc(o_["out"], 1)
                    with pool.Fori(0, n_over) as o:
                        pool.wait_ge(o_["indices"], o + 1)
                        hold()
                        gather(lay, Xg[0], oidx[:, 0:1], o_["gathered"])
                        pool.wait_ge(o_["ye"], o + 1)
                        hold(2)
                        scatter(lay, Y[0], oidx[:, 1:2], o_["scattered"])
                        pool.wait_ge(o_["scattered"], o * 16 + 16)
                        hold(3).then_inc(o_["out"], 1)

            def load_expert_rows(lay):
                for c in range(C):
                    if c >= 2:
                        pool.wait_ge(s_yadd, 4 * lay + c - 1)
                    pool.dma_start(y_in[c % 2], y_dram[lay].rearrange("(s f) d -> s (f d)", f=4)
                                   [128 * c:128 * c + 128, :]).then_inc(s_yld[c % 2], 16)

            load_gain(0)
            pool.dma_start(zf_w, ewin_v[:, :, ZF0:ZF0 + H]).then_inc(s_small, 16)
            then(nc.gpsimd.memset(K[64:128, :, :], 0.0))
            pool.wait_ge(s_nt, 8)
            alibi_rows(H)
            pool.wait_ge(s_zfv, 5)
            for i in range(2):
                pool.dma_start(c_dram[i].rearrange("(h s) -> h s", h=H), zf[2 + i]).then_inc(s_cst, 16)
            normalise(DIL)
            pool.wait_ge(s_cst, 32)
            pool.wait_ge(s_qk, 4 * H)
            pool.dma_start(Q[65:66, :, :].rearrange("p h s -> p (h s)"), const_aug[2:3, :]).then_inc(s_aug, 16)
            pool.dma_start(Q[64:65, :, :].rearrange("p h s -> p (h s)"), c_dram[1:2, :]).then_inc(s_aug, 16)
            pool.dma_start(K[65:66, :, :].rearrange("p h s -> p (h s)"), c_dram[0:1, :]).then_inc(s_aug, 16)
            normalise(FOX)
            pool.wait_ge(s_tr, 4 * 2 * H)
            load_gain(1)
            routing(0)
            expert_rows(0)
            further_tiles(0)
            load_gain(2)
            load_expert_rows(0)
            then(nc.gpsimd.memset(K[64:128, 0:2, :], 0.0))
            pool.wait_ge(s_nt, 8 * 3)
            alibi_rows(2)
            normalise(SWA)
            pool.wait_ge(s_tr, 4 * 3 * H)
            pool.dma_start(qkv_gain[:, 0:QR], o_q_norm[0:1, :].partition_broadcast(128)
                           .rearrange("a b n -> a (b n)")).then_inc(s_small, 16)
            pool.dma_start(qkv_gain[:, QR:QR + KVR], o_kv_norm[0:1, :].partition_broadcast(128)
                           .rearrange("a b n -> a (b n)")).then_inc(s_small, 16)
            pool.dma_start(qrot, const_qrot).then_inc(s_small, 16)
            pool.dma_start(P[:, 0, 1152:1280], const_krot).then_inc(s_small, 16)
            t = T_ODD + 4
            pool.wait_ge(s_ld[t % 4], tile_ready(t))
            uq = W[t % 4][:, 0:3072].rearrange("p (kh n) -> p kh n", n=128)
            nc.gpsimd.tensor_copy(uq[:, :, 96:112], uq[:, :, 80:96]).then_inc(s_perm, 1)
            nc.gpsimd.tensor_copy(uq[:, :, 112:128], uq[:, :, 64:80]).then_inc(s_perm, 1)
            normalise(MLA)
            pool.wait_ge(s_tr, 4 * 4 * H)
            load_gain(3)
            routing(1)
            expert_rows(1)
            further_tiles(1)
            load_gain(4)
            load_expert_rows(1)

        @block.tensor
        def _(pe):
            pe.wait_ge(s_const, 16)
            group = [0]

            def group_start():
                g = group[0]
                if g >= 2:
                    pe.wait_ge(s_pjA, g - 1)
                    pe.wait_ge(s_pjV, g - 1)
                group[0] += 1
                return bank[6 + g % 2]

            def w_tile(n):
                return W[n % 4][:, :].rearrange("p (k n) -> p k n", k=KD)

            def norm_transposes(v):
                for c in range(C):
                    pe.wait_ge(s_hn, 4 * v + c + 1)
                    for half in range(2):
                        if c or v:
                            pe.wait_ge((s_ntA, s_ntV)[half], 4 * v + c)
                        for kk in range(4):
                            k = 4 * half + kk
                            last = nc.tensor.transpose(bank[3 + half][:, 128 * kk:128 * kk + 128],
                                                       hn_row[:, c, 128 * k:128 * k + 128], ident)
                        last.then_inc(s_nt, 1)

            def norm_ready(v):
                pe.wait_ge(s_ntA, 4 * v + 4)
                pe.wait_ge(s_ntV, 4 * v + 4)

            def project_features(n, blocks):
                w = w_tile(n)
                pe.wait_ge(s_ld[n % 4], tile_ready(n))
                for fb in range(blocks):
                    b = group_start()
                    for k in range(KD):
                        last = nc.tensor.matmul(b[:, :], w[:, k, 128 * fb:128 * fb + 128], hnT[:, k, :],
                                                start=(k == 0), stop=(k == KD - 1))
                    last.then_inc(s_pj, 1)

            def project_rows(n, c0, width, per_group):
                w = w_tile(n)
                pe.wait_ge(s_ld[n % 4], tile_ready(n))
                for c in range(C):
                    if c % per_group == 0:
                        b = group_start()
                    at = (c % per_group) * width
                    for k in range(KD):
                        last = nc.tensor.matmul(b[:, at:at + width], hnT[:, k, 128 * c:128 * c + 128],
                                                w[:, k, c0:c0 + width], start=(k == 0), stop=(k == KD - 1))
                    if c % per_group == per_group - 1:
                        last.then_inc(s_pj, 1)

            def scores(f, u):
                g = H * f + u
                kv = u // 4 if f == SWA else u
                for i in range(4):
                    b = 4 * g + i
                    if b >= 3:
                        pe.wait_ge(s_msk, b - 2)
                    k0, n = 128 * FIRST_KEY[f][i], LEN[f][i]
                    nc.tensor.matmul(bank[b % 3][:, 0:n], Q[:, u, 128 * i:128 * i + 128],
                                     K[:, kv, k0:k0 + n], start=True, stop=True).then_inc(s_qk, 1)

            def transposes(f, u):
                g = H * f + u
                pe.wait_ge(s_nrm, 4 * g + 4)
                for j in range(4):
                    t = 4 * g + j
                    if t >= 2:
                        pe.wait_ge((s_teA, s_teV)[j % 2], t // 2)
                    for a, i in enumerate(q_chunks(f, j)):
                        at = p_col(f, i) + 128 * (j - FIRST_KEY[f][i])
                        last = nc.tensor.transpose(bank[3 + j % 2][:, 128 * a:128 * a + 128],
                                                   P[:, u % 2, at:at + 128], ident)
                    last.then_inc(s_tr, 1)

            def head_outputs(f, u):
                g = H * f + u
                vc = 64 * (u // 4) if f == SWA else 64 * u
                if g == 0:
                    pe.wait_ge(s_zfv, 1)
                elif u % 2 == 0:
                    pe.wait_ge(s_oev, g // 2)
                for j in range(4):
                    pe.wait_ge((s_teA, s_teV)[j % 2], 2 * g + j // 2 + 1)
                    n = 128 * len(q_chunks(f, j))
                    last = nc.tensor.matmul(bank[5][64 * (u % 2):64 * (u % 2) + 64, 128 * j:128 * j + n],
                                            V[:, j, vc:vc + 64], PT[:, pt_col(f, j):pt_col(f, j) + n],
                                            start=(j == 0), stop=(j == 3), skip_group_check=True)
                last.then_inc(s_pv, 1)

            def attention(f, groups, aug):
                pe.wait_ge(s_pjA, groups)
                pe.wait_ge(s_pjV, groups)
                pe.wait_ge(s_aug, aug)
                scores(f, 0)
                for u in range(H):
                    if u + 1 < H:
                        scores(f, u + 1)
                    transposes(f, u)
                    head_outputs(f, u)

            def mixer_out(lay, n0):
                pe.wait_ge(s_oev, 8 * (lay + 1))
                for half in range(2):
                    n = n0 + half
                    pe.wait_ge(s_ld[n % 4], tile_ready(n))
                    for c in range(C):
                        g = 8 * lay + 4 * half + c
                        if g >= 2:
                            pe.wait_ge(s_oga, g - 1)
                        for k in range(KD):
                            last = nc.tensor.matmul(bank[g % 2][:, :], oT[:, k, 128 * c:128 * c + 128],
                                                    w_tile(n)[:, k, :], start=(k == 0), stop=(k == KD - 1))
                        last.then_inc(s_og, 1)

            def routing(lay):
                pe.wait_ge(s_small, (80, 208)[lay])
                for c in range(C):
                    for k in range(KD):
                        last = nc.tensor.matmul(bank[6][:, 36 * c:36 * c + 36], hnT[:, k, 128 * c:128 * c + 128],
                                                wr[:, k, :], start=(k == 0), stop=(k == KD - 1))
                last.then_inc(s_lg, 1)
                pe.wait_ge(s_oh, lay + 1)
                for c in range(C):
                    for cc in range(c):
                        nc.tensor.matmul(bank[7][:, 32 * c:32 * c + 32], ones, ohs[:, cc, :],
                                         start=(cc == 0), stop=False)
                    nc.tensor.matmul(bank[7][:, 32 * c:32 * c + 32], tri, ohs[:, c, :], start=(c == 0), stop=True)
                for c in range(C):
                    last = nc.tensor.matmul(bank[7][:, 128:160], ones, ohs[:, c, :], start=(c == 0), stop=(c == C - 1))
                last.then_inc(s_rank, 1)

            def transpose_rows(e2, src):
                for k in range(4):
                    last = nc.tensor.transpose(bank[e2][:, 128 * k:128 * k + 128],
                                               src.rearrange("p (x k) -> p k x", k=4)[:, k, :], ident)
                return last

            def gate_up(e2, w):
                for half in range(2):
                    for k in range(4):
                        xt = XT[e2][:, 128 * k + 64 * half:128 * k + 64 * half + 64]
                        at = 1024 * half + 256 * k
                        first, end = half + k == 0, half + k == 4
                        nc.tensor.matmul(bank[2 + e2][0:64, 0:256], xt, w[:, at:at + 256], start=first, stop=end)
                        last = nc.tensor.matmul(bank[2 + e2][64:128, 0:256], xt, w[:, 2048 + at:2304 + at],
                                                start=first, stop=end)
                return last

            def hidden_transposes(e2):
                for c in range(2):
                    last = nc.tensor.transpose(bank[4][:, 128 * c:128 * c + 128],
                                               hid[e2].rearrange("p (x c) -> p c x", c=2)[:, c, :], ident)
                return last

            def down(e2, d):
                for c in range(2):
                    nc.tensor.matmul(bank[5 + e2][0:64, :], hT[e2][:, 64 * c:64 * c + 64],
                                     d[:, 1024 * c:1024 * c + 512], start=(c == 0), stop=(c == 1))
                    last = nc.tensor.matmul(bank[5 + e2][64:128, :], hT[e2][:, 64 * c:64 * c + 64],
                                            d[:, 1024 * c + 512:1024 * c + 1024], start=(c == 0), stop=(c == 1))
                return last

            def experts(lay):
                base, t0 = NE * lay, T_MOE[lay]
                pe.wait_ge(s_g[0], 16 * (8 * lay + 1))
                transpose_rows(0, Xg[0]).then_inc(s_xt, 1)

                def step(e, s, more, wait_out=True):
                    e2 = s % 2
                    pe.wait_ge(s_ld[s], e * 12 + (tile_ready(t0 + s) - 12 * s))
                    pe.wait_ge(s_xte, e + (base + 1))
                    gate_up(e2, W[s]).then_inc(s_gu, 1)
                    if more:
                        s1 = (s + 1) % 4
                        turn = e * 4 + (16 * 8 * lay + 16 - 4 * s + (16 if s == 3 else 0))
                        pe.wait_ge(s_g[s1], turn)
                        transpose_rows(1 - e2, Xg[s1]).then_inc(s_xt, 1)
                    pe.wait_ge(s_hid, e + (base + 1))
                    hidden_transposes(e2).then_inc(s_ht, 1)
                    pe.wait_ge(s_hte, e + (base + 1))
                    if wait_out:
                        pe.wait_ge(s_ye, e + (base - 1))
                    down(e2, D[s]).then_inc(s_y, 1)

                for s in range(4):
                    step(s, s, True, base + s >= 2)
                with pe.Fori(4, NE - 4, 4) as e:
                    for s in range(4):
                        step(e + s, s, True)
                for s in range(4):
                    step(NE - 4 + s, s, s < 3)

            def further_tiles(lay):
                o_ = ov[lay]
                pe.wait_ge(s_ncell, lay + 1)
                n_over = pe.value_load(ncells[0:1, 0:1], min_val=0, max_val=MAXOV)
                with pe.If(n_over > 0):
                    with pe.Fori(0, n_over) as o:
                        pe.wait_ge(o_["gathered"], o * 16 + 16)
                        transpose_rows(0, Xg[0]).then_inc(o_["xt"], 1)
                        pe.wait_ge(o_["loaded"], o * 48 + 48)
                        pe.wait_ge(o_["xte"], o + 1)
                        gate_up(0, W[0]).then_inc(o_["gu"], 1)
                        pe.wait_ge(o_["hid"], o + 1)
                        hidden_transposes(0).then_inc(o_["ht"], 1)
                        pe.wait_ge(o_["hte"], o + 1)
                        down(0, D[0]).then_inc(o_["y"], 1)

            norm_transposes(0)
            norm_ready(0)
            pe.wait_ge(s_small, 16)
            for k in range(KD):
                last = nc.tensor.matmul(bank[5][0:8, :], zf_w[:, k, :], hnT[:, k, :], start=(k == 0), stop=(k == KD - 1))
            last.then_inc(s_zf, 1)
            for n in range(2):
                project_features(n, 4)
            project_rows(2, 0, 512, 1)
            attention(DIL, 12, 32)
            for n in range(3, 5):
                project_features(n, 4)
            project_rows(5, 0, 512, 1)
            attention(FOX, 24, 80)
            mixer_out(0, 6)
            norm_transposes(1)
            norm_ready(1)
            routing(0)
            experts(0)
            further_tiles(0)

            norm_transposes(2)
            norm_ready(2)
            project_features(T_ODD, 4)
            project_features(T_ODD + 1, 1)
            project_rows(T_ODD + 1, 128, 128, 4)
            attention(SWA, 30, 112)
            project_rows(T_ODD + 2, 0, 512, 1)
            project_rows(T_ODD + 3, 0, 160, 2)
            for c in range(C):
                pe.wait_ge(s_lrow, c + 1)
                if c:
                    pe.wait_ge(s_ltA, c)
                    pe.wait_ge(s_ltV, c)
                for k in range(4):
                    last = nc.tensor.transpose(bank[3][:, 128 * k:128 * k + 128], cq_row[:, c, 128 * k:128 * k + 128], ident)
                last.then_inc(s_lt, 1)
                nc.tensor.transpose(bank[4][:, 0:128], cq_row[:, c, 512:640], ident)
                nc.tensor.transpose(bank[4][:, 128:256], kpe_pad[:, c, :], ident).then_inc(s_lt, 1)
            pe.wait_ge(s_ltA, C)
            pe.wait_ge(s_ltV, C)
            pe.wait_ge(s_perm, 2)
            uq = W[(T_ODD + 4) % 4][:, 0:3072].rearrange("p (k h n) -> p k h n", k=3, h=H)
            for hh in range(H):
                b = group_start()
                for k in range(3):
                    last = nc.tensor.matmul(b[:, :], uq[:, k, hh, :], hnT[:, k, :], start=(k == 0), stop=(k == 2))
                last.then_inc(s_pj, 1)
            t = T_ODD + 5
            pe.wait_ge(s_ld[t % 4], tile_ready(t))
            ukv = W[t % 4][:, 0:2048].rearrange("p (k h n) -> p k h n", k=2, h=H)
            for pair in range(4):
                b = group_start()
                for k in range(2):
                    for a in range(2):
                        last = nc.tensor.matmul(b[64 * a:64 * a + 64, :], ukv[:, k, 2 * pair + a, 0:64],
                                                hnT[:, 3 + k, :], start=(k == 0), stop=(k == 1))
                last.then_inc(s_pj, 1)
            for c in range(C):
                b = group_start()
                for k in range(2):
                    last = nc.tensor.matmul(b[:, :].rearrange("p (h n) -> p h n", h=H),
                                            hnT[:, 3 + k, 128 * c:128 * c + 128], ukv[:, k, :, 64:128],
                                            start=(k == 0), stop=(k == 1))
                last.then_inc(s_pj, 1)
            attention(MLA, 52, 112)
            mixer_out(1, T_ODD + 6)
            norm_transposes(3)
            norm_ready(3)
            routing(1)
            experts(1)
            further_tiles(1)

        @block.scalar
        def _(act):
            order = [0]
            group = [0]

            def then(ins):
                order[0] += 1
                ins.then_inc(s_av, 1)
                act.wait_ge(s_av, order[0])

            def chunk_ready(v, c):
                if v == 0:
                    return s_x[c], 16
                if v % 2:
                    return s_oga, 8 * (v // 2) + 5 + c
                return s_yadd, 4 * (v // 2 - 1) + 1 + c

            def norm(v):
                for c in range(C):
                    act.wait_ge(*chunk_ready(v, c))
                    if c:
                        act.wait_ge(s_sq, 4 * v + c)
                    nc.scalar.activation(junk, h[:, c, :], ACT.Square, accum_out=ssq[:, c:c + 1]).then_inc(s_sq, 1)
                act.wait_ge(s_ms, v + 1)
                nc.scalar.activation(rstd[:, 0:4], ssq[:, 0:4], ACT.Sqrt).then_inc(s_sqrt, 1)

            def norm_out(v):
                for c in range(C):
                    act.wait_ge(s_nt, 8 * v + 2 * c + 1)
                    nc.scalar.activation(hnT[:, 0:4, 128 * c:128 * c + 128],
                                         bank[3][:, :].rearrange("p (k t) -> p k t", k=4), ACT.Copy).then_inc(s_ntA, 1)

            def next_group():
                g = group[0]
                act.wait_ge(s_pj, g + 1)
                group[0] += 1
                return bank[6 + g % 2]

            def features_out(dst, scale, heads):
                for hh in range(0, heads, 2):
                    b = next_group()
                    nc.scalar.activation(dst[0:64, hh, :], b[0:64, :], ACT.Copy, scale=scale).then_inc(s_pjA, 1)

            def rows_out():
                for c in range(C):
                    b = next_group()
                    nc.scalar.activation(V[0:64, c, :], b[0:64, :], ACT.Copy).then_inc(s_pjA, 1)

            def exps(f, u, blocks):
                for i in blocks:
                    b = 4 * (H * f + u) + i
                    act.wait_ge(s_msk, b + 1)
                    if f == SWA:
                        nc.scalar.activation(esink[:, b % 8:b % 8 + 1], sinks[:, u:u + 1], ACT.Exp,
                                             bias=nm[:, b % 8:b % 8 + 1])
                    blk = P[:, u % 2, p_col(f, i):p_col(f, i) + LEN[f][i]]
                    nc.scalar.activation(blk, blk, ACT.Exp, bias=nm[:, b % 8:b % 8 + 1], scale=-1.0,
                                         accum_out=den[:, b % 8:b % 8 + 1]).then_inc(s_exp, 1)

            def probs_out(f, u, j):
                g = H * f + u
                act.wait_ge(s_tr, 4 * g + j + 1)
                if g:
                    act.wait_ge(s_pv, g)
                n = 128 * len(q_chunks(f, j))
                nc.scalar.activation(PT[:, pt_col(f, j):pt_col(f, j) + n], bank[3][:, 0:n], ACT.Copy).then_inc(s_teA, 1)

            def pair_out(f, u):
                act.wait_ge(s_pv, H * f + u + 1)
                chunk = u // 2 + (4 if f in (DIL, SWA) else 0)
                nc.scalar.activation(oT[:, chunk, :], bank[5][:, :], ACT.Copy).then_inc(s_oev, 1)

            def attention(f):
                exps(f, 0, range(4))
                for u in range(H):
                    if u and u % 2 == 0:
                        pair_out(f, u - 1)
                    if u + 1 < H:
                        exps(f, u + 1, (0, 1))
                    probs_out(f, u, 0)
                    probs_out(f, u, 2)
                    if u + 1 < H:
                        exps(f, u + 1, (2, 3))
                pair_out(f, H - 1)

            def routing(lay):
                act.wait_ge(s_rsub, 2 * lay + 1)
                nc.scalar.activation(gexp, gexp, ACT.Exp).then_inc(s_rexp, 1)
                act.wait_ge(s_rsub, 2 * lay + 2)
                nc.scalar.activation(ed, ed, ACT.Exp).then_inc(s_rexp, 1)

            def silu(e2, done):
                nc.scalar.activation(sil[e2][64:128, :], bank[2 + e2][0:64, 0:256], ACT.Silu).then_inc(done, 1)

            def hidden_out(e2, done):
                nc.scalar.activation(hT[e2].rearrange("p (c t) -> p c t", c=2),
                                     bank[4][:, 0:256].rearrange("p (c t) -> p c t", c=2)[:, :, 64:128],
                                     ACT.Copy).then_inc(done, 1)

            def experts(lay):
                base = NE * lay
                with act.Fori(0, NE, 2) as e:
                    for e2 in range(2):
                        act.wait_ge(s_gu, e + (base + e2 + 1))
                        silu(e2, s_sil)
                        act.wait_ge(s_ht, e + (base + e2 + 1))
                        hidden_out(e2, s_hte)

            def further_tiles(lay):
                o_ = ov[lay]
                act.wait_ge(s_ncell, lay + 1)
                n_over = act.value_load(ncells[0:1, 0:1], min_val=0, max_val=MAXOV)
                with act.If(n_over > 0):
                    with act.Fori(0, n_over) as o:
                        act.wait_ge(o_["gu"], o + 1)
                        silu(0, o_["sil"])
                        act.wait_ge(o_["ht"], o + 1)
                        hidden_out(0, o_["hte"])

            norm(0)
            norm_out(0)
            act.wait_ge(s_zfv, 2)
            then(nc.scalar.activation(zf[2], zf[1], ACT.Exp))
            nc.scalar.activation(zf[1], zf[2], ACT.Ln, bias=1.0).then_inc(s_zfa, 1)
            features_out(Q, -0.125, H)
            features_out(K, 1.0, H)
            rows_out()
            attention(DIL)
            features_out(Q, -0.125, H)
            features_out(K, 1.0, H)
            rows_out()
            attention(FOX)
            norm(1)
            norm_out(1)
            routing(0)
            experts(0)
            further_tiles(0)
            norm(2)
            norm_out(2)
            features_out(Q, -0.125, H)
            features_out(K, 1.0, 2)
            b = next_group()
            nc.scalar.activation(V[0:64, :, 0:128], b[0:64, :].rearrange("p (c n) -> p c n", c=C), ACT.Copy)\
              .then_inc(s_pjA, 1)
            attention(SWA)
            for c in range(C):
                b = next_group()
                nc.scalar.activation(cq_row[0:64, c, 0:512], b[0:64, :], ACT.Copy).then_inc(s_pjA, 1)
            for c in (0, 2):
                b = next_group()
                nc.scalar.activation(cq_row[0:64, c:c + 2, 512:672],
                                     b[0:64, 0:320].rearrange("p (c n) -> p c n", c=2), ACT.Copy).then_inc(s_pjA, 1)
            act.wait_ge(s_pjA, 36)
            act.wait_ge(s_pjV, 36)
            for c in range(C):
                nc.scalar.activation(junk[:, 0:QR], cq_row[:, c, 0:QR], ACT.Square, accum_out=ssq[:, c:c + 1])\
                  .then_inc(s_lsq, 1)
                nc.scalar.activation(junk[:, 512:512 + KVR], cq_row[:, c, QR:QR + KVR], ACT.Square,
                                     accum_out=ssq[:, 4 + c:5 + c]).then_inc(s_lsq, 1)
                act.wait_ge(s_lsq, 2 * c + 2)
            act.wait_ge(s_lms, 1)
            nc.scalar.activation(rstd[:, :], ssq[:, :], ACT.Sqrt).then_inc(s_lrt, 1)
            for c in range(C):
                act.wait_ge(s_lt, 2 * c + 1)
                nc.scalar.activation(hnT[:, 0:4, 128 * c:128 * c + 128],
                                     bank[3][:, :].rearrange("p (k t) -> p k t", k=4), ACT.Copy).then_inc(s_ltA, 1)
            for hh in range(H):
                b = next_group()
                nc.scalar.activation(Q[0:64, hh, :], b[0:64, :], ACT.Copy, scale=-((NOPE + ROPE) ** -0.5))\
                  .then_inc(s_pjA, 1)
            features_out(K, 1.0, H)
            rows_out()
            attention(MLA)
            norm(3)
            norm_out(3)
            routing(1)
            experts(1)
            further_tiles(1)
            norm(4)

        @block.vector
        def _(dve):
            order = [0]
            group = [0]

            def then(ins):
                order[0] += 1
                ins.then_inc(s_dv, 1)
                dve.wait_ge(s_dv, order[0])

            def norm(v):
                dve.wait_ge(s_sq, 4 * v + 4)
                nc.vector.tensor_scalar(ssq[:, 0:4], ssq[:, 0:4], 1.0 / DM, 1e-6, ALU.mult, ALU.add).then_inc(s_ms, 1)
                dve.wait_ge(s_sqrt, v + 1)
                then(nc.vector.reciprocal(rstd[:, 0:4], rstd[:, 0:4]))
                dve.wait_ge(s_gain, 16 * (v + 1))
                for c in range(C):
                    nc.vector.scalar_tensor_tensor(hn_row[:, c, :], h[:, c, :], rstd[:, c:c + 1], gain,
                                                   ALU.mult, ALU.mult).then_inc(s_hn, 1)
                    if c and v < 4:
                        norm_out(v, c - 1)
                if v < 4:
                    norm_out(v, C - 1)

            def norm_out(v, c):
                dve.wait_ge(s_nt, 8 * v + 2 * c + 2)
                nc.vector.tensor_copy(hnT[:, 4:8, 128 * c:128 * c + 128],
                                      bank[4][:, :].rearrange("p (k t) -> p k t", k=4)).then_inc(s_ntV, 1)

            def next_group():
                g = group[0]
                dve.wait_ge(s_pj, g + 1)
                group[0] += 1
                return bank[6 + g % 2]

            def features_out(dst, scale, heads):
                for hh in range(1, heads, 2):
                    b = next_group()
                    nc.vector.tensor_scalar(dst[0:64, hh, :], b[64:128, :], scale, None, ALU.mult).then_inc(s_pjV, 1)

            def rows_out():
                for c in range(C):
                    b = next_group()
                    nc.vector.tensor_copy(V[64:128, c, :], b[64:128, :]).then_inc(s_pjV, 1)

            def masks(f, u):
                g = H * f + u
                if g >= 2:
                    dve.wait_ge(s_tr, 4 * (g - 1))
                at, width = MASK[f]
                for i in range(4):
                    b, n = 4 * g + i, LEN[f][i]
                    dve.wait_ge(s_qk, b + 1)
                    start = sinks[:, H + u:H + u + 1] if f == SWA else 3e38
                    nc.vector.tensor_tensor_reduce(
                        out=P[:, u % 2, p_col(f, i):p_col(f, i) + n], in0=bank[b % 3][:, 0:n],
                        in1=cst[:, at + width - n:at + width], scale=1.0, scalar=start,
                        op0=ALU.add, op1=ALU.min, accum_out=nm[:, b % 8:b % 8 + 1]).then_inc(s_msk, 1)

            def invert(f, u):
                for i in range(4):
                    b = 4 * (H * f + u) + i
                    d = den[:, b % 8:b % 8 + 1]
                    dve.wait_ge(s_exp, b + 1)
                    if f == SWA:
                        then(nc.vector.tensor_tensor(d, d, esink[:, b % 8:b % 8 + 1], ALU.add))
                    nc.vector.reciprocal(rden[:, b % 8:b % 8 + 1], d).then_inc(s_rd, 1)

            def probs_out(f, u, j):
                g = H * f + u
                dve.wait_ge(s_tr, 4 * g + j + 1)
                if g:
                    dve.wait_ge(s_pv, g)
                n = 128 * len(q_chunks(f, j))
                nc.vector.tensor_copy(PT[:, pt_col(f, j):pt_col(f, j) + n], bank[4][:, 0:n]).then_inc(s_teV, 1)

            def attention(f):
                masks(f, 0)
                invert(f, 0)
                for u in range(H):
                    if u + 1 < H:
                        masks(f, u + 1)
                    probs_out(f, u, 1)
                    probs_out(f, u, 3)
                    if u + 1 < H:
                        invert(f, u + 1)

            def mixer_add(lay):
                for half in range(2):
                    for c in range(C):
                        g = 8 * lay + 4 * half + c
                        dve.wait_ge(s_og, g + 1)
                        part = h[:, c, 512 * half:512 * half + 512]
                        nc.vector.tensor_tensor(part, bank[g % 2][:, :], part, ALU.add).then_inc(s_oga, 1)

            def first_at(value, best, score, at_best, onehot):
                n = value.shape[2]
                bb = best.unsqueeze(2).to_broadcast([128, C, n])
                io = iota[:, 0:n].unsqueeze(1).to_broadcast([128, C, n])
                then(nc.vector.tensor_tensor(score, value, bb, ALU.is_ge))
                then(nc.vector.scalar_tensor_tensor(score, score, -64.0, io, ALU.mult, ALU.add))
                then(nc.vector.tensor_reduce(at_best, score, X, ALU.min))
                then(nc.vector.tensor_tensor(onehot, score, at_best.unsqueeze(2).to_broadcast([128, C, n]),
                                             ALU.is_equal))

            def routing(lay):
                dve.wait_ge(s_lg, lay + 1)
                then(nc.vector.tensor_tensor(lg, bank[6][:, 0:144].rearrange("p (c n) -> p c n", c=C),
                                             rbias.unsqueeze(1).to_broadcast([128, C, 36]), ALU.add))
                glog = lg[:, :, 0:4]
                then(nc.vector.tensor_reduce(gmax, glog, X, ALU.max))
                nc.vector.tensor_tensor(gexp, glog, gmax.unsqueeze(2).to_broadcast([128, C, 4]), ALU.subtract)\
                  .then_inc(s_rsub, 1)
                first_at(glog, gmax, gpick, gmin, goh)
                then(nc.vector.tensor_scalar(gpen, goh, BIG, -BIG, ALU.mult, ALU.add))
                e4 = em[0].rearrange("p c (g e) -> p c g e", g=4)
                then(nc.vector.tensor_tensor(e4, lg[:, :, 4:36].rearrange("p c (g e) -> p c g e", g=4),
                                             goh.unsqueeze(3).to_broadcast([128, C, 4, 8]), ALU.mult))
                then(nc.vector.tensor_tensor(e4, e4, gpen.unsqueeze(3).to_broadcast([128, C, 4, 8]), ALU.add))
                then(nc.vector.tensor_reduce(emax[0], em[0], X, ALU.max))
                first_at(em[0], emax[0], pick[0], emin[0], oh[0])
                then(nc.vector.scalar_tensor_tensor(em[1], oh[0], -3 * BIG, em[0], ALU.mult, ALU.add))
                then(nc.vector.tensor_reduce(emax[1], em[1], X, ALU.max))
                first_at(em[1], emax[1], pick[1], emin[1], oh[1])
                nc.vector.tensor_tensor(ed, emax[1], emax[0], ALU.subtract).then_inc(s_rsub, 1)
                nc.vector.tensor_tensor(ohs, oh[0], oh[1], ALU.add).then_inc(s_oh, 1)
                dve.wait_ge(s_rexp, 2 * lay + 2)
                then(nc.vector.tensor_reduce(gsum, gexp, X, ALU.add))
                nc.vector.tensor_scalar(esum, ed, 1.0, None, ALU.add)
                then(nc.vector.reciprocal(gw, gsum))
                then(nc.vector.reciprocal(einv, esum))
                then(nc.vector.tensor_tensor(wgt[:, 0, :], einv, gw, ALU.mult))
                then(nc.vector.tensor_tensor(wgt[:, 1, :], wgt[:, 0, :], ed, ALU.mult))
                recv = rec.rearrange("p (n w) -> p n w", w=4)
                ids = cst[:, C_TOK:C_TOK + 16].rearrange("p (w n) -> p n w", w=2)
                nc.vector.tensor_copy(recv[:, :, 0:2], ids)
                nc.vector.tensor_copy(recv.bitcast(f32)[:, :, 2:4],
                                      wgt.rearrange("p k c -> p (k c)").unsqueeze(2).to_broadcast([128, 8, 2]))
                dve.wait_ge(s_rank, lay + 1)
                rank = bank[7][:, 0:128].rearrange("p (c n) -> p c n", c=C)
                for k in range(2):
                    then(nc.vector.tensor_tensor(pick[k], rank, oh[k], ALU.mult))
                    then(nc.vector.tensor_reduce(rpos[k], pick[k], X, ALU.add))
                    then(nc.vector.scalar_tensor_tensor(rpos[k], rpos[k], float(NE), emin[k], ALU.mult, ALU.add))
                    last = nc.vector.tensor_scalar(slot[:, 4 * k:4 * k + 4], rpos[k], 64.0, None, ALU.add)
                last.then_inc(s_slot, 1)
                cnt = bank[7][0:1, 128:160]
                big = [ovbig[i].rearrange("p (a b) -> p a b", b=NE) for i in range(2)]
                b7 = ovbig[0][:, 0:224].rearrange("p (e t) -> p e t", t=7)
                then(nc.vector.tensor_copy(ends, cnt))
                then(nc.vector.tensor_tensor(b7, ends.unsqueeze(2).to_broadcast([1, NE, 7]),
                                             cst[0:1, C_THR:C_THR + 7].unsqueeze(1).to_broadcast([1, NE, 7]), ALU.is_gt))
                then(nc.vector.tensor_reduce(extra, b7, X, ALU.add))
                then(nc.vector.memset(ovbig[1][:, 0:NE], 0.0))
                then(nc.vector.tensor_tensor_scan(ends, extra, ovbig[1][:, 0:NE], 0.0, ALU.add, ALU.add))
                then(nc.vector.tensor_tensor(big[0], ends.unsqueeze(1).to_broadcast([1, MAXOV, NE]),
                                             cst[0:1, C_IOTA:C_IOTA + MAXOV].unsqueeze(2).to_broadcast([1, MAXOV, NE]),
                                             ALU.is_le))
                then(nc.vector.tensor_tensor(big[1], big[0], extra.unsqueeze(1).to_broadcast([1, MAXOV, NE]), ALU.mult))
                then(nc.vector.tensor_reduce(oe, big[0], X, ALU.add))
                then(nc.vector.tensor_reduce(ostart, big[1], X, ALU.add))
                then(nc.vector.tensor_tensor(ostart, cst[0:1, C_IOTA + 1:C_IOTA + 1 + MAXOV], ostart, ALU.subtract))
                nc.vector.tensor_copy(ncells[:, 0:1], ends[:, NE - 1:NE])
                nc.vector.tensor_copy(ncells[:, 1:1 + MAXOV], oe)
                nc.vector.tensor_copy(ncells[:, 1 + MAXOV:1 + 2 * MAXOV], ostart).then_inc(s_ncell, 1)

            def indices(gather_idx, scatter_idx, records, done):
                half = cst[:, C_HALF:C_HALF + 1]
                nc.vector.tensor_scalar(gather_idx, records[:, :, 0], half, None, ALU.add)
                nc.vector.tensor_scalar(scatter_idx, records[:, :, 1], half, None, ALU.add).then_inc(done, 1)

            def hidden(e2, weight, done):
                nc.vector.scalar_tensor_tensor(hid[e2][64:128, :], bank[2 + e2][64:128, 0:256], weight,
                                               sil[e2][64:128, :], ALU.mult, ALU.mult).then_inc(done, 1)

            def experts(lay):
                base = NE * lay
                dve.wait_ge(s_recs, 32 * (lay + 1))
                indices(gidx, sidx, recs.rearrange("p (e w) -> p e w", w=4), s_idx)
                weights = recs.bitcast(f32)
                dve.wait_ge(s_xt, base + 1)
                nc.vector.tensor_copy(XT[0], bank[0][:, :]).then_inc(s_xte, 1)

                def step(e, e2, wcol, more, scattered):
                    dve.wait_ge(s_sil, e + (base + 1))
                    hidden(e2, weights[64:128, wcol], s_hid)
                    if more:
                        dve.wait_ge(s_xt, e + (base + 2))
                        nc.vector.tensor_copy(XT[1 - e2], bank[1 - e2][:, :]).then_inc(s_xte, 1)
                    dve.wait_ge(s_y, e + (base + 1))
                    if scattered is not None:
                        dve.wait_ge(s_sc[e2], scattered)
                    nc.vector.tensor_copy(Y[e2], bank[5 + e2][:, :]).then_inc(s_ye, 1)

                for e in range(2):
                    step(e, e, slice(4 * e + 2, 4 * e + 3), True, 8 * base if base else None)
                with dve.Fori(2, NE - 3, 2) as e:
                    for e2 in range(2):
                        step(e + e2, e2, bass.ds(dve.snap(e * 4 + (4 * e2 + 2)), 1), True, e * 8 + 8 * base)
                for e2 in range(2):
                    e = NE - 2 + e2
                    step(e, e2, slice(4 * e + 2, 4 * e + 3), e2 == 0, 8 * (base + NE - 2))

            def further_tiles(lay):
                o_ = ov[lay]
                n_over = dve.value_load(ncells[0:1, 0:1], min_val=0, max_val=MAXOV)
                with dve.If(n_over > 0):
                    dve.wait_ge(s_sc[0], 256 * (lay + 1))
                    with dve.Fori(0, n_over) as o:
                        dve.wait_ge(o_["records"], o * 32 + 32)
                        indices(oidx[:, 0:1], oidx[:, 1:2], orec.unsqueeze(1), o_["indices"])
                        dve.wait_ge(o_["xt"], o + 1)
                        nc.vector.tensor_copy(XT[0], bank[0][:, :]).then_inc(o_["xte"], 1)
                        dve.wait_ge(o_["sil"], o + 1)
                        hidden(0, orec.bitcast(f32)[64:128, 2:3], o_["hid"])
                        dve.wait_ge(o_["y"], o + 1)
                        nc.vector.tensor_copy(Y[0], bank[5][:, :]).then_inc(o_["ye"], 1)

            def add_expert_rows(lay):
                for c in range(C):
                    dve.wait_ge(s_yld[c % 2], 16 * (2 * lay + c // 2 + 1))
                    for k in range(2):
                        ins = nc.vector.tensor_tensor(h[:, c, :], h[:, c, :], y_in[c % 2][:, DM * k:DM * k + DM], ALU.add)
                        if k == 0:
                            then(ins)
                    ins.then_inc(s_yadd, 1)

            dve.wait_ge(s_const, 16)
            dve.wait_ge(s_heads, 32)
            nc.vector.tensor_scalar(sinks[:, H:2 * H], sinks[:, 0:H], -1.0, None, ALU.mult)
            norm(0)
            dve.wait_ge(s_zf, 1)
            nc.vector.tensor_scalar(zf[0], bank[5][0:8, :], bf_sb[:, 0:1], None, ALU.add).then_inc(s_zfv, 1)
            dve.wait_ge(s_zfv, 1)
            nc.vector.scalar_tensor_tensor(zf[1], zf[0], -1.0, zf[0], ALU.mult, ALU.min).then_inc(s_zfv, 1)
            features_out(Q, -0.125, H)
            dve.wait_ge(s_zfa, 1)
            nc.vector.scalar_tensor_tensor(zf[0], zf[0], 0.0, zf[1], ALU.min, ALU.subtract).then_inc(s_zfv, 1)
            dve.wait_ge(s_zfv, 3)
            then(nc.vector.memset(zf[1], 0.0))
            nc.vector.tensor_tensor_scan(zf[2], zf[0], zf[1], 0.0, ALU.add, ALU.add).then_inc(s_zfv, 1)
            dve.wait_ge(s_zfv, 4)
            nc.vector.tensor_scalar(zf[3], zf[2], -1.0, None, ALU.mult).then_inc(s_zfv, 1)
            features_out(K, 1.0, H)
            rows_out()
            attention(DIL)
            features_out(Q, -0.125, H)
            features_out(K, 1.0, H)
            rows_out()
            attention(FOX)
            mixer_add(0)
            norm(1)
            routing(0)
            experts(0)
            further_tiles(0)
            add_expert_rows(0)
            norm(2)
            features_out(Q, -0.125, H)
            features_out(K, 1.0, 2)
            b = next_group()
            nc.vector.tensor_copy(V[64:128, :, 0:128], b[64:128, :].rearrange("p (c n) -> p c n", c=C)).then_inc(s_pjV, 1)
            attention(SWA)
            for c in range(C):
                b = next_group()
                nc.vector.tensor_copy(cq_row[64:128, c, 0:512], b[64:128, :]).then_inc(s_pjV, 1)
            for c in (0, 2):
                b = next_group()
                nc.vector.tensor_copy(cq_row[64:128, c:c + 2, 512:672],
                                      b[64:128, 0:320].rearrange("p (c n) -> p c n", c=2)).then_inc(s_pjV, 1)
            dve.wait_ge(s_pjA, 36)
            dve.wait_ge(s_pjV, 36)
            dve.wait_ge(s_small, 144)
            t1, t2 = cq_row[:, :, 640:656], cq_row[:, :, 656:672]
            for a, (t, cs) in enumerate(((t1, 0), (t2, 1), (t1, 1), (t2, 0))):
                nc.vector.tensor_tensor(ktmp[:, a, :, :], t, krot[:, cs, :, :], ALU.mult)
            then(nc.vector.memset(kpe_pad[:, :, 0:64], 0.0))
            for at in (64, 96):
                nc.vector.tensor_tensor(kpe_pad[:, :, at:at + 16], ktmp[:, 0], ktmp[:, 1], ALU.subtract)
                nc.vector.tensor_tensor(kpe_pad[:, :, at + 16:at + 32], ktmp[:, 2], ktmp[:, 3], ALU.add)
            dve.wait_ge(s_lsq, 8)
            nc.vector.tensor_scalar(ssq[:, 0:4], ssq[:, 0:4], 1.0 / QR, 1e-6, ALU.mult, ALU.add)
            nc.vector.tensor_scalar(ssq[:, 4:8], ssq[:, 4:8], 1.0 / KVR, 1e-6, ALU.mult, ALU.add).then_inc(s_lms, 1)
            dve.wait_ge(s_lrt, 1)
            then(nc.vector.reciprocal(rstd[:, :], rstd[:, :]))

            def latent_out(c):
                dve.wait_ge(s_lt, 2 * c + 2)
                nc.vector.tensor_copy(hnT[:, 4, 128 * c:128 * c + 128], bank[4][:, 0:128])
                nc.vector.tensor_copy(K[64:128, :, 128 * c:128 * c + 128],
                                      bank[4][64:128, 128:256].unsqueeze(1).to_broadcast([64, H, 128])).then_inc(s_ltV, 1)

            for c in range(C):
                nc.vector.scalar_tensor_tensor(cq_row[:, c, 0:QR], cq_row[:, c, 0:QR], rstd[:, c:c + 1],
                                               qkv_gain[:, 0:QR], ALU.mult, ALU.mult)
                nc.vector.scalar_tensor_tensor(cq_row[:, c, QR:QR + KVR], cq_row[:, c, QR:QR + KVR], rstd[:, 4 + c:5 + c],
                                               qkv_gain[:, QR:QR + KVR], ALU.mult, ALU.mult).then_inc(s_lrow, 1)
                if c:
                    latent_out(c - 1)
            latent_out(C - 1)
            for hh in range(H):
                b = next_group()
                nc.vector.tensor_tensor(Q[64:128, hh, :], b[64:128, :], qrot[64:128, :], ALU.mult).then_inc(s_pjV, 1)
            features_out(K, 1.0, H)
            rows_out()
            attention(MLA)
            mixer_add(1)
            norm(3)
            routing(1)
            experts(1)
            further_tiles(1)
            add_expert_rows(1)
            norm(4)


_INS = ["x", "attn_norm", "ffn_norm", "final_norm", "e_w_in", "e_b_f", "e_w_out", "o_w_in", "o_q_norm", "o_kv_norm",
        "o_w_uq", "o_w_ukv", "o_sinks", "o_w_out", "moe_w_group", "moe_b_group", "moe_w_router", "moe_b_router",
        "moe_w_gate", "moe_w_up", "moe_w_down"]


def kernel(**inputs):
    import concourse.bacc as bacc
    from concourse.bass_utils import run_bass_kernel_spmd

    nc = bacc.Bacc("TRN2", target_bir_lowering=False, num_devices=1)
    arrays, args = {}, []
    consts = shape_constants()
    for name in _INS + list(consts):
        a = np.ascontiguousarray(inputs[name] if name in inputs else consts[name])
        arrays[f"in_{name}"] = a
        args.append(nc.dram_tensor(f"in_{name}", a.shape, mybir.dt.from_np(a.dtype), kind="ExternalInput").ap())
    args.append(nc.dram_tensor("out_0", (1, S, DM), mybir.dt.float32, kind="ExternalOutput").ap())
    trunk(nc, *args)
    return run_bass_kernel_spmd(nc, [arrays], core_ids=[0]).results[0]["out_0"]
```

```python
import concourse.bass as bass
from concourse import mybir
from contextlib import ExitStack
import numpy as np

DM, S, C = 1024, 512, 4
KD = DM // 128
H, HD = 8, 64
NE, DE, SLOTS = 32, 256, 64
QR, KVR, NOPE, ROPE = 384, 256, 64, 32
OOB = 1 << 20
BIG = 1e30
MAXOV = (2 * S - 1) // SLOTS

C_ID, C_TRI, C_ONE, C_CAUSAL, C_DIL, C_SWA = 0, 128, 256, 384, 896, 1408
C_IOTA, C_TOK, C_OOB, C_THR, C_EPS, C_RANK = 1664, 1696, 1712, 1713, 1720, 1721
C_END = 1721 + 128


def shape_constants():
    p = np.arange(128)[:, None]
    t = np.zeros((128, C_END), np.float32)
    t[:, C_ID:C_ID + 128] = np.eye(128)
    t[:, C_TRI:C_TRI + 128] = p < np.arange(128)[None, :]
    t[:, C_ONE:C_ONE + 128] = 1.0
    d = p - np.arange(512)[None, :] + 384
    t[:, C_CAUSAL:C_CAUSAL + 512] = np.where(d >= 0, 0.0, BIG)
    count = (d >= 0) * ((d <= 128) * 1 + (d % 4 == 0) * 1 + (d % 16 == 0) * 1)
    t[:, C_DIL:C_DIL + 512] = np.where(count > 0, -np.log(np.maximum(count, 1)), BIG)
    d = 128 + p - np.arange(256)[None, :]
    t[:, C_SWA:C_SWA + 256] = np.where((d >= 0) & (d <= 127), 0.0, BIG)
    t[:, C_IOTA:C_IOTA + 32] = np.arange(32)
    tok = np.arange(C)[None, :] * 128 + p
    for k in range(2):
        t[:, C_TOK + 4 * k:C_TOK + 4 * k + 4] = 2 * tok
        t[:, C_TOK + 8 + 4 * k:C_TOK + 12 + 4 * k] = 2 * (2 * tok + k)
    t[:, C_OOB:C_OOB + 1] = OOB + (p >= 64)
    t[:, C_EPS] = 1e-6
    t[:, C_RANK:C_RANK + 128] = np.arange(128) % SLOTS
    t[:, C_THR:C_THR + 7] = SLOTS * np.arange(1, 8)
    slope = 2.0 ** -np.arange(1, H + 1)
    pos = np.arange(S) - 256.0
    aug = np.zeros((4, H, S), np.float32)
    aug[0] = slope[:, None] * pos[None, :]
    aug[1] = -slope[:, None]
    aug[2] = 1.0
    aug[3] = pos[None, :]
    inv = np.float32(10000.0) ** (-np.arange(0, ROPE, 2, dtype=np.float32) / np.float32(ROPE))
    ang = (np.arange(S, dtype=np.float32)[:, None] * inv[None, :]).astype(np.float64)
    cos, sin = np.cos(ang), np.sin(ang)
    sc = -((NOPE + ROPE) ** -0.5)
    qrot = np.zeros((128, S), np.float32)
    qrot[64:80] = qrot[80:96] = sc * cos.T
    qrot[96:112] = -sc * sin.T
    qrot[112:128] = sc * sin.T
    krot = np.zeros((128, 2, C, 16), np.float32)
    krot[:, 0] = cos.reshape(C, 128, 16).transpose(1, 0, 2)
    krot[:, 1] = sin.reshape(C, 128, 16).transpose(1, 0, 2)
    return {"const_table": t, "const_aug": aug.reshape(4, H * S), "const_qrot": qrot,
            "const_krot": krot.reshape(128, 128)}


def trunk(nc, x, attn_norm, ffn_norm, final_norm, e_w_in, e_b_f, e_w_out, o_w_in, o_q_norm, o_kv_norm,
          o_w_uq, o_w_ukv, o_sinks, o_w_out, moe_w_group, moe_b_group, moe_w_router, moe_b_router,
          moe_w_gate, moe_w_up, moe_w_down, const_table, const_aug, const_qrot, const_krot, out):
    f32, i32 = mybir.dt.float32, mybir.dt.int32
    ALU, ACT = mybir.AluOpType, mybir.ActivationFunctionType
    X = mybir.AxisListType.X

    hn_dram = [nc.dram_tensor(f"hn_rows{l}", (2 * S, DM // 2), f32, kind="Internal").ap() for l in range(2)]
    tab_dram = [nc.dram_tensor(f"expert_table{l}", (S * NE, 4), i32, kind="Internal").ap() for l in range(2)]
    c_dram = nc.dram_tensor("forget_sums", (2, H * S), f32, kind="Internal").ap()
    y_dram = [nc.dram_tensor(f"expert_rows{l}", (2 * 2 * S, DM // 2), f32, kind="Internal").ap() for l in range(2)]

    wg_v = [moe_w_gate[l].rearrange("g e (h p k) f -> (g e) p h (k f)", h=2, p=128) for l in range(2)]
    wu_v = [moe_w_up[l].rearrange("g e (h p k) f -> (g e) p h (k f)", h=2, p=128) for l in range(2)]
    wd_v = [moe_w_down[l].rearrange("g e (p c) d -> (g e) p (c d)", p=128) for l in range(2)]
    ewin_v = e_w_in.rearrange("a (k p) n -> p (a k) n", p=128)
    owin_v = o_w_in.rearrange("a (k p) n -> p (a k) n", p=128)
    ewout_v = e_w_out.rearrange("a (k p) n -> p (a k) n", p=128)
    owout_v = o_w_out.rearrange("a (k p) n -> p (a k) n", p=128)

    fw = H * HD
    FOX0, ZF0, DIL0 = 0, 3 * fw, 3 * fw + H
    EVEN_COLS = [DIL0, DIL0 + fw, DIL0 + 2 * fw, FOX0, FOX0 + fw, FOX0 + 2 * fw]
    QS0 = QR + KVR + ROPE
    KS0 = QS0 + fw
    BESIDE = [4, 5, 10, 11]
    LOOP0 = BESIDE[-1] + 1
    T_ODD = 8 + NE - len(BESIDE)
    T_MOE = [8, T_ODD + 8]

    def expert_tile(lay, e):
        return T_MOE[lay] + e - sum(b < e for b in BESIDE)

    DIL, FOX, SWA, MLA = range(4)
    LEN = {f: [128 * (i + 1) for i in range(4)] for f in (DIL, FOX, MLA)}
    LEN[SWA] = [128, 256, 256, 256]
    FIRST_KEY = {f: [0] * 4 for f in (DIL, FOX, MLA)}
    FIRST_KEY[SWA] = [0, 0, 1, 2]
    MASK = {DIL: (C_DIL, 512), FOX: (C_CAUSAL, 512), MLA: (C_CAUSAL, 512), SWA: (C_SWA, 256)}

    def p_col(f, i):
        return sum(LEN[f][:i])

    def q_chunks(f, j):
        return [i for i in range(4) if FIRST_KEY[f][i] <= j <= i]

    def pt_col(f, j):
        return sum(128 * len(q_chunks(f, jj)) for jj in range(j))

    ctx = ExitStack()
    with ctx:
        def sb(name, shape, dt=f32):
            return ctx.enter_context(nc.sbuf_tensor(name, shape, dt))

        def sem(name):
            return ctx.enter_context(nc.semaphore(name))

        h = sb("h", [128, C, DM])
        hnT = sb("hnT", [128, KD, S])
        Q = sb("Q", [128, H, S])
        K = sb("K", [128, H, S])
        oT = sb("oT", [128, KD, S])
        V = sb("V", [128, C, 512])
        W = [sb(f"W{i}", [128, 4096]) for i in range(4)]
        D = [sb(f"D{i}", [128, 2048]) for i in range(4)]
        P = sb("P", [128, 2, 1280])
        PT = sb("PT", [128, 1280])
        cst = sb("cst", [128, C_END])
        nm = sb("nm", [128, 8])
        den = sb("den", [128, 8])
        rden = sb("rden", [128, 8])
        esink = sb("esink", [128, 8])
        sinks = sb("sinks", [128, 2 * H])
        ssq = sb("ssq", [128, 8])
        rstd = sb("rstd", [128, 8])
        ncells = sb("ncells", [1, 32], i32)
        turn = sb("turn", [1, 4])
        bf_sb = sb("bf_sb", [8, 1])
        warm = sb("warm", [1, 4])
        bank = [ctx.enter_context(nc.psum_tensor(f"bank{i}", [128, 512], f32)) for i in range(8)]

        ident = cst[:, C_ID:C_ID + 128]
        iota = cst[:, C_IOTA:C_IOTA + 32]

        hn_row = Q[:, :, :].rearrange("p h s -> p (h s)").rearrange("p (c d) -> p c d", c=C)
        flatQ = Q[:, :, :].rearrange("p h s -> p (h s)")
        flatK = K[:, :, :].rearrange("p h s -> p (h s)")
        flatV = V[:, :, :].rearrange("p c s -> p (c s)")
        flatO = oT[:, :, :].rearrange("p k s -> p (k s)")
        flatT = hnT[:, :, :].rearrange("p k s -> p (k s)")
        WB, DB = [flatO, flatQ], [flatT[:, 0:2048], flatT[:, 2048:4096]]
        gain = P[:, 0, 0:DM]
        eps = cst[:, C_EPS:C_EPS + 1]
        Xg = [flatK[:, 512 * i:512 * i + 512] for i in range(4)]
        XT = [flatK[:, 2048 + 512 * i:2560 + 512 * i] for i in range(2)]
        sil = [PT[:, 256 * i:256 * i + 256] for i in range(2)]
        hid = [PT[:, 512 + 256 * i:768 + 256 * i] for i in range(2)]
        hT = [PT[:, 1024 + 128 * i:1152 + 128 * i] for i in range(2)]
        Y = [flatV[:, 512 * i:512 * i + 512] for i in range(2)]
        wr = flatV[:, 1024:1312].rearrange("p (k n) -> p k n", k=KD)
        rbias = flatV[:, 1312:1348]
        rec = flatV[:, 1348:1380].bitcast(i32)
        wtab = flatV[:, 1380:1412]
        pad = flatV[:, 1412:1444]
        gidx = flatV[:, 1508:1540].bitcast(i32)
        sidx = flatV[:, 1540:1572].bitcast(i32)
        slot = flatV[:, 1572:1580].bitcast(i32)
        ibuf = flatV[:, 1580:1588].bitcast(i32)
        orec = flatV[:, 1588:1592].bitcast(i32)
        oidx = flatV[:, 1592:1594].bitcast(i32)
        zf_w = D[2][:, 0:64].rearrange("p (k n) -> p k n", k=KD)
        zf = [D[3][0:8, 512 * i:512 * i + 512] for i in range(4)]
        junk = flatV[:, 0:1024]
        PTs = [PT[:, :], D[2][:, 640:1920]]
        pt_bank = [3, 4, 6, 7]
        cq_row = flatQ[:, 0:2688].rearrange("p (c n) -> p c n", c=C)
        kpe_pad = PT[:, 0:512].rearrange("p (c n) -> p c n", c=C)
        ktmp = PT[:, 512:768].rearrange("p (a c n) -> p a c n", a=4, c=C)
        qkv_gain = P[:, 0, 0:QR + KVR]
        qrot = P[:, 0, 640:1152]
        krot = P[:, 0, 1152:1280].rearrange("p (a c n) -> p a c n", a=2, c=C)
        y_in = [flatQ[:, 0:2048], flatK[:, 0:2048], flatQ[:, 2048:4096], flatK[:, 2048:4096]]
        tab_init = Xg[1].bitcast(i32)
        rank_hot = P[:, 0, 0:1024].rearrange("p (n r) -> p n r", n=2 * C)
        facts = PT[:, 0:1024].rearrange("p (n q e) -> p n q e", n=2 * C, q=4)

        R = P[:, 1, :]

        def r(at, *dims):
            n = int(np.prod(dims))
            v = R[:, at:at + n]
            if len(dims) == 2:
                v = v.rearrange("p (a b) -> p a b", a=dims[0])
            if len(dims) == 3:
                v = v.rearrange("p (a b c) -> p a b c", a=dims[0], b=dims[1])
            return v

        lg, gmax, gexp, gsum = r(0, 4, 36), r(144, 4), r(148, 4, 4), r(164, 4)
        gw, gpick, gmin, goh, gpen = r(168, 4), r(172, 4, 4), r(188, 4), r(192, 4, 4), r(208, 4, 4)
        em = [r(224, 4, 32), r(352, 4, 32)]
        pick = [r(480, 4, 32), r(608, 4, 32)]
        oh = [facts[:, 0:C, 3, :], facts[:, C:2 * C, 3, :]]
        ohs = r(992, 64).bitcast(mybir.dt.bfloat16).rearrange("p (c e) -> p c e", c=C)
        tri_ones = P[:, 0, 1024:1152].bitcast(mybir.dt.bfloat16)
        tri, ones = tri_ones[:, 0:128], tri_ones[:, 128:256]
        emax = [r(1120, 4), r(1124, 4)]
        emin = [r(1128, 4), r(1132, 4)]
        ed, esum, einv, wgt = r(1136, 4), r(1140, 4), r(1144, 4), r(1148, 2, 4)
        rpos = [r(1156, 4), r(1160, 4)]
        rslot = [r(736, 4), r(740, 4)]
        extra, ends = R[0:1, 1164:1196], R[0:1, 1196:1228]
        oe, ostart = R[0:1, 1228:1243], R[0:1, 1243:1258]
        ovbig = [P[0:1, 0, 0:480], P[0:1, 0, 480:960]]

        s_const = sem("const_loaded")
        s_heads = sem("head_constants_loaded")
        s_x = [sem(f"x_loaded{c}") for c in range(C)]
        s_small = sem("small_loaded")
        s_ld = [sem(f"tile_loaded{i}") for i in range(4)]
        s_lb = [sem(f"expert_beside_loaded{i}") for i in range(2)]
        s_half = sem("half_of_first_tile_loaded")
        s_gain = sem("gain_loaded")
        s_sq = sem("squares_summed")
        s_sqrt = sem("root_taken")
        s_hn = sem("normed_rows")
        s_nt = sem("norm_transposed")
        s_ntA = sem("norm_t_out_act")
        s_ntV = sem("norm_t_out_dve")
        s_pj = sem("projected")
        s_pjA = sem("proj_out_act")
        s_pjV = sem("proj_out_dve")
        s_aug = sem("position_rows")
        s_zf = sem("forget_logits")
        s_cst = sem("forget_sums_stored")
        s_zfa = sem("forget_act")
        s_zfv = sem("forget_dve")
        s_qk = sem("scores_ready")
        s_msk = sem("scores_masked")
        s_exp = sem("probs_ready")
        s_nrm = sem("probs_normalised")
        s_tr = sem("probs_transposed")
        s_teA = sem("probs_t_out_act")
        s_teV = sem("probs_t_out_dve")
        s_pv = sem("head_output")
        s_oev = sem("head_pair_out")
        s_og = sem("mixer_projected")
        s_oga = sem("mixer_added")
        s_lrow = sem("latent_rows_normed")
        s_lt = sem("latent_transposed")
        s_ltA = sem("latent_out_act")
        s_ltV = sem("latent_out_dve")
        s_lsq = sem("latent_squares")
        s_lms = sem("latent_mean_square")
        s_lrt = sem("latent_root")
        s_perm = sem("rotary_columns")
        s_hnst = sem("normed_rows_stored")
        s_lg = sem("router_logits")
        s_rsub = sem("router_differences")
        s_rexp = sem("router_exps")
        s_oh = sem("expert_one_hots")
        s_rank = sem("expert_ranks")
        s_facts = sem("slot_facts")
        s_slots = sem("slots_filled")
        s_idx = sem("expert_indices")
        s_ncell = sem("further_tiles_listed")
        s_slot0 = sem("further_tiles_over")
        s_ib = sem("index_column")
        s_g = [sem(f"rows_gathered{i}") for i in range(4)]
        s_xt = sem("rows_transposed")
        s_xte = sem("rows_t_out")
        s_gu = sem("gate_up_done")
        s_sil = sem("silu_done")
        s_hid = sem("hidden_done")
        s_ht = sem("hidden_transposed")
        s_hte = sem("hidden_t_out")
        s_y = sem("down_done")
        s_ye = sem("down_out")
        s_sc = [sem(f"rows_scattered{i}") for i in range(2)]
        ov = [{n: sem(f"further{l}_{n}") for n in
               ("loaded", "records", "indices", "gathered", "xt", "xte", "gu", "sil", "hid", "ht", "hte",
                "y", "ye", "scattered", "out", "init", "table")} for l in range(2)]
        s_yld = [sem(f"expert_rows_loaded{c}") for c in range(C)]
        s_yadd = sem("expert_rows_added")
        s_out = sem("output_stored")
        s_dv = sem("dve_order")
        s_av = sem("act_order")
        s_pl = sem("pool_order")

        block = ctx.enter_context(nc.Block())

        def tile_ready(n):
            return 48 * (n // 4 + 1)

        def last_read(n):
            if n < 6:
                return s_pj, 4 * (n + 1)
            if n < 8:
                return s_og, 4 * (n - 5)
            if n < T_ODD:
                return s_y, n - T_MOE[0] + len(BESIDE) + 1
            if n < T_ODD + 6:
                return s_pj, (28, 30, 34, 36, 44, 52)[n - T_ODD]
            return s_og, 8 + 4 * (n - T_ODD - 5)

        @block.sync
        def _(sp):
            for c in range(C):
                sp.dma_start(h[:, c, :], x[0, 128 * c:128 * c + 128, :]).then_inc(s_x[c], 16)
                if c == 0:
                    sp.dma_start(cst[:, :], const_table).then_inc(s_const, 16)

            def slot_free(n):
                if n >= 4:
                    sp.wait_ge(*last_read(n - 4))

            def load_cols(n, src, c0, width):
                slot_free(n)
                dst = W[n % 4][:, :].rearrange("p (k n) -> p k n", k=KD)
                sp.dma_start(dst[:, :, 0:width], src[:, :, c0:c0 + width]).then_inc(s_ld[n % 4], 48)

            def load_expert(lay, w, gate_up, down, done, down_free=None):
                for v, at in ((wg_v[lay], 0), (wu_v[lay], 2048)):
                    dst = gate_up[:, at:at + 2048].rearrange("p (h x) -> p h x", h=2)
                    sp.dma_start(dst, v[bass.ds(w, 1), :, :, :].rearrange("a p h x -> (a p) h x"))\
                      .then_inc(done, 16)
                if down_free is not None:
                    sp.wait_ge(*down_free)
                sp.dma_start(down, wd_v[lay][bass.ds(w, 1), :, :].rearrange("a p x -> (a p) x"))\
                  .then_inc(done, 16)

            def experts(lay):
                base = NE * lay
                for s in range(4):
                    slot_free(T_MOE[lay] + s)
                    load_expert(lay, s, W[s][:, :], D[s][:, :], s_ld[s])
                sp.wait_ge(s_og, 8 * (lay + 1))
                load_expert(lay, BESIDE[0], WB[0], DB[0], s_lb[0], (s_lg, C * (lay + 1)))
                sp.wait_ge(s_hnst, 64 * (lay + 1))
                load_expert(lay, BESIDE[1], WB[1], DB[1], s_lb[1])
                for e in range(6, LOOP0 + 4):
                    before = base + e - 6 + 1
                    sp.wait_ge(s_gu, before)
                    if e in BESIDE:
                        i = e % 2
                        load_expert(lay, e, WB[i], DB[i], s_lb[i], (s_y, before))
                    else:
                        s = expert_tile(lay, e) % 4
                        load_expert(lay, e, W[s][:, :], D[s][:, :], s_ld[s], (s_y, before))
                with sp.Fori(LOOP0 + 4, NE - 3, 4) as e:
                    for s in range(4):
                        w = sp.snap(e + s)
                        before = e + (base + s - 3)
                        sp.wait_ge(s_gu, before)
                        load_expert(lay, w, W[s][:, :], D[s][:, :], s_ld[s], (s_y, before))

            def further_tiles(lay):
                o_ = ov[lay]
                sp.wait_ge(s_ncell, lay + 1)
                n_over = sp.value_load(ncells[0:1, 0:1], min_val=0, max_val=MAXOV)
                with sp.If(n_over > 0):
                    sp.wait_ge(s_y, NE * (lay + 1))
                    with sp.Fori(0, n_over) as o:
                        ex = sp.value_load(ncells[0:1, bass.ds(o + 1, 1)], min_val=0, max_val=NE - 1)
                        rk = sp.value_load(ncells[0:1, bass.ds(o + (1 + MAXOV), 1)], min_val=1, max_val=7)
                        sp.wait_ge(o_["out"], o + 2)
                        load_expert(lay, ex, W[0][:, :], D[0][:, :], o_["loaded"])
                        tv = tab_dram[lay].rearrange("(r e) w -> r (e w)", e=NE)
                        for half in range(2):
                            sp.dma_start(orec[64 * half:64 * half + 64, :],
                                         tv[bass.ds(sp.snap(rk * SLOTS), SLOTS), bass.ds(sp.snap(ex * 4), 4)])\
                              .then_inc(o_["records"], 16)
                    sp.wait_ge(o_["out"], n_over + 2)
                    sp.sem_inc(s_slot0, 1)

            sp.wait_ge(s_gain, 16)
            for half in range(2):
                sp.dma_start(W[0][:, :].rearrange("p (k n) -> p k n", k=KD)[:, :, 256 * half:256 * half + 256],
                             ewin_v[:, :, DIL0 + 256 * half:DIL0 + 256 * half + 256])\
                  .then_inc((s_half, s_ld[0])[half], (16, 48)[half])
            for n, c0 in enumerate(EVEN_COLS):
                if n:
                    load_cols(n, ewin_v, c0, 512)
            for half in range(2):
                load_cols(6 + half, ewout_v, 512 * half, 512)
            experts(0)
            further_tiles(0)
            load_cols(T_ODD, owin_v, QS0, 512)
            load_cols(T_ODD + 1, owin_v, KS0, 256)
            sp.wait_ge(s_yld[C - 1], 16)
            load_cols(T_ODD + 2, owin_v, 0, 512)
            load_cols(T_ODD + 3, owin_v, 512, 160)
            slot_free(T_ODD + 4)
            for k in range(3):
                dst = W[(T_ODD + 4) % 4][:, 0:3072].rearrange("p (k h n) -> p k h n", k=3, h=H)
                sp.dma_start(dst[:, k, :, 0:96],
                             o_w_uq[0, 128 * k:128 * k + 128, :].rearrange("p (h n) -> p h n", h=H))\
                  .then_inc(s_ld[(T_ODD + 4) % 4], 16)
            slot_free(T_ODD + 5)
            sp.dma_start(W[(T_ODD + 5) % 4][:, 0:2048].rearrange("p (k n) -> p k n", k=2),
                         o_w_ukv.rearrange("a (k p) n -> p (a k) n", p=128)).then_inc(s_ld[(T_ODD + 5) % 4], 48)
            for half in range(2):
                load_cols(T_ODD + 6 + half, owout_v, 512 * half, 512)
            experts(1)
            further_tiles(1)
            for c in range(C):
                sp.wait_ge(s_hn, 16 + c + 1)
                sp.dma_start(out[0, 128 * c:128 * c + 128, :], hn_row[:, c, :]).then_inc(s_out, 16)
            sp.wait_ge(s_out, 16 * C)

        @block.gpsimd
        def _(pool):
            order = [0]
            last_half_row = pool.to_reg(2 * S - 1)
            last_result = pool.to_reg(4 * S - 1)

            def then(ins):
                order[0] += 1
                ins.then_inc(s_pl, 1)
                pool.wait_ge(s_pl, order[0])

            def hold(at=1):
                return nc.gpsimd.tensor_tensor(turn[:, at:at + 1], turn[:, 0:1], turn[:, 0:1], ALU.add)

            def load_gain(v):
                src = (attn_norm[0:1, :], ffn_norm[0:1, :], attn_norm[1:2, :], ffn_norm[1:2, :],
                       final_norm.rearrange("(a n) -> a n", a=1))[v]
                pool.dma_start(gain, src.partition_broadcast(128).rearrange("a b n -> a (b n)")).then_inc(s_gain, 16)

            load_gain(0)
            then(nc.gpsimd.memset(turn[:, :], 0.0))
            pool.dma_start(sinks[:, 0:H], o_sinks[0:1, :].partition_broadcast(128).rearrange("a b n -> a (b n)")
                           ).then_inc(s_heads, 16)
            pool.dma_start(bf_sb[:, :], e_b_f.rearrange("a n -> n a")).then_inc(s_heads, 16)

            def alibi_rows(kv_heads):
                pool.dma_start(Q[64:66, :, :].rearrange("p h s -> p (h s)"), const_aug[0:2, :]).then_inc(s_aug, 16)
                pool.dma_start(K[64:66, 0:kv_heads, :].rearrange("p h s -> p (h s)"),
                               const_aug[2:4, 0:kv_heads * S]).then_inc(s_aug, 16)

            def routing(lay):
                pool.wait_ge(s_oga, 8 * lay + 1)
                pool.dma_start(wr[:, :, 0:4], moe_w_group[lay].rearrange("(k p) n -> p k n", p=128)).then_inc(s_small, 16)
                pool.dma_start(wr[:, :, 4:36], moe_w_router[lay].rearrange("(k p) n -> p k n", p=128)).then_inc(s_small, 16)
                pool.dma_start(rbias[:, 0:4], moe_b_group[lay:lay + 1, :].partition_broadcast(128)
                               .rearrange("a b n -> a (b n)")).then_inc(s_small, 16)
                pool.dma_start(rbias[:, 4:36], moe_b_router[lay:lay + 1, :].partition_broadcast(128)
                               .rearrange("a b n -> a (b n)")).then_inc(s_small, 16)
                for c in range(C):
                    pool.wait_ge(s_hn, 4 * (2 * lay + 1) + c + 1)
                    pool.dma_start(hn_dram[lay].rearrange("(s h) d -> s (h d)", h=2)[128 * c:128 * c + 128, :],
                                   hn_row[:, c, :]).then_inc(s_hnst, 16)

            def gather(lay, dst, idx_col, done):
                pool.indirect_dma_start(out=dst, out_offset=None, in_=hn_dram[lay],
                                        in_offset=bass.IndirectOffsetOnAxis(ap=idx_col, axis=0),
                                        bounds_check=last_half_row, oob_is_err=False).then_inc(done, 16)

            def scatter(lay, src, idx_col, done):
                pool.indirect_dma_start(out=y_dram[lay],
                                        out_offset=bass.IndirectOffsetOnAxis(ap=idx_col, axis=0),
                                        in_=src, in_offset=None,
                                        bounds_check=last_result, oob_is_err=False).then_inc(done, 16)

            def expert_rows(lay):
                base = NE * lay
                pool.wait_ge(s_idx, lay + 1)
                pool.wait_ge(s_hnst, 64 * (lay + 1))

                for s in range(4):
                    nc.gpsimd.tensor_copy(ibuf[:, s:s + 1], gidx[:, s:s + 1]).then_inc(s_ib, 1)
                    pool.wait_ge(s_ib, 64 * lay + s + 1)
                    gather(lay, Xg[s], ibuf[:, s:s + 1], s_g[s])
                pool.wait_ge(s_ncell, lay + 1)
                load_gain(2 * lay + 2)

                def scatter_first(e, s, col):
                    pool.wait_ge(s_ye, e + (base + 1))
                    nc.gpsimd.tensor_copy(ibuf[:, 4 + s:5 + s], sidx[:, col]).then_inc(s_ib, 1)

                with pool.Fori(0, NE - 7, 4) as e0:
                    for s in range(4):
                        e = e0 + s
                        ahead = pool.snap(e0 + (s + 4))
                        scatter_first(e, s, bass.ds(pool.snap(e), 1))
                        pool.wait_ge(s_xt, e + (base + 1))
                        nc.gpsimd.tensor_copy(ibuf[:, s:s + 1], gidx[:, bass.ds(ahead, 1)]).then_inc(s_ib, 1)
                        pool.wait_ge(s_ib, e0 * 2 + (64 * lay + 2 * s + 6))
                        hold()
                        scatter(lay, Y[s % 2], ibuf[:, 4 + s:5 + s], s_sc[s % 2])
                        gather(lay, Xg[s], ibuf[:, s:s + 1], s_g[s])
                for s in range(4):
                    e = NE - 4 + s
                    scatter_first(e, s, slice(e, e + 1))
                    pool.wait_ge(s_ib, 64 * lay + 4 + 2 * (NE - 4) + s + 1)
                    scatter(lay, Y[s % 2], ibuf[:, 4 + s:5 + s], s_sc[s % 2])
                for s in range(2):
                    pool.wait_ge(s_sc[s], 16 * 16 * (lay + 1))

            def further_tiles(lay):
                o_ = ov[lay]
                pool.wait_ge(s_ncell, lay + 1)
                n_over = pool.value_load(ncells[0:1, 0:1], min_val=0, max_val=MAXOV)
                with pool.If(n_over > 0):
                    nc.gpsimd.memset(tab_init, OOB).then_inc(o_["out"], 1)
                    pool.wait_ge(o_["out"], 1)
                    pool.dma_start(tab_dram[lay].rearrange("(p r) w -> p (r w)", p=128), tab_init)\
                        .then_inc(o_["init"], 16)
                    pool.wait_ge(o_["init"], 16)
                    for kc in range(2 * C):
                        pool.indirect_dma_start(out=tab_dram[lay],
                                                out_offset=bass.IndirectOffsetOnAxis(ap=slot[:, kc:kc + 1], axis=0),
                                                in_=rec[:, 4 * kc:4 * kc + 4], in_offset=None,
                                                bounds_check=S * NE - 1, oob_is_err=False).then_inc(o_["table"], 16)
                    pool.wait_ge(o_["table"], 32 * C)
                    hold(3).then_inc(o_["out"], 1)
                    with pool.Fori(0, n_over) as o:
                        pool.wait_ge(o_["indices"], o + 1)
                        hold()
                        gather(lay, Xg[0], oidx[:, 0:1], o_["gathered"])
                        pool.wait_ge(o_["ye"], o + 1)
                        hold(2)
                        scatter(lay, Y[0], oidx[:, 1:2], o_["scattered"])
                        pool.wait_ge(o_["scattered"], o * 16 + 16)
                        hold(3).then_inc(o_["out"], 1)

            def load_expert_rows(lay):
                for c in range(C):
                    pool.dma_start(y_in[c], y_dram[lay].rearrange("(s f) d -> s (f d)", f=4)
                                   [128 * c:128 * c + 128, :]).then_inc(s_yld[c], 16)

            pool.dma_start(zf_w, ewin_v[:, :, ZF0:ZF0 + H]).then_inc(s_small, 16)
            then(nc.gpsimd.memset(K[64:128, :, :], 0.0))
            pool.wait_ge(s_nt, 8)
            alibi_rows(H)
            pool.wait_ge(s_zfv, 5)
            for i in range(2):
                pool.dma_start(c_dram[i].rearrange("(h s) -> h s", h=H), zf[2 + i]).then_inc(s_cst, 16)
            pool.wait_ge(s_cst, 32)
            pool.wait_ge(s_qk, 4 * H)
            pool.dma_start(Q[65:66, :, :].rearrange("p h s -> p (h s)"), const_aug[2:3, :]).then_inc(s_aug, 16)
            pool.dma_start(Q[64:65, :, :].rearrange("p h s -> p (h s)"), c_dram[1:2, :]).then_inc(s_aug, 16)
            pool.dma_start(K[65:66, :, :].rearrange("p h s -> p (h s)"), c_dram[0:1, :]).then_inc(s_aug, 16)
            pool.wait_ge(s_tr, 4 * 2 * H)
            load_gain(1)
            routing(0)
            expert_rows(0)
            further_tiles(0)
            load_expert_rows(0)
            pool.wait_ge(s_yadd, C)
            then(nc.gpsimd.memset(K[64:128, 0:2, :], 0.0))
            pool.wait_ge(s_nt, 8 * 3)
            alibi_rows(2)
            pool.wait_ge(s_tr, 4 * 3 * H)
            pool.dma_start(qkv_gain[:, 0:QR], o_q_norm[0:1, :].partition_broadcast(128)
                           .rearrange("a b n -> a (b n)")).then_inc(s_small, 16)
            pool.dma_start(qkv_gain[:, QR:QR + KVR], o_kv_norm[0:1, :].partition_broadcast(128)
                           .rearrange("a b n -> a (b n)")).then_inc(s_small, 16)
            pool.dma_start(qrot, const_qrot).then_inc(s_small, 16)
            pool.dma_start(P[:, 0, 1152:1280], const_krot).then_inc(s_small, 16)
            t = T_ODD + 4
            pool.wait_ge(s_ld[t % 4], tile_ready(t))
            uq = W[t % 4][:, 0:3072].rearrange("p (kh n) -> p kh n", n=128)
            nc.gpsimd.tensor_copy(uq[:, :, 96:112], uq[:, :, 80:96]).then_inc(s_perm, 1)
            nc.gpsimd.tensor_copy(uq[:, :, 112:128], uq[:, :, 64:80]).then_inc(s_perm, 1)
            pool.wait_ge(s_tr, 4 * 4 * H)
            load_gain(3)
            routing(1)
            expert_rows(1)
            further_tiles(1)
            load_expert_rows(1)

        @block.tensor
        def _(pe):
            pe.wait_ge(s_const, 16)
            group = [0]

            def group_start():
                g = group[0]
                if g >= 2:
                    pe.wait_ge(s_pjA, g - 1)
                    pe.wait_ge(s_pjV, g - 1)
                group[0] += 1
                return bank[6 + g % 2]

            def w_tile(n):
                return W[n % 4][:, :].rearrange("p (k n) -> p k n", k=KD)

            def router_logits(v, c):
                pe.wait_ge(s_ntA, 4 * v + c + 1)
                pe.wait_ge(s_ntV, 4 * v + c + 1)
                for k in range(KD):
                    last = nc.tensor.matmul(bank[6][:, 36 * c:36 * c + 36], hnT[:, k, 128 * c:128 * c + 128],
                                            wr[:, k, :], start=(k == 0), stop=(k == KD - 1))
                last.then_inc(s_lg, 1)

            def norm_transposes(v):
                if v % 2:
                    pe.wait_ge(s_small, (80, 208)[v // 2])
                for c in range(C):
                    pe.wait_ge(s_hn, 4 * v + c + 1)
                    for half in range(2):
                        if c or v:
                            pe.wait_ge((s_ntA, s_ntV)[half], 4 * v + c)
                        for kk in range(4):
                            k = 4 * half + kk
                            last = nc.tensor.transpose(bank[3 + half][:, 128 * kk:128 * kk + 128],
                                                       hn_row[:, c, 128 * k:128 * k + 128], ident)
                        last.then_inc(s_nt, 1)
                    if v % 2 and c:
                        router_logits(v, c - 1)
                if v % 2:
                    router_logits(v, C - 1)

            def norm_ready(v):
                pe.wait_ge(s_ntA, 4 * v + 4)
                pe.wait_ge(s_ntV, 4 * v + 4)

            def project_features(n, blocks):
                w = w_tile(n)
                pe.wait_ge(*((s_half, 16) if n == 0 else (s_ld[n % 4], tile_ready(n))))
                for fb in range(blocks):
                    if n == 0 and fb == 2:
                        pe.wait_ge(s_ld[0], tile_ready(0))
                    b = group_start()
                    for k in range(KD):
                        last = nc.tensor.matmul(b[:, :], w[:, k, 128 * fb:128 * fb + 128], hnT[:, k, :],
                                                start=(k == 0), stop=(k == KD - 1))
                    last.then_inc(s_pj, 1)

            def project_rows(n, c0, width, per_group):
                w = w_tile(n)
                pe.wait_ge(s_ld[n % 4], tile_ready(n))
                for c in range(C):
                    if c % per_group == 0:
                        b = group_start()
                    at = (c % per_group) * width
                    for k in range(KD):
                        last = nc.tensor.matmul(b[:, at:at + width], hnT[:, k, 128 * c:128 * c + 128],
                                                w[:, k, c0:c0 + width], start=(k == 0), stop=(k == KD - 1))
                    if c % per_group == per_group - 1:
                        last.then_inc(s_pj, 1)

            def scores(f, u):
                g = H * f + u
                kv = u // 4 if f == SWA else u
                for i in range(4):
                    b = 4 * g + i
                    if b >= 3:
                        pe.wait_ge(s_msk, b - 2)
                    k0, n = 128 * FIRST_KEY[f][i], LEN[f][i]
                    nc.tensor.matmul(bank[b % 3][:, 0:n], Q[:, u, 128 * i:128 * i + 128],
                                     K[:, kv, k0:k0 + n], start=True, stop=True).then_inc(s_qk, 1)

            def transposes(f, u):
                g = H * f + u
                pe.wait_ge(s_nrm, 4 * g + 4)
                for j in range(4):
                    if g:
                        pe.wait_ge((s_teA, s_teV)[j % 2], 2 * g - 1 + j // 2)
                    for a, i in enumerate(q_chunks(f, j)):
                        at = p_col(f, i) + 128 * (j - FIRST_KEY[f][i])
                        last = nc.tensor.transpose(bank[pt_bank[j]][:, 128 * a:128 * a + 128],
                                                   P[:, u % 2, at:at + 128], ident)
                    last.then_inc(s_tr, 1)

            def pair_outputs(f, u):
                g = H * f + u
                if g == 0:
                    pe.wait_ge(s_zfv, 1)
                else:
                    pe.wait_ge(s_oev, g // 2)
                for j in range(4):
                    pe.wait_ge((s_teA, s_teV)[j % 2], 2 * (g + 1) + j // 2 + 1)
                    n = 128 * len(q_chunks(f, j))
                    for a in range(2):
                        vc = 64 * (u // 4) if f == SWA else 64 * (u + a)
                        last = nc.tensor.matmul(bank[5][64 * a:64 * a + 64, 128 * j:128 * j + n],
                                                V[:, j, vc:vc + 64], PTs[a][:, pt_col(f, j):pt_col(f, j) + n],
                                                start=(j == 0), stop=(j == 3), skip_group_check=True)
                last.then_inc(s_pv, 1)

            def first_scores(f, groups, aug):
                pe.wait_ge(s_pjA, groups)
                pe.wait_ge(s_pjV, groups)
                pe.wait_ge(s_aug, aug)
                scores(f, 0)
                scores(f, 1)

            def attention(f, groups):
                pe.wait_ge(s_pjA, groups)
                pe.wait_ge(s_pjV, groups)
                for u in range(0, H, 2):
                    for a in range(2):
                        transposes(f, u + a)
                        if u + 2 < H:
                            scores(f, u + 2 + a)
                    pair_outputs(f, u)

            def mixer_out(lay, n0):
                pe.wait_ge(s_oev, 8 * (lay + 1))
                for half in range(2):
                    n = n0 + half
                    pe.wait_ge(s_ld[n % 4], tile_ready(n))
                    for c in range(C):
                        g = 8 * lay + 4 * half + c
                        if g >= 2:
                            pe.wait_ge(s_oga, g - 1)
                        for k in range(KD):
                            last = nc.tensor.matmul(bank[g % 2][:, :], oT[:, k, 128 * c:128 * c + 128],
                                                    w_tile(n)[:, k, :], start=(k == 0), stop=(k == KD - 1))
                        last.then_inc(s_og, 1)

            def routing(lay):
                pe.wait_ge(s_oh, lay + 1)
                for c in range(C):
                    for cc in range(c):
                        nc.tensor.matmul(bank[7][:, 32 * c:32 * c + 32], ones, ohs[:, cc, :],
                                         start=(cc == 0), stop=False)
                    nc.tensor.matmul(bank[7][:, 32 * c:32 * c + 32], tri, ohs[:, c, :], start=(c == 0), stop=True)
                for c in range(C):
                    last = nc.tensor.matmul(bank[7][:, 128:160], ones, ohs[:, c, :], start=(c == 0), stop=(c == C - 1))
                last.then_inc(s_rank, 1)
                for n in range(2 * C):
                    if n % C == 0:
                        pe.wait_ge(s_facts, 3 * lay + 2 + n // C)
                    last = nc.tensor.matmul(bank[6][:, 0:128], rank_hot[:, n, :],
                                            facts[:, n, :, :].rearrange("p q e -> p (q e)"),
                                            start=(n == 0), stop=(n == 2 * C - 1))
                last.then_inc(s_slots, 1)

            def transpose_rows(e2, src):
                for k in range(4):
                    last = nc.tensor.transpose(bank[e2][:, 128 * k:128 * k + 128],
                                               src.rearrange("p (x k) -> p k x", k=4)[:, k, :], ident)
                return last

            def gate_up(e2, w):
                for half in range(2):
                    for k in range(4):
                        xt = XT[e2][:, 128 * k + 64 * half:128 * k + 64 * half + 64]
                        at = 1024 * half + 256 * k
                        first, end = half + k == 0, half + k == 4
                        nc.tensor.matmul(bank[2 + e2][0:64, 0:256], xt, w[:, at:at + 256], start=first, stop=end)
                        last = nc.tensor.matmul(bank[2 + e2][64:128, 0:256], xt, w[:, 2048 + at:2304 + at],
                                                start=first, stop=end)
                return last

            def hidden_transposes(e2):
                for c in range(2):
                    last = nc.tensor.transpose(bank[4][:, 128 * c:128 * c + 128],
                                               hid[e2].rearrange("p (x c) -> p c x", c=2)[:, c, :], ident)
                return last

            def down(e2, d):
                for c in range(2):
                    nc.tensor.matmul(bank[5 + e2][0:64, :], hT[e2][:, 64 * c:64 * c + 64],
                                     d[:, 1024 * c:1024 * c + 512], start=(c == 0), stop=(c == 1))
                    last = nc.tensor.matmul(bank[5 + e2][64:128, :], hT[e2][:, 64 * c:64 * c + 64],
                                            d[:, 1024 * c + 512:1024 * c + 1024], start=(c == 0), stop=(c == 1))
                return last

            def experts(lay):
                base = NE * lay
                pe.wait_ge(s_g[0], 16 * (8 * lay + 1))
                transpose_rows(0, Xg[0]).then_inc(s_xt, 1)

                def step(e, s, gate_up_w, down_w, landed, more, wait_out=True):
                    e2 = s % 2
                    pe.wait_ge(*landed)
                    pe.wait_ge(s_xte, e + (base + 1))
                    gate_up(e2, gate_up_w).then_inc(s_gu, 1)
                    if more:
                        s1 = (s + 1) % 4
                        turn = e * 4 + (16 * 8 * lay + 16 - 4 * s + (16 if s == 3 else 0))
                        pe.wait_ge(s_g[s1], turn)
                        transpose_rows(1 - e2, Xg[s1]).then_inc(s_xt, 1)
                    pe.wait_ge(s_hid, e + (base + 1))
                    hidden_transposes(e2).then_inc(s_ht, 1)
                    pe.wait_ge(s_hte, e + (base + 1))
                    if wait_out:
                        pe.wait_ge(s_ye, e + (base - 1))
                    down(e2, down_w).then_inc(s_y, 1)

                def numbered(e):
                    if e in BESIDE:
                        i = e % 2
                        slot_ = WB[i], DB[i], (s_lb[i], 48 * (2 * lay + BESIDE.index(e) // 2 + 1))
                    else:
                        n = expert_tile(lay, e)
                        slot_ = W[n % 4], D[n % 4], (s_ld[n % 4], tile_ready(n))
                    step(e, e % 4, *slot_, e + 1 < NE, base + e >= 2)

                for e in range(LOOP0):
                    numbered(e)
                with pe.Fori(LOOP0, NE - 4, 4) as e:
                    for s in range(4):
                        landed = s_ld[s], e * 12 + (tile_ready(expert_tile(lay, LOOP0 + s)) - 12 * LOOP0)
                        step(e + s, s, W[s], D[s], landed, True)
                for e in range(NE - 4, NE):
                    numbered(e)

            def further_tiles(lay):
                o_ = ov[lay]
                pe.wait_ge(s_ncell, lay + 1)
                n_over = pe.value_load(ncells[0:1, 0:1], min_val=0, max_val=MAXOV)
                with pe.If(n_over > 0):
                    with pe.Fori(0, n_over) as o:
                        pe.wait_ge(o_["gathered"], o * 16 + 16)
                        transpose_rows(0, Xg[0]).then_inc(o_["xt"], 1)
                        pe.wait_ge(o_["loaded"], o * 48 + 48)
                        pe.wait_ge(o_["xte"], o + 1)
                        gate_up(0, W[0]).then_inc(o_["gu"], 1)
                        pe.wait_ge(o_["hid"], o + 1)
                        hidden_transposes(0).then_inc(o_["ht"], 1)
                        pe.wait_ge(o_["hte"], o + 1)
                        down(0, D[0]).then_inc(o_["y"], 1)

            norm_transposes(0)
            norm_ready(0)
            project_features(0, 4)
            pe.wait_ge(s_small, 16)
            for k in range(KD):
                last = nc.tensor.matmul(bank[5][0:8, :], zf_w[:, k, :], hnT[:, k, :], start=(k == 0), stop=(k == KD - 1))
            last.then_inc(s_zf, 1)
            project_features(1, 4)
            first_scores(DIL, 8, 32)
            project_rows(2, 0, 512, 1)
            attention(DIL, 12)
            for n in range(3, 5):
                project_features(n, 4)
            first_scores(FOX, 20, 80)
            project_rows(5, 0, 512, 1)
            attention(FOX, 24)
            mixer_out(0, 6)
            norm_transposes(1)
            routing(0)
            experts(0)
            further_tiles(0)

            norm_transposes(2)
            norm_ready(2)
            project_features(T_ODD, 4)
            project_features(T_ODD + 1, 1)
            first_scores(SWA, 29, 112)
            project_rows(T_ODD + 1, 128, 128, 4)
            attention(SWA, 30)
            project_rows(T_ODD + 2, 0, 512, 1)
            project_rows(T_ODD + 3, 0, 160, 2)
            for c in range(C):
                pe.wait_ge(s_lrow, c + 1)
                if c:
                    pe.wait_ge(s_ltA, c)
                    pe.wait_ge(s_ltV, c)
                for k in range(4):
                    last = nc.tensor.transpose(bank[3][:, 128 * k:128 * k + 128], cq_row[:, c, 128 * k:128 * k + 128], ident)
                last.then_inc(s_lt, 1)
                nc.tensor.transpose(bank[4][:, 0:128], cq_row[:, c, 512:640], ident)
                nc.tensor.transpose(bank[4][:, 128:256], kpe_pad[:, c, :], ident).then_inc(s_lt, 1)
            pe.wait_ge(s_ltA, C)
            pe.wait_ge(s_ltV, C)
            pe.wait_ge(s_perm, 2)
            uq = W[(T_ODD + 4) % 4][:, 0:3072].rearrange("p (k h n) -> p k h n", k=3, h=H)
            for hh in range(H):
                b = group_start()
                for k in range(3):
                    last = nc.tensor.matmul(b[:, :], uq[:, k, hh, :], hnT[:, k, :], start=(k == 0), stop=(k == 2))
                last.then_inc(s_pj, 1)
            t = T_ODD + 5
            pe.wait_ge(s_ld[t % 4], tile_ready(t))
            ukv = W[t % 4][:, 0:2048].rearrange("p (k h n) -> p k h n", k=2, h=H)
            for pair in range(4):
                b = group_start()
                for k in range(2):
                    for a in range(2):
                        last = nc.tensor.matmul(b[64 * a:64 * a + 64, :], ukv[:, k, 2 * pair + a, 0:64],
                                                hnT[:, 3 + k, :], start=(k == 0), stop=(k == 1))
                last.then_inc(s_pj, 1)
            first_scores(MLA, 48, 112)
            for c in range(C):
                b = group_start()
                for k in range(2):
                    last = nc.tensor.matmul(b[:, :].rearrange("p (h n) -> p h n", h=H),
                                            hnT[:, 3 + k, 128 * c:128 * c + 128], ukv[:, k, :, 64:128],
                                            start=(k == 0), stop=(k == 1))
                last.then_inc(s_pj, 1)
            attention(MLA, 52)
            mixer_out(1, T_ODD + 6)
            norm_transposes(3)
            routing(1)
            experts(1)
            further_tiles(1)

        @block.scalar
        def _(act):
            order = [0]
            group = [0]

            def then(ins):
                order[0] += 1
                ins.then_inc(s_av, 1)
                act.wait_ge(s_av, order[0])

            def chunk_ready(v, c):
                if v == 0:
                    return s_x[c], 16
                if v % 2:
                    return s_oga, 8 * (v // 2) + 5 + c
                return s_yadd, 4 * (v // 2 - 1) + 1 + c

            def norm(v):
                if v % 2 == 0:
                    nc.scalar.activation(warm[:, v // 2:v // 2 + 1], eps[0:1, 0:1], ACT.Sqrt)
                for c in range(C):
                    n = 4 * v + c + 1
                    act.wait_ge(*chunk_ready(v, c))
                    nc.scalar.activation(junk, h[:, c, :], ACT.Square, accum_out=ssq[:, c:c + 1]).then_inc(s_sq, 1)
                    act.wait_ge(s_sq, n)
                    nc.scalar.activation(rstd[:, c:c + 1], ssq[:, c:c + 1], ACT.Sqrt, scale=1.0 / DM, bias=eps[:, 0:1])\
                      .then_inc(s_sqrt, 1)

            def norm_out(v):
                for c in range(C):
                    act.wait_ge(s_nt, 8 * v + 2 * c + 1)
                    nc.scalar.activation(hnT[:, 0:4, 128 * c:128 * c + 128],
                                         bank[3][:, :].rearrange("p (k t) -> p k t", k=4), ACT.Copy).then_inc(s_ntA, 1)

            def next_group():
                g = group[0]
                act.wait_ge(s_pj, g + 1)
                group[0] += 1
                return bank[6 + g % 2]

            def features_out(dst, scale, heads):
                for hh in range(0, heads, 2):
                    b = next_group()
                    nc.scalar.activation(dst[0:64, hh, :], b[0:64, :], ACT.Copy, scale=scale).then_inc(s_pjA, 1)

            def rows_out():
                for c in range(C):
                    b = next_group()
                    nc.scalar.activation(V[0:64, c, :], b[0:64, :], ACT.Copy).then_inc(s_pjA, 1)

            def exps(f, u):
                for i in range(4):
                    b = 4 * (H * f + u) + i
                    act.wait_ge(s_msk, b + 1)
                    if f == SWA:
                        nc.scalar.activation(esink[:, b % 8:b % 8 + 1], sinks[:, u:u + 1], ACT.Exp,
                                             bias=nm[:, b % 8:b % 8 + 1])
                    blk = P[:, u % 2, p_col(f, i):p_col(f, i) + LEN[f][i]]
                    nc.scalar.activation(blk, blk, ACT.Exp, bias=nm[:, b % 8:b % 8 + 1], scale=-1.0,
                                         accum_out=den[:, b % 8:b % 8 + 1]).then_inc(s_exp, 1)

            def probs_out(f, u):
                g = H * f + u
                for j in (0, 2):
                    act.wait_ge(s_tr, 4 * g + j + 1)
                    if g >= 2:
                        act.wait_ge(s_pv, g // 2)
                    n = 128 * len(q_chunks(f, j))
                    nc.scalar.activation(PTs[u % 2][:, pt_col(f, j):pt_col(f, j) + n], bank[pt_bank[j]][:, 0:n],
                                         ACT.Copy).then_inc(s_teA, 1)

            def pair_out(f, u):
                act.wait_ge(s_pv, (H * f + u) // 2 + 1)
                chunk = u // 2 + (4 if f in (DIL, SWA) else 0)
                nc.scalar.activation(oT[:, chunk, :], bank[5][:, :], ACT.Copy).then_inc(s_oev, 1)

            def first_exps(f):
                exps(f, 0)
                exps(f, 1)

            def attention(f):
                for u in range(H):
                    probs_out(f, u)
                    if u + 2 < H:
                        exps(f, u + 2)
                    if u % 2:
                        pair_out(f, u - 1)

            def routing(lay):
                act.wait_ge(s_rsub, 2 * lay + 1)
                nc.scalar.activation(gexp, gexp, ACT.Exp).then_inc(s_rexp, 1)
                act.wait_ge(s_rsub, 2 * lay + 2)
                nc.scalar.activation(ed, ed, ACT.Exp).then_inc(s_rexp, 1)

            def silu(e2, done):
                nc.scalar.activation(sil[e2][64:128, :], bank[2 + e2][0:64, 0:256], ACT.Silu).then_inc(done, 1)

            def hidden_out(e2, done):
                nc.scalar.activation(hT[e2].rearrange("p (c t) -> p c t", c=2),
                                     bank[4][:, 0:256].rearrange("p (c t) -> p c t", c=2)[:, :, 64:128],
                                     ACT.Copy).then_inc(done, 1)

            def experts(lay):
                base = NE * lay
                with act.Fori(0, NE, 2) as e:
                    for e2 in range(2):
                        act.wait_ge(s_gu, e + (base + e2 + 1))
                        silu(e2, s_sil)
                        act.wait_ge(s_ht, e + (base + e2 + 1))
                        hidden_out(e2, s_hte)

            def further_tiles(lay):
                o_ = ov[lay]
                act.wait_ge(s_ncell, lay + 1)
                n_over = act.value_load(ncells[0:1, 0:1], min_val=0, max_val=MAXOV)
                with act.If(n_over > 0):
                    with act.Fori(0, n_over) as o:
                        act.wait_ge(o_["gu"], o + 1)
                        silu(0, o_["sil"])
                        act.wait_ge(o_["ht"], o + 1)
                        hidden_out(0, o_["hte"])

            act.wait_ge(s_const, 16)
            norm(0)
            norm_out(0)
            features_out(Q, -0.125, H)
            act.wait_ge(s_zfv, 2)
            then(nc.scalar.activation(zf[2], zf[1], ACT.Exp))
            nc.scalar.activation(zf[1], zf[2], ACT.Ln, bias=1.0).then_inc(s_zfa, 1)
            features_out(K, 1.0, H)
            first_exps(DIL)
            rows_out()
            attention(DIL)
            features_out(Q, -0.125, H)
            features_out(K, 1.0, H)
            first_exps(FOX)
            rows_out()
            attention(FOX)
            norm(1)
            norm_out(1)
            routing(0)
            experts(0)
            further_tiles(0)
            norm(2)
            norm_out(2)
            features_out(Q, -0.125, H)
            features_out(K, 1.0, 2)
            first_exps(SWA)
            b = next_group()
            nc.scalar.activation(V[0:64, :, 0:128], b[0:64, :].rearrange("p (c n) -> p c n", c=C), ACT.Copy)\
              .then_inc(s_pjA, 1)
            attention(SWA)
            for c in range(C):
                b = next_group()
                nc.scalar.activation(cq_row[0:64, c, 0:512], b[0:64, :], ACT.Copy).then_inc(s_pjA, 1)
            for c in (0, 2):
                b = next_group()
                nc.scalar.activation(cq_row[0:64, c:c + 2, 512:672],
                                     b[0:64, 0:320].rearrange("p (c n) -> p c n", c=2), ACT.Copy).then_inc(s_pjA, 1)
            act.wait_ge(s_pjA, 36)
            act.wait_ge(s_pjV, 36)
            for c in range(C):
                nc.scalar.activation(junk[:, 0:QR], cq_row[:, c, 0:QR], ACT.Square, accum_out=ssq[:, c:c + 1])\
                  .then_inc(s_lsq, 1)
                nc.scalar.activation(junk[:, 512:512 + KVR], cq_row[:, c, QR:QR + KVR], ACT.Square,
                                     accum_out=ssq[:, 4 + c:5 + c]).then_inc(s_lsq, 1)
                act.wait_ge(s_lsq, 2 * c + 2)
            act.wait_ge(s_lms, 1)
            nc.scalar.activation(rstd[:, :], ssq[:, :], ACT.Sqrt).then_inc(s_lrt, 1)
            for c in range(C):
                act.wait_ge(s_lt, 2 * c + 1)
                nc.scalar.activation(hnT[:, 0:4, 128 * c:128 * c + 128],
                                     bank[3][:, :].rearrange("p (k t) -> p k t", k=4), ACT.Copy).then_inc(s_ltA, 1)
            for hh in range(H):
                b = next_group()
                nc.scalar.activation(Q[0:64, hh, :], b[0:64, :], ACT.Copy, scale=-((NOPE + ROPE) ** -0.5))\
                  .then_inc(s_pjA, 1)
            features_out(K, 1.0, H)
            first_exps(MLA)
            rows_out()
            attention(MLA)
            norm(3)
            norm_out(3)
            routing(1)
            experts(1)
            further_tiles(1)
            norm(4)

        @block.vector
        def _(dve):
            order = [0]
            group = [0]

            def then(ins):
                order[0] += 1
                ins.then_inc(s_dv, 1)
                dve.wait_ge(s_dv, order[0])

            def norm_chunk(v, c):
                dve.wait_ge(s_sqrt, 4 * v + c + 1)
                then(nc.vector.reciprocal(rstd[:, c:c + 1], rstd[:, c:c + 1]))
                if c == 0:
                    dve.wait_ge(s_gain, 16 * (v + 1))
                nc.vector.scalar_tensor_tensor(hn_row[:, c, :], h[:, c, :], rstd[:, c:c + 1], gain,
                                               ALU.mult, ALU.mult).then_inc(s_hn, 1)

            def norm_outs(v):
                for c in range(C):
                    norm_out(v, c)

            def norm_out(v, c):
                dve.wait_ge(s_nt, 8 * v + 2 * c + 2)
                nc.vector.tensor_copy(hnT[:, 4:8, 128 * c:128 * c + 128],
                                      bank[4][:, :].rearrange("p (k t) -> p k t", k=4)).then_inc(s_ntV, 1)

            def next_group():
                g = group[0]
                dve.wait_ge(s_pj, g + 1)
                group[0] += 1
                return bank[6 + g % 2]

            def features_out(dst, scale, heads):
                for hh in range(1, heads, 2):
                    b = next_group()
                    nc.vector.tensor_scalar(dst[0:64, hh, :], b[64:128, :], scale, None, ALU.mult).then_inc(s_pjV, 1)

            def rows_out():
                for c in range(C):
                    b = next_group()
                    nc.vector.tensor_copy(V[64:128, c, :], b[64:128, :]).then_inc(s_pjV, 1)

            def masks(f, u):
                g = H * f + u
                if g >= 2:
                    dve.wait_ge(s_tr, 4 * (g - 1))
                at, width = MASK[f]
                for i in range(4):
                    b, n = 4 * g + i, LEN[f][i]
                    dve.wait_ge(s_qk, b + 1)
                    start = sinks[:, H + u:H + u + 1] if f == SWA else 3e38
                    nc.vector.tensor_tensor_reduce(
                        out=P[:, u % 2, p_col(f, i):p_col(f, i) + n], in0=bank[b % 3][:, 0:n],
                        in1=cst[:, at + width - n:at + width], scale=1.0, scalar=start,
                        op0=ALU.add, op1=ALU.min, accum_out=nm[:, b % 8:b % 8 + 1]).then_inc(s_msk, 1)

            def normalise(f, u):
                for i in range(4):
                    b = 4 * (H * f + u) + i
                    d = den[:, b % 8:b % 8 + 1]
                    dve.wait_ge(s_exp, b + 1)
                    if f == SWA:
                        then(nc.vector.tensor_tensor(d, d, esink[:, b % 8:b % 8 + 1], ALU.add))
                    ins = nc.vector.reciprocal(rden[:, b % 8:b % 8 + 1], d)
                then(ins)
                for i in range(4):
                    b = 4 * (H * f + u) + i
                    blk = P[:, u % 2, p_col(f, i):p_col(f, i) + LEN[f][i]]
                    nc.vector.tensor_scalar(blk, blk, rden[:, b % 8:b % 8 + 1], None, ALU.mult).then_inc(s_nrm, 1)

            def probs_out(f, u):
                g = H * f + u
                for j in (1, 3):
                    dve.wait_ge(s_tr, 4 * g + j + 1)
                    if g >= 2:
                        dve.wait_ge(s_pv, g // 2)
                    n = 128 * len(q_chunks(f, j))
                    nc.vector.tensor_copy(PTs[u % 2][:, pt_col(f, j):pt_col(f, j) + n],
                                          bank[pt_bank[j]][:, 0:n]).then_inc(s_teV, 1)

            def first_probs(f):
                masks(f, 0)
                masks(f, 1)
                normalise(f, 0)
                normalise(f, 1)

            def attention(f):
                for u in range(0, H, 2):
                    for a in range(2):
                        probs_out(f, u + a)
                        if u + 2 < H:
                            masks(f, u + 2 + a)
                    if u + 2 < H:
                        normalise(f, u + 2)
                        normalise(f, u + 3)

            def mixer_add(lay):
                for half in range(2):
                    for c in range(C):
                        g = 8 * lay + 4 * half + c
                        dve.wait_ge(s_og, g + 1)
                        part = h[:, c, 512 * half:512 * half + 512]
                        nc.vector.tensor_tensor(part, bank[g % 2][:, :], part, ALU.add).then_inc(s_oga, 1)
                        if half:
                            norm_chunk(2 * lay + 1, c)
                norm_outs(2 * lay + 1)

            def first_at(value, best, score, at_best, onehot):
                n = value.shape[2]
                bb = best.unsqueeze(2).to_broadcast([128, C, n])
                io = iota[:, 0:n].unsqueeze(1).to_broadcast([128, C, n])
                then(nc.vector.tensor_tensor(score, value, bb, ALU.is_ge))
                then(nc.vector.scalar_tensor_tensor(score, score, -64.0, io, ALU.mult, ALU.add))
                then(nc.vector.tensor_reduce(at_best, score, X, ALU.min))
                then(nc.vector.tensor_tensor(onehot, score, at_best.unsqueeze(2).to_broadcast([128, C, n]),
                                             ALU.is_equal))

            def routing(lay):
                nc.vector.tensor_copy(tri_ones, cst[:, C_TRI:C_ONE + 128])
                dve.wait_ge(s_lg, C * (lay + 1))
                then(nc.vector.tensor_tensor(lg, bank[6][:, 0:144].rearrange("p (c n) -> p c n", c=C),
                                             rbias.unsqueeze(1).to_broadcast([128, C, 36]), ALU.add))
                glog = lg[:, :, 0:4]
                then(nc.vector.tensor_reduce(gmax, glog, X, ALU.max))
                nc.vector.tensor_tensor(gexp, glog, gmax.unsqueeze(2).to_broadcast([128, C, 4]), ALU.subtract)\
                  .then_inc(s_rsub, 1)
                first_at(glog, gmax, gpick, gmin, goh)
                then(nc.vector.tensor_scalar(gpen, goh, BIG, -BIG, ALU.mult, ALU.add))
                e4 = em[0].rearrange("p c (g e) -> p c g e", g=4)
                then(nc.vector.tensor_tensor(e4, lg[:, :, 4:36].rearrange("p c (g e) -> p c g e", g=4),
                                             goh.unsqueeze(3).to_broadcast([128, C, 4, 8]), ALU.mult))
                then(nc.vector.tensor_tensor(e4, e4, gpen.unsqueeze(3).to_broadcast([128, C, 4, 8]), ALU.add))
                then(nc.vector.tensor_reduce(emax[0], em[0], X, ALU.max))
                first_at(em[0], emax[0], pick[0], emin[0], oh[0])
                then(nc.vector.scalar_tensor_tensor(em[1], oh[0], -3 * BIG, em[0], ALU.mult, ALU.add))
                then(nc.vector.tensor_reduce(emax[1], em[1], X, ALU.max))
                first_at(em[1], emax[1], pick[1], emin[1], oh[1])
                nc.vector.tensor_tensor(ed, emax[1], emax[0], ALU.subtract).then_inc(s_rsub, 1)
                nc.vector.tensor_tensor(ohs, oh[0], oh[1], ALU.add).then_inc(s_oh, 1)
                dve.wait_ge(s_rexp, 2 * lay + 2)
                then(nc.vector.tensor_reduce(gsum, gexp, X, ALU.add))
                nc.vector.tensor_scalar(esum, ed, 1.0, None, ALU.add)
                then(nc.vector.reciprocal(gw, gsum))
                then(nc.vector.reciprocal(einv, esum))
                then(nc.vector.tensor_tensor(wgt[:, 0, :], einv, gw, ALU.mult))
                then(nc.vector.tensor_tensor(wgt[:, 1, :], wgt[:, 0, :], ed, ALU.mult))
                for k in range(2):
                    part = facts[:, C * k:C * k + C]
                    for q in range(2):
                        ids = cst[:, C_TOK + 8 * q + C * k:C_TOK + 8 * q + C * k + C]
                        nc.vector.tensor_tensor(part[:, :, q, :], oh[k], ids.unsqueeze(2).to_broadcast([128, C, NE]),
                                                ALU.mult)
                    ins = nc.vector.tensor_tensor(part[:, :, 2, :], oh[k],
                                                  wgt[:, k, :].unsqueeze(2).to_broadcast([128, C, NE]), ALU.mult)
                ins.then_inc(s_facts, 1)
                dve.wait_ge(s_rank, lay + 1)
                rank = bank[7][:, 0:128].rearrange("p (c n) -> p c n", c=C)
                for k in range(2):
                    ins = nc.vector.tensor_tensor(pick[k], rank, oh[k], ALU.mult)
                then(ins)
                for k in range(2):
                    ins = nc.vector.tensor_reduce(rpos[k], pick[k], X, ALU.add)
                then(ins)
                for k in range(2):
                    nc.vector.tensor_tensor(rank_hot[:, C * k:C * k + C, :],
                                                  cst[:, C_RANK:C_RANK + 128].unsqueeze(1).to_broadcast([128, C, 128]),
                                                  rpos[k].unsqueeze(2).to_broadcast([128, C, 128]), ALU.is_equal)\
                      .then_inc(s_facts, 1)
                recv = rec.rearrange("p (n w) -> p n w", w=4)
                ids = cst[:, C_TOK:C_TOK + 16].rearrange("p (w n) -> p n w", w=2)
                nc.vector.tensor_copy(recv[:, :, 0:2], ids)
                nc.vector.tensor_copy(recv.bitcast(f32)[:, :, 2:4],
                                      wgt.rearrange("p k c -> p (k c)").unsqueeze(2).to_broadcast([128, 8, 2]))
                for k in range(2):
                    ins = nc.vector.scalar_tensor_tensor(rslot[k], rpos[k], float(NE), emin[k], ALU.mult, ALU.add)
                then(ins)
                for k in range(2):
                    nc.vector.tensor_scalar(slot[:, 4 * k:4 * k + 4], rslot[k], 64.0, None, ALU.add)
                dve.wait_ge(s_slots, lay + 1)
                found = bank[6][:, 0:128].rearrange("p (q e) -> p q e", q=4)
                then(nc.vector.tensor_scalar(pad, found[:, 3, :], -float(OOB), cst[:, C_OOB:C_OOB + 1],
                                             ALU.mult, ALU.add))
                nc.vector.tensor_tensor(gidx, found[:, 0, :], pad, ALU.add)
                nc.vector.tensor_tensor(sidx, found[:, 1, :], pad, ALU.add)
                nc.vector.tensor_copy(wtab, found[:, 2, :]).then_inc(s_idx, 1)
                cnt = bank[7][0:1, 128:160]
                big = [ovbig[i].rearrange("p (a b) -> p a b", b=NE) for i in range(2)]
                b7 = ovbig[0][:, 0:224].rearrange("p (e t) -> p e t", t=7)
                then(nc.vector.tensor_copy(ends, cnt))
                then(nc.vector.tensor_tensor(b7, ends.unsqueeze(2).to_broadcast([1, NE, 7]),
                                             cst[0:1, C_THR:C_THR + 7].unsqueeze(1).to_broadcast([1, NE, 7]), ALU.is_gt))
                then(nc.vector.tensor_reduce(extra, b7, X, ALU.add))
                then(nc.vector.memset(ovbig[1][:, 0:NE], 0.0))
                then(nc.vector.tensor_tensor_scan(ends, extra, ovbig[1][:, 0:NE], 0.0, ALU.add, ALU.add))
                then(nc.vector.tensor_tensor(big[0], ends.unsqueeze(1).to_broadcast([1, MAXOV, NE]),
                                             cst[0:1, C_IOTA:C_IOTA + MAXOV].unsqueeze(2).to_broadcast([1, MAXOV, NE]),
                                             ALU.is_le))
                then(nc.vector.tensor_tensor(big[1], big[0], extra.unsqueeze(1).to_broadcast([1, MAXOV, NE]), ALU.mult))
                then(nc.vector.tensor_reduce(oe, big[0], X, ALU.add))
                then(nc.vector.tensor_reduce(ostart, big[1], X, ALU.add))
                then(nc.vector.tensor_tensor(ostart, cst[0:1, C_IOTA + 1:C_IOTA + 1 + MAXOV], ostart, ALU.subtract))
                nc.vector.tensor_copy(ncells[:, 0:1], ends[:, NE - 1:NE])
                nc.vector.tensor_copy(ncells[:, 1:1 + MAXOV], oe)
                nc.vector.tensor_copy(ncells[:, 1 + MAXOV:1 + 2 * MAXOV], ostart).then_inc(s_ncell, 1)

            def indices(gather_idx, scatter_idx, records, done):
                half = cst[:, C_OOB:C_OOB + 1]
                nc.vector.tensor_scalar(gather_idx, records[:, :, 0], half, -float(OOB), ALU.add, ALU.add)
                nc.vector.tensor_scalar(scatter_idx, records[:, :, 1], half, -float(OOB), ALU.add, ALU.add)\
                  .then_inc(done, 1)

            def hidden(e2, weight, done):
                nc.vector.scalar_tensor_tensor(hid[e2][64:128, :], bank[2 + e2][64:128, 0:256], weight,
                                               sil[e2][64:128, :], ALU.mult, ALU.mult).then_inc(done, 1)

            def experts(lay):
                base = NE * lay
                dve.wait_ge(s_xt, base + 1)
                nc.vector.tensor_copy(XT[0], bank[0][:, :]).then_inc(s_xte, 1)

                def step(e, e2, wcol, more, scattered):
                    dve.wait_ge(s_sil, e + (base + 1))
                    hidden(e2, wtab[64:128, wcol], s_hid)
                    if more:
                        dve.wait_ge(s_xt, e + (base + 2))
                        nc.vector.tensor_copy(XT[1 - e2], bank[1 - e2][:, :]).then_inc(s_xte, 1)
                    dve.wait_ge(s_y, e + (base + 1))
                    if scattered is not None:
                        dve.wait_ge(s_sc[e2], scattered)
                    nc.vector.tensor_copy(Y[e2], bank[5 + e2][:, :]).then_inc(s_ye, 1)

                for e in range(2):
                    step(e, e, slice(e, e + 1), True, 8 * base if base else None)
                with dve.Fori(2, NE - 3, 2) as e:
                    for e2 in range(2):
                        step(e + e2, e2, bass.ds(dve.snap(e + e2), 1), True, e * 8 + 8 * base)
                for e2 in range(2):
                    e = NE - 2 + e2
                    step(e, e2, slice(e, e + 1), e2 == 0, 8 * (base + NE - 2))

            def further_tiles(lay):
                o_ = ov[lay]
                n_over = dve.value_load(ncells[0:1, 0:1], min_val=0, max_val=MAXOV)
                with dve.If(n_over > 0):
                    dve.wait_ge(s_sc[0], 256 * (lay + 1))
                    with dve.Fori(0, n_over) as o:
                        dve.wait_ge(o_["records"], o * 32 + 32)
                        indices(oidx[:, 0:1], oidx[:, 1:2], orec.unsqueeze(1), o_["indices"])
                        dve.wait_ge(o_["xt"], o + 1)
                        nc.vector.tensor_copy(XT[0], bank[0][:, :]).then_inc(o_["xte"], 1)
                        dve.wait_ge(o_["sil"], o + 1)
                        hidden(0, orec.bitcast(f32)[64:128, 2:3], o_["hid"])
                        dve.wait_ge(o_["y"], o + 1)
                        nc.vector.tensor_copy(Y[0], bank[5][:, :]).then_inc(o_["ye"], 1)

            def add_expert_rows(lay):
                for c in range(C):
                    dve.wait_ge(s_yld[c], 16 * (lay + 1))
                    then(nc.vector.tensor_tensor(h[:, c, :], h[:, c, :], y_in[c][:, 0:DM], ALU.add))
                    nc.vector.tensor_tensor(h[:, c, :], h[:, c, :], y_in[c][:, DM:2 * DM], ALU.add).then_inc(s_yadd, 1)
                    if c:
                        norm_chunk(2 * lay + 2, c - 1)
                norm_chunk(2 * lay + 2, C - 1)

            dve.wait_ge(s_const, 16)
            for c in range(C):
                norm_chunk(0, c)
                norm_out(0, c)
            features_out(Q, -0.125, H)
            dve.wait_ge(s_heads, 32)
            nc.vector.tensor_scalar(sinks[:, H:2 * H], sinks[:, 0:H], -1.0, None, ALU.mult)
            dve.wait_ge(s_zf, 1)
            nc.vector.tensor_scalar(zf[0], bank[5][0:8, :], bf_sb[:, 0:1], None, ALU.add).then_inc(s_zfv, 1)
            dve.wait_ge(s_zfv, 1)
            nc.vector.scalar_tensor_tensor(zf[1], zf[0], -1.0, zf[0], ALU.mult, ALU.min).then_inc(s_zfv, 1)
            dve.wait_ge(s_zfa, 1)
            nc.vector.scalar_tensor_tensor(zf[0], zf[0], 0.0, zf[1], ALU.min, ALU.subtract).then_inc(s_zfv, 1)
            dve.wait_ge(s_zfv, 3)
            then(nc.vector.memset(zf[1], 0.0))
            nc.vector.tensor_tensor_scan(zf[2], zf[0], zf[1], 0.0, ALU.add, ALU.add).then_inc(s_zfv, 1)
            dve.wait_ge(s_zfv, 4)
            nc.vector.tensor_scalar(zf[3], zf[2], -1.0, None, ALU.mult).then_inc(s_zfv, 1)
            features_out(K, 1.0, H)
            first_probs(DIL)
            rows_out()
            attention(DIL)
            features_out(Q, -0.125, H)
            features_out(K, 1.0, H)
            first_probs(FOX)
            rows_out()
            attention(FOX)
            mixer_add(0)
            routing(0)
            experts(0)
            further_tiles(0)
            add_expert_rows(0)
            norm_outs(2)
            features_out(Q, -0.125, H)
            features_out(K, 1.0, 2)
            first_probs(SWA)
            b = next_group()
            nc.vector.tensor_copy(V[64:128, :, 0:128], b[64:128, :].rearrange("p (c n) -> p c n", c=C)).then_inc(s_pjV, 1)
            attention(SWA)
            for c in range(C):
                b = next_group()
                nc.vector.tensor_copy(cq_row[64:128, c, 0:512], b[64:128, :]).then_inc(s_pjV, 1)
            for c in (0, 2):
                b = next_group()
                nc.vector.tensor_copy(cq_row[64:128, c:c + 2, 512:672],
                                      b[64:128, 0:320].rearrange("p (c n) -> p c n", c=2)).then_inc(s_pjV, 1)
            dve.wait_ge(s_pjA, 36)
            dve.wait_ge(s_pjV, 36)
            dve.wait_ge(s_small, 144)
            t1, t2 = cq_row[:, :, 640:656], cq_row[:, :, 656:672]
            for a, (t, cs) in enumerate(((t1, 0), (t2, 1), (t1, 1), (t2, 0))):
                nc.vector.tensor_tensor(ktmp[:, a, :, :], t, krot[:, cs, :, :], ALU.mult)
            then(nc.vector.memset(kpe_pad[:, :, 0:64], 0.0))
            for at in (64, 96):
                nc.vector.tensor_tensor(kpe_pad[:, :, at:at + 16], ktmp[:, 0], ktmp[:, 1], ALU.subtract)
                nc.vector.tensor_tensor(kpe_pad[:, :, at + 16:at + 32], ktmp[:, 2], ktmp[:, 3], ALU.add)
            dve.wait_ge(s_lsq, 8)
            nc.vector.tensor_scalar(ssq[:, 0:4], ssq[:, 0:4], 1.0 / QR, 1e-6, ALU.mult, ALU.add)
            nc.vector.tensor_scalar(ssq[:, 4:8], ssq[:, 4:8], 1.0 / KVR, 1e-6, ALU.mult, ALU.add).then_inc(s_lms, 1)
            dve.wait_ge(s_lrt, 1)
            then(nc.vector.reciprocal(rstd[:, :], rstd[:, :]))

            def latent_out(c):
                dve.wait_ge(s_lt, 2 * c + 2)
                nc.vector.tensor_copy(hnT[:, 4, 128 * c:128 * c + 128], bank[4][:, 0:128])
                nc.vector.tensor_copy(K[64:128, :, 128 * c:128 * c + 128],
                                      bank[4][64:128, 128:256].unsqueeze(1).to_broadcast([64, H, 128])).then_inc(s_ltV, 1)

            for c in range(C):
                nc.vector.scalar_tensor_tensor(cq_row[:, c, 0:QR], cq_row[:, c, 0:QR], rstd[:, c:c + 1],
                                               qkv_gain[:, 0:QR], ALU.mult, ALU.mult)
                nc.vector.scalar_tensor_tensor(cq_row[:, c, QR:QR + KVR], cq_row[:, c, QR:QR + KVR], rstd[:, 4 + c:5 + c],
                                               qkv_gain[:, QR:QR + KVR], ALU.mult, ALU.mult).then_inc(s_lrow, 1)
                if c:
                    latent_out(c - 1)
            latent_out(C - 1)
            for hh in range(H):
                b = next_group()
                nc.vector.tensor_tensor(Q[64:128, hh, :], b[64:128, :], qrot[64:128, :], ALU.mult).then_inc(s_pjV, 1)
            features_out(K, 1.0, H)
            first_probs(MLA)
            rows_out()
            attention(MLA)
            mixer_add(1)
            routing(1)
            experts(1)
            further_tiles(1)
            add_expert_rows(1)


_INS = ["x", "attn_norm", "ffn_norm", "final_norm", "e_w_in", "e_b_f", "e_w_out", "o_w_in", "o_q_norm", "o_kv_norm",
        "o_w_uq", "o_w_ukv", "o_sinks", "o_w_out", "moe_w_group", "moe_b_group", "moe_w_router", "moe_b_router",
        "moe_w_gate", "moe_w_up", "moe_w_down"]


def kernel(**inputs):
    import concourse.bacc as bacc
    from concourse.bass_utils import run_bass_kernel_spmd

    nc = bacc.Bacc("TRN2", target_bir_lowering=False, num_devices=1)
    arrays, args = {}, []
    consts = shape_constants()
    for name in _INS + list(consts):
        a = np.ascontiguousarray(inputs[name] if name in inputs else consts[name])
        arrays[f"in_{name}"] = a
        args.append(nc.dram_tensor(f"in_{name}", a.shape, mybir.dt.from_np(a.dtype), kind="ExternalInput").ap())
    args.append(nc.dram_tensor("out_0", (1, S, DM), mybir.dt.float32, kind="ExternalOutput").ap())
    trunk(nc, *args)
    return run_bass_kernel_spmd(nc, [arrays], core_ids=[0]).results[0]["out_0"]
```

```python
import concourse.bass as bass
from concourse import mybir
from contextlib import ExitStack
import numpy as np

DM, S, C = 1024, 512, 4
KD = DM // 128
H, HD = 8, 64
NE, DE, SLOTS = 32, 256, 64
QR, KVR, NOPE, ROPE = 384, 256, 64, 32
OOB = 1 << 20
BIG = 1e30
MAXOV = (2 * S - 1) // SLOTS

C_ID, C_TRI, C_ONE, C_IOTA, C_TOK, C_OOB, C_THR, C_EPS, C_RANK = 0, 128, 256, 384, 416, 432, 433, 440, 441
C_MASKS = C_RANK + 128
C_CAUSAL, C_DIL, C_SWA, C_END = C_MASKS, C_MASKS + 512, C_MASKS + 1024, C_MASKS + 1280


def shape_constants():
    p = np.arange(128)[:, None]
    t = np.zeros((128, C_END), np.float32)
    t[:, C_ID:C_ID + 128] = np.eye(128)
    t[:, C_TRI:C_TRI + 128] = p < np.arange(128)[None, :]
    t[:, C_ONE:C_ONE + 128] = 1.0
    d = p - np.arange(512)[None, :] + 384
    t[:, C_CAUSAL:C_CAUSAL + 512] = np.where(d >= 0, 0.0, BIG)
    count = (d >= 0) * ((d <= 128) * 1 + (d % 4 == 0) * 1 + (d % 16 == 0) * 1)
    t[:, C_DIL:C_DIL + 512] = np.where(count > 0, -np.log(np.maximum(count, 1)), BIG)
    d = 128 + p - np.arange(256)[None, :]
    t[:, C_SWA:C_SWA + 256] = np.where((d >= 0) & (d <= 127), 0.0, BIG)
    t[:, C_IOTA:C_IOTA + 32] = np.arange(32)
    tok = np.arange(C)[None, :] * 128 + p
    for k in range(2):
        t[:, C_TOK + 4 * k:C_TOK + 4 * k + 4] = 2 * tok
        t[:, C_TOK + 8 + 4 * k:C_TOK + 12 + 4 * k] = 2 * (2 * tok + k)
    t[:, C_OOB:C_OOB + 1] = OOB + (p >= 64)
    t[:, C_EPS] = 1e-6
    t[:, C_RANK:C_RANK + 128] = np.arange(128) % SLOTS
    t[:, C_THR:C_THR + 7] = SLOTS * np.arange(1, 8)
    slope = 2.0 ** -np.arange(1, H + 1)
    pos = np.arange(S) - 256.0
    aug = np.zeros((4, H, S), np.float32)
    aug[0] = slope[:, None] * pos[None, :]
    aug[1] = -slope[:, None]
    aug[2] = 1.0
    aug[3] = pos[None, :]
    inv = np.float32(10000.0) ** (-np.arange(0, ROPE, 2, dtype=np.float32) / np.float32(ROPE))
    ang = (np.arange(S, dtype=np.float32)[:, None] * inv[None, :]).astype(np.float64)
    cos, sin = np.cos(ang), np.sin(ang)
    sc = -((NOPE + ROPE) ** -0.5)
    qrot = np.zeros((128, S), np.float32)
    qrot[64:80] = qrot[80:96] = sc * cos.T
    qrot[96:112] = -sc * sin.T
    qrot[112:128] = sc * sin.T
    krot = np.zeros((128, 2, C, 16), np.float32)
    krot[:, 0] = cos.reshape(C, 128, 16).transpose(1, 0, 2)
    krot[:, 1] = sin.reshape(C, 128, 16).transpose(1, 0, 2)
    return {"const_table": t, "const_aug": aug.reshape(4, H * S), "const_qrot": qrot,
            "const_krot": krot.reshape(128, 128)}


def trunk(nc, x, attn_norm, ffn_norm, final_norm, e_w_in, e_b_f, e_w_out, o_w_in, o_q_norm, o_kv_norm,
          o_w_uq, o_w_ukv, o_sinks, o_w_out, moe_w_group, moe_b_group, moe_w_router, moe_b_router,
          moe_w_gate, moe_w_up, moe_w_down, const_table, const_aug, const_qrot, const_krot, out):
    f32, i32 = mybir.dt.float32, mybir.dt.int32
    ALU, ACT = mybir.AluOpType, mybir.ActivationFunctionType
    X = mybir.AxisListType.X

    hn_dram = [nc.dram_tensor(f"hn_rows{l}", (2 * S, DM // 2), f32, kind="Internal").ap() for l in range(2)]
    tab_dram = [nc.dram_tensor(f"expert_table{l}", (S * NE, 4), i32, kind="Internal").ap() for l in range(2)]
    c_dram = nc.dram_tensor("forget_sums", (2, H * S), f32, kind="Internal").ap()
    y_dram = [nc.dram_tensor(f"expert_rows{l}", (2 * 2 * S, DM // 2), f32, kind="Internal").ap() for l in range(2)]

    wg_v = [moe_w_gate[l].rearrange("g e (h p k) f -> (g e) p h (k f)", h=2, p=128) for l in range(2)]
    wu_v = [moe_w_up[l].rearrange("g e (h p k) f -> (g e) p h (k f)", h=2, p=128) for l in range(2)]
    wd_v = [moe_w_down[l].rearrange("g e (p c) d -> (g e) p (c d)", p=128) for l in range(2)]
    ewin_v = e_w_in.rearrange("a (k p) n -> p (a k) n", p=128)
    owin_v = o_w_in.rearrange("a (k p) n -> p (a k) n", p=128)
    ewout_v = e_w_out.rearrange("a (k p) n -> p (a k) n", p=128)
    owout_v = o_w_out.rearrange("a (k p) n -> p (a k) n", p=128)

    fw = H * HD
    FOX0, ZF0, DIL0 = 0, 3 * fw, 3 * fw + H
    EVEN_COLS = [DIL0, DIL0 + fw, DIL0 + 2 * fw, FOX0, FOX0 + fw, FOX0 + 2 * fw]
    QS0 = QR + KVR + ROPE
    KS0 = QS0 + fw
    BESIDE = [4, 5, 10, 11]
    LOOP0 = BESIDE[-1] + 1
    T_ODD = 8 + NE - len(BESIDE)
    T_MOE = [8, T_ODD + 8]

    def expert_tile(lay, e):
        return T_MOE[lay] + e - sum(b < e for b in BESIDE)

    DIL, FOX, SWA, MLA = range(4)
    LEN = {f: [128 * (i + 1) for i in range(4)] for f in (DIL, FOX, MLA)}
    LEN[SWA] = [128, 256, 256, 256]
    FIRST_KEY = {f: [0] * 4 for f in (DIL, FOX, MLA)}
    FIRST_KEY[SWA] = [0, 0, 1, 2]
    MASK = {DIL: (C_DIL, 512), FOX: (C_CAUSAL, 512), MLA: (C_CAUSAL, 512), SWA: (C_SWA, 256)}

    def p_col(f, i):
        return sum(LEN[f][:i])

    def q_chunks(f, j):
        return [i for i in range(4) if FIRST_KEY[f][i] <= j <= i]

    def pt_col(f, j):
        return sum(128 * len(q_chunks(f, jj)) for jj in range(j))

    ctx = ExitStack()
    with ctx:
        def sb(name, shape, dt=f32):
            return ctx.enter_context(nc.sbuf_tensor(name, shape, dt))

        def sem(name):
            return ctx.enter_context(nc.semaphore(name))

        h = sb("h", [128, C, DM])
        hnT = sb("hnT", [128, KD, S])
        Q = sb("Q", [128, H, S])
        K = sb("K", [128, H, S])
        oT = sb("oT", [128, KD, S])
        V = sb("V", [128, C, 512])
        W = [sb(f"W{i}", [128, 4096]) for i in range(4)]
        D = [sb(f"D{i}", [128, 2048]) for i in range(4)]
        P = sb("P", [128, 2, 1280])
        PT = sb("PT", [128, 1280])
        cst = sb("cst", [128, C_END])
        nm = sb("nm", [128, 8])
        den = sb("den", [128, 8])
        rden = sb("rden", [128, 8])
        esink = sb("esink", [128, 8])
        sinks = sb("sinks", [128, 2 * H])
        ssq = sb("ssq", [128, 8])
        rstd = sb("rstd", [128, 8])
        ncells = sb("ncells", [1, 32], i32)
        turn = sb("turn", [1, 4])
        bf_sb = sb("bf_sb", [8, 1])
        warm = sb("warm", [1, 4])
        bank = [ctx.enter_context(nc.psum_tensor(f"bank{i}", [128, 512], f32)) for i in range(8)]

        ident = cst[:, C_ID:C_ID + 128]
        iota = cst[:, C_IOTA:C_IOTA + 32]

        hn_row = Q[:, :, :].rearrange("p h s -> p (h s)").rearrange("p (c d) -> p c d", c=C)
        flatQ = Q[:, :, :].rearrange("p h s -> p (h s)")
        flatK = K[:, :, :].rearrange("p h s -> p (h s)")
        flatV = V[:, :, :].rearrange("p c s -> p (c s)")
        flatO = oT[:, :, :].rearrange("p k s -> p (k s)")
        flatT = hnT[:, :, :].rearrange("p k s -> p (k s)")
        WB, DB = [flatO, flatQ], [flatT[:, 0:2048], flatT[:, 2048:4096]]
        gain = P[:, 0, 0:DM]
        eps = cst[:, C_EPS:C_EPS + 1]
        Xg = [flatK[:, 512 * i:512 * i + 512] for i in range(4)]
        XT = [flatK[:, 2048 + 512 * i:2560 + 512 * i] for i in range(2)]
        sil = [PT[:, 256 * i:256 * i + 256] for i in range(2)]
        hid = [PT[:, 512 + 256 * i:768 + 256 * i] for i in range(2)]
        hT = [PT[:, 1024 + 128 * i:1152 + 128 * i] for i in range(2)]
        Y = [flatV[:, 0:512], flatV[:, 512:1024], flatK[:, 3072:3584], flatK[:, 3584:4096]]
        wr = flatV[:, 1024:1312].rearrange("p (k n) -> p k n", k=KD)
        rbias = flatV[:, 1312:1348]
        rec = flatV[:, 1348:1380].bitcast(i32)
        wtab = flatV[:, 1380:1412]
        pad = flatV[:, 1412:1444]
        gidx = flatV[:, 1508:1540].bitcast(i32)
        sidx = flatV[:, 1540:1572].bitcast(i32)
        slot = flatV[:, 1572:1580].bitcast(i32)
        ibuf = flatV[:, 1580:1588].bitcast(i32)
        orec = flatV[:, 1588:1592].bitcast(i32)
        oidx = flatV[:, 1592:1594].bitcast(i32)
        zf_w = D[2][:, 0:64].rearrange("p (k n) -> p k n", k=KD)
        zf = [D[3][0:8, 512 * i:512 * i + 512] for i in range(4)]
        junk = flatV[:, 0:1024]
        PTs = [PT[:, :], D[2][:, 640:1920]]
        pt_bank = [3, 4, 6, 7]
        cq_row = flatK[:, 1024:3712].rearrange("p (c n) -> p c n", c=C)
        kpe_T = oT[64:128, 0, :]
        kpe_pad = PT[:, 0:512].rearrange("p (c n) -> p c n", c=C)
        ktmp = PT[:, 512:768].rearrange("p (a c n) -> p a c n", a=4, c=C)
        qkv_gain = P[:, 1, 0:QR + KVR]
        qrot = P[:, 0, 640:1152]
        krot_in = P[:, 1, QR + KVR:QR + KVR + 128]
        krot = krot_in.rearrange("p (a c n) -> p a c n", a=2, c=C)
        y_in = [flatQ[:, 0:2048], flatK[:, 0:2048], flatQ[:, 2048:4096], flatK[:, 2048:4096]]
        tab_init = Xg[1].bitcast(i32)
        f16 = mybir.dt.float16
        rank_hot = P[:, 0, 0:512].bitcast(f16).rearrange("p (n r) -> p n r", n=2 * C)
        rank_hot32 = flatK[:, 3072:4096].rearrange("p (n r) -> p n r", n=2 * C)
        facts = PT[:, 0:384].bitcast(f16).rearrange("p (n q e) -> p n q e", n=2 * C, q=3)
        wfacts = PT[:, 384:640].rearrange("p (n e) -> p n e", n=2 * C)

        R = P[:, 1, :]

        def r(at, *dims):
            n = int(np.prod(dims))
            v = R[:, at:at + n]
            if len(dims) == 2:
                v = v.rearrange("p (a b) -> p a b", a=dims[0])
            if len(dims) == 3:
                v = v.rearrange("p (a b c) -> p a b c", a=dims[0], b=dims[1])
            return v

        lg, gmax, gexp, gsum = r(0, 4, 36), r(144, 4), r(148, 4, 4), r(164, 4)
        gw, gpick, gmin, goh, gpen = r(168, 4), r(172, 4, 4), r(188, 4), r(192, 4, 4), r(208, 4, 4)
        em = [r(224, 4, 32), r(352, 4, 32)]
        pick = [r(480, 4, 32), r(608, 4, 32)]
        oh = [PT[:, 640 + 128 * k:768 + 128 * k].rearrange("p (c e) -> p c e", c=C) for k in range(2)]
        ohs = r(992, 64).bitcast(mybir.dt.bfloat16).rearrange("p (c e) -> p c e", c=C)
        tri_ones = P[:, 0, 1024:1152].bitcast(mybir.dt.bfloat16)
        tri, ones = tri_ones[:, 0:128], tri_ones[:, 128:256]
        emax = [r(1120, 4), r(1124, 4)]
        emin = [r(1128, 4), r(1132, 4)]
        ed, esum, einv, wgt = r(1136, 4), r(1140, 4), r(1144, 4), r(1148, 2, 4)
        rpos = [r(1156, 4), r(1160, 4)]
        rslot = [r(736, 4), r(740, 4)]
        extra, ends = R[0:1, 1164:1196], R[0:1, 1196:1228]
        oe, ostart = R[0:1, 1228:1243], R[0:1, 1243:1258]
        ovbig = [P[0:1, 0, 0:480], P[0:1, 0, 480:960]]

        s_const = sem("const_loaded")
        s_masks = sem("masks_loaded")
        s_heads = sem("head_constants_loaded")
        s_x = [sem(f"x_loaded{c}") for c in range(C)]
        s_small = sem("small_loaded")
        s_ld = [sem(f"tile_loaded{i}") for i in range(4)]
        s_lb = [sem(f"expert_beside_loaded{i}") for i in range(2)]
        s_dn = [sem(f"down_tile_loaded{i}") for i in range(4)]
        s_dnb = [sem(f"down_beside_loaded{i}") for i in range(2)]
        s_yhalf = sem("second_choices_loaded")
        s_half = sem("half_of_first_tile_loaded")
        s_gain = sem("gain_loaded")
        s_sq = sem("squares_summed")
        s_sqrt = sem("root_taken")
        s_hn = sem("normed_rows")
        s_nt = sem("norm_transposed")
        s_ntA = sem("norm_t_out_act")
        s_ntV = sem("norm_t_out_dve")
        s_pj = sem("projected")
        s_pjA = sem("proj_out_act")
        s_pjV = sem("proj_out_dve")
        s_aug = sem("position_rows")
        s_zf = sem("forget_logits")
        s_cst = sem("forget_sums_stored")
        s_zfa = sem("forget_act")
        s_zfv = sem("forget_dve")
        s_qk = sem("scores_ready")
        s_msk = sem("scores_masked")
        s_exp = sem("probs_ready")
        s_nrm = sem("probs_normalised")
        s_tr = sem("probs_transposed")
        s_teA = sem("probs_t_out_act")
        s_teV = sem("probs_t_out_dve")
        s_pv = sem("head_output")
        s_oev = sem("head_pair_out")
        s_og = sem("mixer_projected")
        s_oga = sem("mixer_added")
        s_lrow = sem("latent_rows_normed")
        s_lt = sem("latent_transposed")
        s_ltA = sem("latent_out_act")
        s_ltV = sem("latent_out_dve")
        s_lsq = sem("latent_squares")
        s_lms = sem("latent_mean_square")
        s_lrt = sem("latent_root")
        s_perm = sem("rotary_copies")
        s_hnst = sem("normed_rows_stored")
        s_lg = sem("router_logits")
        s_rsub = sem("router_differences")
        s_rexp = sem("router_exps")
        s_oh = sem("expert_one_hots")
        s_rank = sem("expert_ranks")
        s_facts = sem("slot_facts")
        s_slots = sem("slots_filled")
        s_idx = sem("expert_indices")
        s_ncell = sem("further_tiles_listed")
        s_slot0 = sem("further_tiles_over")
        s_ib = sem("index_column")
        s_g = [sem(f"rows_gathered{i}") for i in range(4)]
        s_xt = sem("rows_transposed")
        s_xte = sem("rows_t_out")
        s_gu = sem("gate_up_done")
        s_sil = sem("silu_done")
        s_hid = sem("hidden_done")
        s_ht = sem("hidden_transposed")
        s_hte = sem("hidden_t_out")
        s_y = sem("down_done")
        s_ye = sem("down_out")
        s_sc = [sem(f"rows_scattered{i}") for i in range(4)]
        ov = [{n: sem(f"further{l}_{n}") for n in
               ("loaded", "records", "indices", "gathered", "xt", "xte", "gu", "sil", "hid", "ht", "hte",
                "y", "ye", "down", "scattered", "out", "init", "table")} for l in range(2)]
        s_yld = [sem(f"expert_rows_loaded{c}") for c in range(C)]
        s_yadd = sem("expert_rows_added")
        s_out = sem("output_stored")
        s_dv = sem("dve_order")
        s_av = sem("act_order")
        s_pl = sem("pool_order")

        block = ctx.enter_context(nc.Block())

        def tile_ready(n):
            return 48 * (n // 4 + 1)

        def last_read(n):
            if n < 6:
                return s_pj, 4 * (n + 1)
            if n < 8:
                return s_og, 4 * (n - 5)
            if n < T_ODD:
                return s_y, n - T_MOE[0] + len(BESIDE) + 1
            if n < T_ODD + 6:
                return s_pj, (28, 30, 34, 36, 44, 52)[n - T_ODD]
            return s_og, 8 + 4 * (n - T_ODD - 5)

        @block.sync
        def _(sp):
            for c in range(C):
                sp.dma_start(h[:, c, :], x[0, 128 * c:128 * c + 128, :]).then_inc(s_x[c], 16)
                if c == 0:
                    sp.dma_start(cst[:, 0:C_MASKS], const_table[:, 0:C_MASKS]).then_inc(s_const, 16)

            def slot_free(n):
                if n >= 4:
                    sp.wait_ge(*last_read(n - 4))

            def load_cols(n, src, c0, width):
                slot_free(n)
                dst = W[n % 4][:, :].rearrange("p (k n) -> p k n", k=KD)
                sp.dma_start(dst[:, :, 0:width], src[:, :, c0:c0 + width]).then_inc(s_ld[n % 4], 48)

            def load_expert(lay, w, gate_up, down, done, down_done, down_free=None, up_after=None):
                for v, at, count in ((wg_v[lay], 0, 16), (wu_v[lay], 2048, 32)):
                    dst = gate_up[:, at:at + 2048].rearrange("p (h x) -> p h x", h=2)
                    if at and up_after is not None:
                        sp.wait_ge(*up_after)
                    sp.dma_start(dst, v[bass.ds(w, 1), :, :, :].rearrange("a p h x -> (a p) h x"))\
                      .then_inc(done, count)
                if down_free is not None:
                    sp.wait_ge(*down_free)
                sp.dma_start(down, wd_v[lay][bass.ds(w, 1), :, :].rearrange("a p x -> (a p) x"))\
                  .then_inc(down_done, 16)

            def experts(lay):
                base = NE * lay
                for s in range(4):
                    slot_free(T_MOE[lay] + s)
                    load_expert(lay, s, W[s][:, :], D[s][:, :], s_ld[s], s_dn[s])
                sp.wait_ge(s_og, 8 * (lay + 1))
                load_expert(lay, BESIDE[0], WB[0], DB[0], s_lb[0], s_dnb[0], (s_lg, C * (lay + 1)))
                sp.wait_ge(s_hnst, 64 * (lay + 1))
                load_expert(lay, BESIDE[1], WB[1], DB[1], s_lb[1], s_dnb[1], up_after=(s_g[0], 16 * (8 * lay + 1)))
                for e in range(6, LOOP0 + 4):
                    before = base + e - 6 + 1
                    sp.wait_ge(s_gu, before)
                    if e in BESIDE:
                        i = e % 2
                        load_expert(lay, e, WB[i], DB[i], s_lb[i], s_dnb[i], (s_y, before))
                    else:
                        s = expert_tile(lay, e) % 4
                        load_expert(lay, e, W[s][:, :], D[s][:, :], s_ld[s], s_dn[s], (s_y, before))
                with sp.Fori(LOOP0 + 4, NE - 3, 4) as e:
                    for s in range(4):
                        w = sp.snap(e + s)
                        before = e + (base + s - 3)
                        sp.wait_ge(s_gu, before)
                        load_expert(lay, w, W[s][:, :], D[s][:, :], s_ld[s], s_dn[s], (s_y, before))

            def further_tiles(lay):
                o_ = ov[lay]
                sp.wait_ge(s_ncell, lay + 1)
                n_over = sp.value_load(ncells[0:1, 0:1], min_val=0, max_val=MAXOV)
                with sp.If(n_over > 0):
                    sp.wait_ge(s_y, NE * (lay + 1))
                    with sp.Fori(0, n_over) as o:
                        ex = sp.value_load(ncells[0:1, bass.ds(o + 1, 1)], min_val=0, max_val=NE - 1)
                        rk = sp.value_load(ncells[0:1, bass.ds(o + (1 + MAXOV), 1)], min_val=1, max_val=7)
                        sp.wait_ge(o_["out"], o + 2)
                        load_expert(lay, ex, W[0][:, :], D[0][:, :], o_["loaded"], o_["down"])
                        tv = tab_dram[lay].rearrange("(r e) w -> r (e w)", e=NE)
                        for half in range(2):
                            sp.dma_start(orec[64 * half:64 * half + 64, :],
                                         tv[bass.ds(sp.snap(rk * SLOTS), SLOTS), bass.ds(sp.snap(ex * 4), 4)])\
                              .then_inc(o_["records"], 16)
                    sp.wait_ge(o_["out"], n_over + 2)
                    sp.sem_inc(s_slot0, 1)

            sp.wait_ge(s_gain, 16)
            for half in range(2):
                sp.dma_start(W[0][:, :].rearrange("p (k n) -> p k n", k=KD)[:, :, 256 * half:256 * half + 256],
                             ewin_v[:, :, DIL0 + 256 * half:DIL0 + 256 * half + 256])\
                  .then_inc((s_half, s_ld[0])[half], (16, 48)[half])
            sp.dma_start(cst[:, C_MASKS:C_END], const_table[:, C_MASKS:C_END]).then_inc(s_masks, 16)
            def load_expert_rows(lay):
                for i in range(4):
                    sp.wait_ge(s_sc[i], 16 * 8 * (lay + 1))
                y = y_dram[lay].rearrange("(s f) d -> s (f d)", f=4)
                sp.dma_start(y_in[0][:, 0:DM], y[0:128, 0:DM]).then_inc(s_yld[0], 16)
                sp.dma_start(y_in[0][:, DM:2 * DM], y[0:128, DM:2 * DM]).then_inc(s_yhalf, 16)
                for c in range(1, C):
                    sp.dma_start(y_in[c], y[128 * c:128 * c + 128, :]).then_inc(s_yld[c], 16)

            for n, c0 in enumerate(EVEN_COLS):
                if n:
                    load_cols(n, ewin_v, c0, 512)
            for half in range(2):
                load_cols(6 + half, ewout_v, 512 * half, 512)
            experts(0)
            further_tiles(0)
            load_cols(T_ODD, owin_v, 0, 512)
            load_cols(T_ODD + 1, owin_v, 512, QR + KVR + ROPE - 512)
            load_expert_rows(0)
            load_cols(T_ODD + 2, owin_v, QS0, 512)
            load_cols(T_ODD + 3, owin_v, KS0, 256)
            slot_free(T_ODD + 4)
            for k in range(3):
                dst = W[(T_ODD + 4) % 4][:, 0:3072].rearrange("p (k h n) -> p k h n", k=3, h=H)
                sp.dma_start(dst[:, k, :, 0:96],
                             o_w_uq[0, 128 * k:128 * k + 128, :].rearrange("p (h n) -> p h n", h=H))\
                  .then_inc(s_ld[(T_ODD + 4) % 4], 16)
            slot_free(T_ODD + 5)
            sp.dma_start(W[(T_ODD + 5) % 4][:, 0:2048].rearrange("p (k n) -> p k n", k=2),
                         o_w_ukv.rearrange("a (k p) n -> p (a k) n", p=128)).then_inc(s_ld[(T_ODD + 5) % 4], 48)
            for half in range(2):
                load_cols(T_ODD + 6 + half, owout_v, 512 * half, 512)
            experts(1)
            further_tiles(1)
            load_expert_rows(1)
            for c in range(C):
                sp.wait_ge(s_hn, 16 + c + 1)
                sp.dma_start(out[0, 128 * c:128 * c + 128, :], hn_row[:, c, :]).then_inc(s_out, 16)
            sp.wait_ge(s_out, 16 * C)

        @block.gpsimd
        def _(pool):
            order = [0]
            last_half_row = pool.to_reg(2 * S - 1)
            last_result = pool.to_reg(4 * S - 1)

            def then(ins):
                order[0] += 1
                ins.then_inc(s_pl, 1)
                pool.wait_ge(s_pl, order[0])

            def hold(at=1):
                return nc.gpsimd.tensor_tensor(turn[:, at:at + 1], turn[:, 0:1], turn[:, 0:1], ALU.add)

            def load_gain(v):
                src = (attn_norm[0:1, :], ffn_norm[0:1, :], attn_norm[1:2, :], ffn_norm[1:2, :],
                       final_norm.rearrange("(a n) -> a n", a=1))[v]
                pool.dma_start(gain, src.partition_broadcast(128).rearrange("a b n -> a (b n)")).then_inc(s_gain, 16)

            load_gain(0)
            then(nc.gpsimd.memset(turn[:, :], 0.0))
            pool.dma_start(sinks[:, 0:H], o_sinks[0:1, :].partition_broadcast(128).rearrange("a b n -> a (b n)")
                           ).then_inc(s_heads, 16)
            pool.dma_start(bf_sb[:, :], e_b_f.rearrange("a n -> n a")).then_inc(s_heads, 16)

            def alibi_rows(kv_heads):
                pool.dma_start(Q[64:66, :, :].rearrange("p h s -> p (h s)"), const_aug[0:2, :]).then_inc(s_aug, 16)
                pool.dma_start(K[64:66, 0:kv_heads, :].rearrange("p h s -> p (h s)"),
                               const_aug[2:4, 0:kv_heads * S]).then_inc(s_aug, 16)

            def routing(lay):
                pool.wait_ge(s_oga, 8 * lay + 1)
                pool.dma_start(wr[:, :, 0:4], moe_w_group[lay].rearrange("(k p) n -> p k n", p=128)).then_inc(s_small, 16)
                pool.dma_start(wr[:, :, 4:36], moe_w_router[lay].rearrange("(k p) n -> p k n", p=128)).then_inc(s_small, 16)
                pool.dma_start(rbias[:, 0:4], moe_b_group[lay:lay + 1, :].partition_broadcast(128)
                               .rearrange("a b n -> a (b n)")).then_inc(s_small, 16)
                pool.dma_start(rbias[:, 4:36], moe_b_router[lay:lay + 1, :].partition_broadcast(128)
                               .rearrange("a b n -> a (b n)")).then_inc(s_small, 16)
                for c in range(C):
                    pool.wait_ge(s_hn, 4 * (2 * lay + 1) + c + 1)
                    pool.dma_start(hn_dram[lay].rearrange("(s h) d -> s (h d)", h=2)[128 * c:128 * c + 128, :],
                                   hn_row[:, c, :]).then_inc(s_hnst, 16)

            def gather(lay, dst, idx_col, done):
                pool.indirect_dma_start(out=dst, out_offset=None, in_=hn_dram[lay],
                                        in_offset=bass.IndirectOffsetOnAxis(ap=idx_col, axis=0),
                                        bounds_check=last_half_row, oob_is_err=False).then_inc(done, 16)

            def scatter(lay, src, idx_col, done):
                pool.indirect_dma_start(out=y_dram[lay],
                                        out_offset=bass.IndirectOffsetOnAxis(ap=idx_col, axis=0),
                                        in_=src, in_offset=None,
                                        bounds_check=last_result, oob_is_err=False).then_inc(done, 16)

            def expert_rows(lay):
                base = NE * lay
                pool.wait_ge(s_idx, lay + 1)
                pool.wait_ge(s_hnst, 64 * (lay + 1))

                for s in range(4):
                    nc.gpsimd.tensor_copy(ibuf[:, s:s + 1], gidx[:, s:s + 1]).then_inc(s_ib, 1)
                    pool.wait_ge(s_ib, 64 * lay + s + 1)
                    gather(lay, Xg[s], ibuf[:, s:s + 1], s_g[s])
                pool.wait_ge(s_ncell, lay + 1)
                load_gain(2 * lay + 2)
                if lay == 0:
                    pool.dma_start(qkv_gain[:, 0:QR], o_q_norm[0:1, :].partition_broadcast(128)
                                   .rearrange("a b n -> a (b n)")).then_inc(s_small, 16)
                    pool.dma_start(qkv_gain[:, QR:QR + KVR], o_kv_norm[0:1, :].partition_broadcast(128)
                                   .rearrange("a b n -> a (b n)")).then_inc(s_small, 16)
                    pool.dma_start(krot_in, const_krot).then_inc(s_small, 16)

                def scatter_first(e, s, col):
                    pool.wait_ge(s_ye, e + (base + 1))
                    nc.gpsimd.tensor_copy(ibuf[:, 4 + s:5 + s], sidx[:, col]).then_inc(s_ib, 1)

                with pool.Fori(0, NE - 7, 4) as e0:
                    for s in range(4):
                        e = e0 + s
                        ahead = pool.snap(e0 + (s + 4))
                        pool.wait_ge(s_xt, e + (base + 1))
                        nc.gpsimd.tensor_copy(ibuf[:, s:s + 1], gidx[:, bass.ds(ahead, 1)]).then_inc(s_ib, 1)
                        pool.wait_ge(s_ib, e0 * 2 + (64 * lay + 2 * s + 5))
                        hold()
                        gather(lay, Xg[s], ibuf[:, s:s + 1], s_g[s])
                        scatter_first(e, s, bass.ds(pool.snap(e), 1))
                        pool.wait_ge(s_ib, e0 * 2 + (64 * lay + 2 * s + 6))
                        hold(2)
                        scatter(lay, Y[s], ibuf[:, 4 + s:5 + s], s_sc[s])
                for s in range(4):
                    e = NE - 4 + s
                    scatter_first(e, s, slice(e, e + 1))
                    pool.wait_ge(s_ib, 64 * lay + 4 + 2 * (NE - 4) + s + 1)
                    scatter(lay, Y[s], ibuf[:, 4 + s:5 + s], s_sc[s])
                for s in range(4):
                    pool.wait_ge(s_sc[s], 16 * 8 * (lay + 1))

            def further_tiles(lay):
                o_ = ov[lay]
                pool.wait_ge(s_ncell, lay + 1)
                n_over = pool.value_load(ncells[0:1, 0:1], min_val=0, max_val=MAXOV)
                with pool.If(n_over > 0):
                    nc.gpsimd.memset(tab_init, OOB).then_inc(o_["out"], 1)
                    pool.wait_ge(o_["out"], 1)
                    pool.dma_start(tab_dram[lay].rearrange("(p r) w -> p (r w)", p=128), tab_init)\
                        .then_inc(o_["init"], 16)
                    pool.wait_ge(o_["init"], 16)
                    for kc in range(2 * C):
                        pool.indirect_dma_start(out=tab_dram[lay],
                                                out_offset=bass.IndirectOffsetOnAxis(ap=slot[:, kc:kc + 1], axis=0),
                                                in_=rec[:, 4 * kc:4 * kc + 4], in_offset=None,
                                                bounds_check=S * NE - 1, oob_is_err=False).then_inc(o_["table"], 16)
                    pool.wait_ge(o_["table"], 32 * C)
                    hold(3).then_inc(o_["out"], 1)
                    with pool.Fori(0, n_over) as o:
                        pool.wait_ge(o_["indices"], o + 1)
                        hold()
                        gather(lay, Xg[0], oidx[:, 0:1], o_["gathered"])
                        pool.wait_ge(o_["ye"], o + 1)
                        hold(2)
                        scatter(lay, Y[0], oidx[:, 1:2], o_["scattered"])
                        pool.wait_ge(o_["scattered"], o * 16 + 16)
                        hold(3).then_inc(o_["out"], 1)

            pool.dma_start(zf_w, ewin_v[:, :, ZF0:ZF0 + H]).then_inc(s_small, 16)
            then(nc.gpsimd.memset(K[64:128, :, :], 0.0))
            pool.wait_ge(s_nt, 8)
            alibi_rows(H)
            pool.wait_ge(s_zfv, 5)
            for i in range(2):
                pool.dma_start(c_dram[i].rearrange("(h s) -> h s", h=H), zf[2 + i]).then_inc(s_cst, 16)
            pool.wait_ge(s_cst, 32)
            pool.wait_ge(s_qk, 4 * H)
            pool.dma_start(Q[65:66, :, :].rearrange("p h s -> p (h s)"), const_aug[2:3, :]).then_inc(s_aug, 16)
            pool.dma_start(Q[64:65, :, :].rearrange("p h s -> p (h s)"), c_dram[1:2, :]).then_inc(s_aug, 16)
            pool.dma_start(K[65:66, :, :].rearrange("p h s -> p (h s)"), c_dram[0:1, :]).then_inc(s_aug, 16)
            pool.wait_ge(s_tr, 4 * 2 * H)
            load_gain(1)
            routing(0)
            expert_rows(0)
            further_tiles(0)
            pool.wait_ge(s_yadd, C)
            then(nc.gpsimd.memset(K[64:128, 0:2, :], 0.0))
            pool.wait_ge(s_nt, 8 * 3)
            alibi_rows(2)
            t = T_ODD + 4
            pool.wait_ge(s_ld[t % 4], tile_ready(t))
            uq = W[t % 4][:, 0:3072].rearrange("p (kh n) -> p kh n", n=128)
            nc.gpsimd.tensor_copy(uq[:, :, 96:112], uq[:, :, 80:96]).then_inc(s_perm, 1)
            nc.gpsimd.tensor_copy(uq[:, :, 112:128], uq[:, :, 64:80]).then_inc(s_perm, 1)
            pool.wait_ge(s_ltV, C)
            for n, (h0, h1) in enumerate(((2, H), (0, 2))):
                pool.wait_ge(s_perm, 2 + n)
                if n:
                    pool.wait_ge(s_qk, 4 * 3 * H)
                nc.gpsimd.tensor_copy(K[64:128, h0:h1, :], kpe_T.unsqueeze(1).to_broadcast([64, h1 - h0, S]))\
                  .then_inc(s_perm, 1)
            pool.wait_ge(s_tr, 4 * 3 * H)
            pool.dma_start(qrot, const_qrot).then_inc(s_small, 16)
            pool.wait_ge(s_tr, 4 * 4 * H)
            load_gain(3)
            routing(1)
            expert_rows(1)
            further_tiles(1)

        @block.tensor
        def _(pe):
            pe.wait_ge(s_const, 16)
            group = [0]

            def group_start():
                g = group[0]
                if g >= 2:
                    pe.wait_ge(s_pjA, g - 1)
                    pe.wait_ge(s_pjV, g - 1)
                group[0] += 1
                return bank[6 + g % 2]

            def w_tile(n):
                return W[n % 4][:, :].rearrange("p (k n) -> p k n", k=KD)

            def router_logits(v, c):
                if c == 0:
                    pe.wait_ge(s_small, (80, 208)[v // 2])
                pe.wait_ge(s_ntA, 4 * v + c + 1)
                pe.wait_ge(s_ntV, 4 * v + c + 1)
                for k in range(KD):
                    last = nc.tensor.matmul(bank[6][:, 36 * c:36 * c + 36], hnT[:, k, 128 * c:128 * c + 128],
                                            wr[:, k, :], start=(k == 0), stop=(k == KD - 1))
                last.then_inc(s_lg, 1)

            def transpose_normed(v, c):
                pe.wait_ge(s_hn, 4 * v + c + 1)
                for half in range(2):
                    if c or v:
                        pe.wait_ge((s_ntA, s_ntV)[half], 4 * v + c)
                    for kk in range(4):
                        k = 4 * half + kk
                        last = nc.tensor.transpose(bank[3 + half][:, 128 * kk:128 * kk + 128],
                                                   hn_row[:, c, 128 * k:128 * k + 128], ident)
                    last.then_inc(s_nt, 1)

            def norm_ready(v):
                pe.wait_ge(s_ntA, 4 * v + 4)
                pe.wait_ge(s_ntV, 4 * v + 4)

            def project_features(n, blocks):
                w = w_tile(n)
                pe.wait_ge(*((s_half, 16) if n == 0 else (s_ld[n % 4], tile_ready(n))))
                for fb in range(blocks):
                    if n == 0 and fb == 2:
                        pe.wait_ge(s_ld[0], tile_ready(0))
                    b = group_start()
                    for k in range(KD):
                        last = nc.tensor.matmul(b[:, :], w[:, k, 128 * fb:128 * fb + 128], hnT[:, k, :],
                                                start=(k == 0), stop=(k == KD - 1))
                    last.then_inc(s_pj, 1)

            def project_rows(n, c0, width, per_group, chunks=range(C)):
                w = w_tile(n)
                pe.wait_ge(s_ld[n % 4], tile_ready(n))
                for c in chunks:
                    if c % per_group == 0:
                        b = group_start()
                    at = (c % per_group) * width
                    for k in range(KD):
                        last = nc.tensor.matmul(b[:, at:at + width], hnT[:, k, 128 * c:128 * c + 128],
                                                w[:, k, c0:c0 + width], start=(k == 0), stop=(k == KD - 1))
                    if c % per_group == per_group - 1:
                        last.then_inc(s_pj, 1)

            def scores(f, u):
                g = H * f + u
                kv = u // 4 if f == SWA else u
                for i in range(4):
                    b = 4 * g + i
                    if b >= 3:
                        pe.wait_ge(s_msk, b - 2)
                    k0, n = 128 * FIRST_KEY[f][i], LEN[f][i]
                    nc.tensor.matmul(bank[b % 3][:, 0:n], Q[:, u, 128 * i:128 * i + 128],
                                     K[:, kv, k0:k0 + n], start=True, stop=True).then_inc(s_qk, 1)

            def transposes(f, u):
                g = H * f + u
                pe.wait_ge(s_nrm, 4 * g + 4)
                for j in range(4):
                    if g:
                        pe.wait_ge((s_teA, s_teV)[j % 2], 2 * g - 1 + j // 2)
                    for a, i in enumerate(q_chunks(f, j)):
                        at = p_col(f, i) + 128 * (j - FIRST_KEY[f][i])
                        last = nc.tensor.transpose(bank[pt_bank[j]][:, 128 * a:128 * a + 128],
                                                   P[:, u % 2, at:at + 128], ident)
                    last.then_inc(s_tr, 1)

            def pair_outputs(f, u):
                g = H * f + u
                if g == 0:
                    pe.wait_ge(s_zfv, 1)
                else:
                    pe.wait_ge(s_oev, g // 2)
                for j in range(4):
                    pe.wait_ge((s_teA, s_teV)[j % 2], 2 * (g + 1) + j // 2 + 1)
                    n = 128 * len(q_chunks(f, j))
                    for a in range(2):
                        vc = 64 * (u // 4) if f == SWA else 64 * (u + a)
                        last = nc.tensor.matmul(bank[5][64 * a:64 * a + 64, 128 * j:128 * j + n],
                                                V[:, j, vc:vc + 64], PTs[a][:, pt_col(f, j):pt_col(f, j) + n],
                                                start=(j == 0), stop=(j == 3), skip_group_check=True)
                last.then_inc(s_pv, 1)

            def first_scores(f, groups, aug):
                pe.wait_ge(s_pjA, groups)
                pe.wait_ge(s_pjV, groups)
                pe.wait_ge(s_aug, aug)
                scores(f, 0)
                scores(f, 1)

            def attention(f, groups):
                pe.wait_ge(s_pjA, groups)
                pe.wait_ge(s_pjV, groups)
                for u in range(0, H, 2):
                    for a in range(2):
                        transposes(f, u + a)
                        if u + 2 < H:
                            scores(f, u + 2 + a)
                    pair_outputs(f, u)

            def mixer_out(lay, n0):
                pe.wait_ge(s_oev, 8 * (lay + 1))
                for half in range(2):
                    n = n0 + half
                    pe.wait_ge(s_ld[n % 4], tile_ready(n))
                    for c in range(C):
                        g = 8 * lay + 4 * half + c
                        if g >= 2:
                            pe.wait_ge(s_oga, g - 1)
                        for k in range(KD):
                            last = nc.tensor.matmul(bank[g % 2][:, :], oT[:, k, 128 * c:128 * c + 128],
                                                    w_tile(n)[:, k, :], start=(k == 0), stop=(k == KD - 1))
                        last.then_inc(s_og, 1)
                        if half and c >= 1:
                            transpose_normed(2 * lay + 1, c - 1)
                        if half and c >= 2:
                            router_logits(2 * lay + 1, c - 2)
                router_logits(2 * lay + 1, C - 2)
                transpose_normed(2 * lay + 1, C - 1)
                router_logits(2 * lay + 1, C - 1)

            def routing(lay):
                pe.wait_ge(s_oh, lay + 1)
                for c in range(C):
                    for cc in range(c):
                        nc.tensor.matmul(bank[7][:, 32 * c:32 * c + 32], ones, ohs[:, cc, :],
                                         start=(cc == 0), stop=False)
                    nc.tensor.matmul(bank[7][:, 32 * c:32 * c + 32], tri, ohs[:, c, :], start=(c == 0), stop=True)
                for c in range(C):
                    last = nc.tensor.matmul(bank[7][:, 128:160], ones, ohs[:, c, :], start=(c == 0), stop=(c == C - 1))
                last.then_inc(s_rank, 1)
                for n in range(2 * C):
                    if n % C == 0:
                        pe.wait_ge(s_facts, 4 * lay + 2 + n // C)
                    last = nc.tensor.matmul(bank[6][:, 0:96], rank_hot[:, n, :],
                                            facts[:, n, :, :].rearrange("p q e -> p (q e)"),
                                            start=(n == 0), stop=(n == 2 * C - 1))
                last.then_inc(s_slots, 1)
                pe.wait_ge(s_facts, 4 * lay + 4)
                for n in range(2 * C):
                    last = nc.tensor.matmul(bank[7][:, 160:192], rank_hot32[:, n, :], wfacts[:, n, :],
                                            start=(n == 0), stop=(n == 2 * C - 1))
                last.then_inc(s_slots, 1)

            def transpose_rows(e2, src):
                for k in range(4):
                    last = nc.tensor.transpose(bank[e2][:, 128 * k:128 * k + 128],
                                               src.rearrange("p (x k) -> p k x", k=4)[:, k, :], ident)
                return last

            def gate_up(e2, w):
                for half in range(2):
                    for k in range(4):
                        xt = XT[e2][:, 128 * k + 64 * half:128 * k + 64 * half + 64]
                        at = 1024 * half + 256 * k
                        first, end = half + k == 0, half + k == 4
                        nc.tensor.matmul(bank[2 + e2][0:64, 0:256], xt, w[:, at:at + 256], start=first, stop=end)
                        last = nc.tensor.matmul(bank[2 + e2][64:128, 0:256], xt, w[:, 2048 + at:2304 + at],
                                                start=first, stop=end)
                return last

            def hidden_transposes(e2):
                for c in range(2):
                    last = nc.tensor.transpose(bank[4][:, 128 * c:128 * c + 128],
                                               hid[e2].rearrange("p (x c) -> p c x", c=2)[:, c, :], ident)
                return last

            def down(e2, d):
                for c in range(2):
                    nc.tensor.matmul(bank[5 + e2][0:64, :], hT[e2][:, 64 * c:64 * c + 64],
                                     d[:, 1024 * c:1024 * c + 512], start=(c == 0), stop=(c == 1))
                    last = nc.tensor.matmul(bank[5 + e2][64:128, :], hT[e2][:, 64 * c:64 * c + 64],
                                            d[:, 1024 * c + 512:1024 * c + 1024], start=(c == 0), stop=(c == 1))
                return last

            def experts(lay):
                base = NE * lay
                pe.wait_ge(s_g[0], 16 * (8 * lay + 1))
                transpose_rows(0, Xg[0]).then_inc(s_xt, 1)

                def step(e, s, gate_up_w, down_w, landed, down_landed, more, wait_out=True):
                    e2 = s % 2
                    pe.wait_ge(*landed)
                    pe.wait_ge(s_xte, e + (base + 1))
                    gate_up(e2, gate_up_w).then_inc(s_gu, 1)
                    if more:
                        s1 = (s + 1) % 4
                        turn = e * 4 + (16 * 8 * lay + 16 - 4 * s + (16 if s == 3 else 0))
                        pe.wait_ge(s_g[s1], turn)
                        transpose_rows(1 - e2, Xg[s1]).then_inc(s_xt, 1)
                    pe.wait_ge(s_hid, e + (base + 1))
                    hidden_transposes(e2).then_inc(s_ht, 1)
                    pe.wait_ge(s_hte, e + (base + 1))
                    pe.wait_ge(*down_landed)
                    if wait_out:
                        pe.wait_ge(s_ye, e + (base - 1))
                    down(e2, down_w).then_inc(s_y, 1)

                ring_turns = (NE - len(BESIDE)) // 4

                def numbered(e):
                    if e in BESIDE:
                        i, turns = e % 2, 2 * lay + BESIDE.index(e) // 2 + 1
                        slot_ = WB[i], DB[i], (s_lb[i], 48 * turns), (s_dnb[i], 16 * turns)
                    else:
                        n = expert_tile(lay, e)
                        turns = ring_turns * lay + (n - T_MOE[lay]) // 4 + 1
                        slot_ = W[n % 4], D[n % 4], (s_ld[n % 4], tile_ready(n)), (s_dn[n % 4], 16 * turns)
                    step(e, e % 4, *slot_, e + 1 < NE, base + e >= 2)

                for e in range(LOOP0):
                    numbered(e)
                with pe.Fori(LOOP0, NE - 4, 4) as e:
                    for s in range(4):
                        landed = s_ld[s], e * 12 + (tile_ready(expert_tile(lay, LOOP0 + s)) - 12 * LOOP0)
                        down_landed = s_dn[s], e * 4 + 16 * (ring_turns * lay + (LOOP0 - len(BESIDE)) // 4 + 1) - 4 * LOOP0
                        step(e + s, s, W[s], D[s], landed, down_landed, True)
                for e in range(NE - 4, NE):
                    numbered(e)

            def further_tiles(lay):
                o_ = ov[lay]
                pe.wait_ge(s_ncell, lay + 1)
                n_over = pe.value_load(ncells[0:1, 0:1], min_val=0, max_val=MAXOV)
                with pe.If(n_over > 0):
                    with pe.Fori(0, n_over) as o:
                        pe.wait_ge(o_["gathered"], o * 16 + 16)
                        transpose_rows(0, Xg[0]).then_inc(o_["xt"], 1)
                        pe.wait_ge(o_["loaded"], o * 48 + 48)
                        pe.wait_ge(o_["xte"], o + 1)
                        gate_up(0, W[0]).then_inc(o_["gu"], 1)
                        pe.wait_ge(o_["hid"], o + 1)
                        hidden_transposes(0).then_inc(o_["ht"], 1)
                        pe.wait_ge(o_["hte"], o + 1)
                        pe.wait_ge(o_["down"], o * 16 + 16)
                        down(0, D[0]).then_inc(o_["y"], 1)

            for c in range(C):
                transpose_normed(0, c)
            norm_ready(0)
            project_features(0, 4)
            pe.wait_ge(s_small, 16)
            for k in range(KD):
                last = nc.tensor.matmul(bank[5][0:8, :], zf_w[:, k, :], hnT[:, k, :], start=(k == 0), stop=(k == KD - 1))
            last.then_inc(s_zf, 1)
            project_features(1, 4)
            first_scores(DIL, 8, 32)
            project_rows(2, 0, 512, 1)
            attention(DIL, 12)
            for n in range(3, 5):
                project_features(n, 4)
            first_scores(FOX, 20, 80)
            project_rows(5, 0, 512, 1)
            attention(FOX, 24)
            mixer_out(0, 6)
            routing(0)
            experts(0)
            further_tiles(0)

            def latent_rows(c):
                pe.wait_ge(s_ntA, 4 * 2 + c + 1)
                pe.wait_ge(s_ntV, 4 * 2 + c + 1)
                project_rows(T_ODD, 0, 512, 1, [c])

            for c in range(C):
                transpose_normed(2, c)
                if c:
                    latent_rows(c - 1)
            latent_rows(C - 1)
            project_rows(T_ODD + 1, 0, QR + KVR + ROPE - 512, 2)
            project_features(T_ODD + 2, 4)
            project_features(T_ODD + 3, 1)
            first_scores(SWA, 35, 112)
            project_rows(T_ODD + 3, 128, 128, 4)
            for c in range(C):
                pe.wait_ge(s_lrow, c + 1)
                if c:
                    pe.wait_ge(s_ltA, c)
                    pe.wait_ge(s_ltV, c)
                for k in range(4):
                    last = nc.tensor.transpose(bank[3][:, 128 * k:128 * k + 128], cq_row[:, c, 128 * k:128 * k + 128], ident)
                last.then_inc(s_lt, 1)
                nc.tensor.transpose(bank[4][:, 0:128], cq_row[:, c, 512:640], ident)
                nc.tensor.transpose(bank[4][:, 128:256], kpe_pad[:, c, :], ident).then_inc(s_lt, 1)
            pe.wait_ge(s_ltA, C)
            pe.wait_ge(s_ltV, C)
            attention(SWA, 36)
            pe.wait_ge(s_perm, 2)
            uq = W[(T_ODD + 4) % 4][:, 0:3072].rearrange("p (k h n) -> p k h n", k=3, h=H)
            for hh in range(H):
                b = group_start()
                for k in range(3):
                    last = nc.tensor.matmul(b[:, :], uq[:, k, hh, :], hnT[:, k, :], start=(k == 0), stop=(k == 2))
                last.then_inc(s_pj, 1)
            t = T_ODD + 5
            pe.wait_ge(s_ld[t % 4], tile_ready(t))
            ukv = W[t % 4][:, 0:2048].rearrange("p (k h n) -> p k h n", k=2, h=H)
            for pair in range(4):
                b = group_start()
                for k in range(2):
                    for a in range(2):
                        last = nc.tensor.matmul(b[64 * a:64 * a + 64, :], ukv[:, k, 2 * pair + a, 0:64],
                                                hnT[:, 3 + k, :], start=(k == 0), stop=(k == 1))
                last.then_inc(s_pj, 1)
            pe.wait_ge(s_perm, 4)
            first_scores(MLA, 48, 112)
            for c in range(C):
                b = group_start()
                for k in range(2):
                    last = nc.tensor.matmul(b[:, :].rearrange("p (h n) -> p h n", h=H),
                                            hnT[:, 3 + k, 128 * c:128 * c + 128], ukv[:, k, :, 64:128],
                                            start=(k == 0), stop=(k == 1))
                last.then_inc(s_pj, 1)
            attention(MLA, 52)
            mixer_out(1, T_ODD + 6)
            routing(1)
            experts(1)
            further_tiles(1)

        @block.scalar
        def _(act):
            order = [0]
            group = [0]

            def then(ins):
                order[0] += 1
                ins.then_inc(s_av, 1)
                act.wait_ge(s_av, order[0])

            def chunk_ready(v, c):
                if v == 0:
                    return s_x[c], 16
                if v % 2:
                    return s_oga, 8 * (v // 2) + 5 + c
                return s_yadd, 4 * (v // 2 - 1) + 1 + c

            def norm(v):
                if v % 2 == 0:
                    nc.scalar.activation(warm[:, v // 2:v // 2 + 1], eps[0:1, 0:1], ACT.Sqrt)
                for c in range(C):
                    n = 4 * v + c + 1
                    act.wait_ge(*chunk_ready(v, c))
                    nc.scalar.activation(junk, h[:, c, :], ACT.Square, accum_out=ssq[:, c:c + 1]).then_inc(s_sq, 1)
                    act.wait_ge(s_sq, n)
                    nc.scalar.activation(rstd[:, c:c + 1], ssq[:, c:c + 1], ACT.Sqrt, scale=1.0 / DM, bias=eps[:, 0:1])\
                      .then_inc(s_sqrt, 1)
                    behind = 1 if v else 2
                    if v <= 3 and c >= behind:
                        norm_out(v, c - behind)
                if v <= 3:
                    for c in range(C - behind, C):
                        norm_out(v, c)

            def norm_out(v, c):
                act.wait_ge(s_nt, 8 * v + 2 * c + 1)
                nc.scalar.activation(hnT[:, 0:4, 128 * c:128 * c + 128],
                                     bank[3][:, :].rearrange("p (k t) -> p k t", k=4), ACT.Copy).then_inc(s_ntA, 1)

            def next_group():
                g = group[0]
                act.wait_ge(s_pj, g + 1)
                group[0] += 1
                return bank[6 + g % 2]

            def features_out(dst, scale, heads):
                for hh in range(0, heads, 2):
                    b = next_group()
                    nc.scalar.activation(dst[0:64, hh, :], b[0:64, :], ACT.Copy, scale=scale).then_inc(s_pjA, 1)

            def rows_out():
                for c in range(C):
                    b = next_group()
                    nc.scalar.activation(V[0:64, c, :], b[0:64, :], ACT.Copy).then_inc(s_pjA, 1)

            def exps(f, u):
                for i in range(4):
                    b = 4 * (H * f + u) + i
                    act.wait_ge(s_msk, b + 1)
                    if f == SWA:
                        nc.scalar.activation(esink[:, b % 8:b % 8 + 1], sinks[:, u:u + 1], ACT.Exp,
                                             bias=nm[:, b % 8:b % 8 + 1])
                    blk = P[:, u % 2, p_col(f, i):p_col(f, i) + LEN[f][i]]
                    nc.scalar.activation(blk, blk, ACT.Exp, bias=nm[:, b % 8:b % 8 + 1], scale=-1.0,
                                         accum_out=den[:, b % 8:b % 8 + 1]).then_inc(s_exp, 1)

            def probs_out(f, u):
                g = H * f + u
                for j in (0, 2):
                    act.wait_ge(s_tr, 4 * g + j + 1)
                    if g >= 2:
                        act.wait_ge(s_pv, g // 2)
                    n = 128 * len(q_chunks(f, j))
                    nc.scalar.activation(PTs[u % 2][:, pt_col(f, j):pt_col(f, j) + n], bank[pt_bank[j]][:, 0:n],
                                         ACT.Copy).then_inc(s_teA, 1)

            def pair_out(f, u):
                act.wait_ge(s_pv, (H * f + u) // 2 + 1)
                chunk = u // 2 + (4 if f in (DIL, SWA) else 0)
                nc.scalar.activation(oT[:, chunk, :], bank[5][:, :], ACT.Copy).then_inc(s_oev, 1)

            def first_exps(f):
                exps(f, 0)
                exps(f, 1)

            def attention(f):
                for u in range(H):
                    probs_out(f, u)
                    if u + 2 < H:
                        exps(f, u + 2)
                    if u % 2:
                        pair_out(f, u - 1)

            def routing(lay):
                act.wait_ge(s_rsub, 2 * lay + 1)
                nc.scalar.activation(gexp, gexp, ACT.Exp).then_inc(s_rexp, 1)
                act.wait_ge(s_rsub, 2 * lay + 2)
                nc.scalar.activation(ed, ed, ACT.Exp).then_inc(s_rexp, 1)

            def silu(e2, done):
                nc.scalar.activation(sil[e2][64:128, :], bank[2 + e2][0:64, 0:256], ACT.Silu).then_inc(done, 1)

            def hidden_out(e2, done):
                nc.scalar.activation(hT[e2].rearrange("p (c t) -> p c t", c=2),
                                     bank[4][:, 0:256].rearrange("p (c t) -> p c t", c=2)[:, :, 64:128],
                                     ACT.Copy).then_inc(done, 1)

            def experts(lay):
                base = NE * lay
                with act.Fori(0, NE, 2) as e:
                    for e2 in range(2):
                        act.wait_ge(s_gu, e + (base + e2 + 1))
                        silu(e2, s_sil)
                        act.wait_ge(s_ht, e + (base + e2 + 1))
                        hidden_out(e2, s_hte)

            def further_tiles(lay):
                o_ = ov[lay]
                act.wait_ge(s_ncell, lay + 1)
                n_over = act.value_load(ncells[0:1, 0:1], min_val=0, max_val=MAXOV)
                with act.If(n_over > 0):
                    with act.Fori(0, n_over) as o:
                        act.wait_ge(o_["gu"], o + 1)
                        silu(0, o_["sil"])
                        act.wait_ge(o_["ht"], o + 1)
                        hidden_out(0, o_["hte"])

            act.wait_ge(s_const, 16)
            norm(0)
            features_out(Q, -0.125, H)
            act.wait_ge(s_zfv, 2)
            then(nc.scalar.activation(zf[2], zf[1], ACT.Exp))
            nc.scalar.activation(zf[1], zf[2], ACT.Ln, bias=1.0).then_inc(s_zfa, 1)
            features_out(K, 1.0, H)
            first_exps(DIL)
            rows_out()
            attention(DIL)
            features_out(Q, -0.125, H)
            features_out(K, 1.0, H)
            first_exps(FOX)
            rows_out()
            attention(FOX)
            norm(1)
            routing(0)
            experts(0)
            further_tiles(0)
            norm(2)
            for c in range(C):
                b = next_group()
                nc.scalar.activation(cq_row[0:64, c, 0:512], b[0:64, :], ACT.Copy).then_inc(s_pjA, 1)
            for c in (0, 2):
                b = next_group()
                nc.scalar.activation(cq_row[0:64, c:c + 2, 512:672],
                                     b[0:64, 0:320].rearrange("p (c n) -> p c n", c=2), ACT.Copy).then_inc(s_pjA, 1)
            act.wait_ge(s_pjA, 30)
            act.wait_ge(s_pjV, 30)
            for c in range(C):
                nc.scalar.activation(junk[:, 0:QR], cq_row[:, c, 0:QR], ACT.Square, accum_out=ssq[:, c:c + 1])\
                  .then_inc(s_lsq, 1)
                nc.scalar.activation(junk[:, 512:512 + KVR], cq_row[:, c, QR:QR + KVR], ACT.Square,
                                     accum_out=ssq[:, 4 + c:5 + c]).then_inc(s_lsq, 1)
                act.wait_ge(s_lsq, 2 * c + 2)
            act.wait_ge(s_lms, 1)
            nc.scalar.activation(rstd[:, :], ssq[:, :], ACT.Sqrt).then_inc(s_lrt, 1)
            features_out(Q, -0.125, H)
            features_out(K, 1.0, 2)
            first_exps(SWA)
            b = next_group()
            nc.scalar.activation(V[0:64, :, 0:128], b[0:64, :].rearrange("p (c n) -> p c n", c=C), ACT.Copy)\
              .then_inc(s_pjA, 1)
            for c in range(C):
                act.wait_ge(s_lt, 2 * c + 1)
                nc.scalar.activation(hnT[:, 0:4, 128 * c:128 * c + 128],
                                     bank[3][:, :].rearrange("p (k t) -> p k t", k=4), ACT.Copy).then_inc(s_ltA, 1)
            attention(SWA)
            for hh in range(H):
                b = next_group()
                nc.scalar.activation(Q[0:64, hh, :], b[0:64, :], ACT.Copy, scale=-((NOPE + ROPE) ** -0.5))\
                  .then_inc(s_pjA, 1)
            features_out(K, 1.0, H)
            first_exps(MLA)
            rows_out()
            attention(MLA)
            norm(3)
            routing(1)
            experts(1)
            further_tiles(1)
            norm(4)

        @block.vector
        def _(dve):
            order = [0]
            group = [0]

            def then(ins):
                order[0] += 1
                ins.then_inc(s_dv, 1)
                dve.wait_ge(s_dv, order[0])

            def norm_chunk(v, c):
                dve.wait_ge(s_sqrt, 4 * v + c + 1)
                then(nc.vector.reciprocal(rstd[:, c:c + 1], rstd[:, c:c + 1]))
                if c == 0:
                    dve.wait_ge(s_gain, 16 * (v + 1))
                nc.vector.scalar_tensor_tensor(hn_row[:, c, :], h[:, c, :], rstd[:, c:c + 1], gain,
                                               ALU.mult, ALU.mult).then_inc(s_hn, 1)

            def norm_out(v, c):
                dve.wait_ge(s_nt, 8 * v + 2 * c + 2)
                nc.vector.tensor_copy(hnT[:, 4:8, 128 * c:128 * c + 128],
                                      bank[4][:, :].rearrange("p (k t) -> p k t", k=4)).then_inc(s_ntV, 1)

            def next_group():
                g = group[0]
                dve.wait_ge(s_pj, g + 1)
                group[0] += 1
                return bank[6 + g % 2]

            def features_out(dst, scale, heads):
                for hh in range(1, heads, 2):
                    b = next_group()
                    nc.vector.tensor_scalar(dst[0:64, hh, :], b[64:128, :], scale, None, ALU.mult).then_inc(s_pjV, 1)

            def rows_out():
                for c in range(C):
                    b = next_group()
                    nc.vector.tensor_copy(V[64:128, c, :], b[64:128, :]).then_inc(s_pjV, 1)

            def masks(f, u):
                g = H * f + u
                if g >= 2:
                    dve.wait_ge(s_tr, 4 * (g - 1))
                at, width = MASK[f]
                for i in range(4):
                    b, n = 4 * g + i, LEN[f][i]
                    dve.wait_ge(s_qk, b + 1)
                    start = sinks[:, H + u:H + u + 1] if f == SWA else 3e38
                    nc.vector.tensor_tensor_reduce(
                        out=P[:, u % 2, p_col(f, i):p_col(f, i) + n], in0=bank[b % 3][:, 0:n],
                        in1=cst[:, at + width - n:at + width], scale=1.0, scalar=start,
                        op0=ALU.add, op1=ALU.min, accum_out=nm[:, b % 8:b % 8 + 1]).then_inc(s_msk, 1)

            def normalise(f, u):
                g = H * f + u
                dve.wait_ge(s_exp, 4 * g + 4)
                sums = slice(4 * (g % 2), 4 * (g % 2) + 4)
                if f == SWA:
                    then(nc.vector.tensor_tensor(den[:, sums], den[:, sums], esink[:, sums], ALU.add))
                then(nc.vector.reciprocal(rden[:, sums], den[:, sums]))
                for i in range(4):
                    b = 4 * (H * f + u) + i
                    blk = P[:, u % 2, p_col(f, i):p_col(f, i) + LEN[f][i]]
                    nc.vector.tensor_scalar(blk, blk, rden[:, b % 8:b % 8 + 1], None, ALU.mult).then_inc(s_nrm, 1)

            def probs_out(f, u):
                g = H * f + u
                for j in (1, 3):
                    dve.wait_ge(s_tr, 4 * g + j + 1)
                    if g >= 2:
                        dve.wait_ge(s_pv, g // 2)
                    n = 128 * len(q_chunks(f, j))
                    nc.vector.tensor_copy(PTs[u % 2][:, pt_col(f, j):pt_col(f, j) + n],
                                          bank[pt_bank[j]][:, 0:n]).then_inc(s_teV, 1)

            def first_probs(f):
                masks(f, 0)
                masks(f, 1)
                normalise(f, 0)
                normalise(f, 1)

            def attention(f):
                for u in range(0, H, 2):
                    for a in range(2):
                        probs_out(f, u + a)
                        if u + 2 < H:
                            masks(f, u + 2 + a)
                    if u + 2 < H:
                        normalise(f, u + 2)
                        normalise(f, u + 3)

            def mixer_add(lay):
                for half in range(2):
                    for c in range(C):
                        g = 8 * lay + 4 * half + c
                        dve.wait_ge(s_og, g + 1)
                        part = h[:, c, 512 * half:512 * half + 512]
                        nc.vector.tensor_tensor(part, bank[g % 2][:, :], part, ALU.add).then_inc(s_oga, 1)
                        if half:
                            if c:
                                norm_out(2 * lay + 1, c - 1)
                            norm_chunk(2 * lay + 1, c)
                norm_out(2 * lay + 1, C - 1)

            def first_at(value, best, score, at_best, onehot):
                n = value.shape[2]
                bb = best.unsqueeze(2).to_broadcast([128, C, n])
                io = iota[:, 0:n].unsqueeze(1).to_broadcast([128, C, n])
                then(nc.vector.tensor_tensor(score, value, bb, ALU.is_ge))
                then(nc.vector.scalar_tensor_tensor(score, score, -64.0, io, ALU.mult, ALU.add))
                then(nc.vector.tensor_reduce(at_best, score, X, ALU.min))
                then(nc.vector.tensor_tensor(onehot, score, at_best.unsqueeze(2).to_broadcast([128, C, n]),
                                             ALU.is_equal))

            def routing(lay):
                nc.vector.tensor_copy(tri_ones, cst[:, C_TRI:C_ONE + 128])
                dve.wait_ge(s_lg, C * (lay + 1))
                then(nc.vector.tensor_tensor(lg, bank[6][:, 0:144].rearrange("p (c n) -> p c n", c=C),
                                             rbias.unsqueeze(1).to_broadcast([128, C, 36]), ALU.add))
                glog = lg[:, :, 0:4]
                then(nc.vector.tensor_reduce(gmax, glog, X, ALU.max))
                nc.vector.tensor_tensor(gexp, glog, gmax.unsqueeze(2).to_broadcast([128, C, 4]), ALU.subtract)\
                  .then_inc(s_rsub, 1)
                first_at(glog, gmax, gpick, gmin, goh)
                then(nc.vector.tensor_scalar(gpen, goh, BIG, -BIG, ALU.mult, ALU.add))
                e4 = em[0].rearrange("p c (g e) -> p c g e", g=4)
                then(nc.vector.tensor_tensor(e4, lg[:, :, 4:36].rearrange("p c (g e) -> p c g e", g=4),
                                             goh.unsqueeze(3).to_broadcast([128, C, 4, 8]), ALU.mult))
                then(nc.vector.tensor_tensor(e4, e4, gpen.unsqueeze(3).to_broadcast([128, C, 4, 8]), ALU.add))
                then(nc.vector.tensor_reduce(emax[0], em[0], X, ALU.max))
                first_at(em[0], emax[0], pick[0], emin[0], oh[0])
                then(nc.vector.scalar_tensor_tensor(em[1], oh[0], -3 * BIG, em[0], ALU.mult, ALU.add))
                then(nc.vector.tensor_reduce(emax[1], em[1], X, ALU.max))
                first_at(em[1], emax[1], pick[1], emin[1], oh[1])
                nc.vector.tensor_tensor(ed, emax[1], emax[0], ALU.subtract).then_inc(s_rsub, 1)
                nc.vector.tensor_tensor(ohs, oh[0], oh[1], ALU.add).then_inc(s_oh, 1)
                for k in range(2):
                    part = facts[:, C * k:C * k + C]
                    for q in range(2):
                        ids = cst[:, C_TOK + 8 * q + C * k:C_TOK + 8 * q + C * k + C]
                        nc.vector.tensor_tensor(part[:, :, q, :], oh[k], ids.unsqueeze(2).to_broadcast([128, C, NE]),
                                                ALU.mult)
                    ins = nc.vector.tensor_copy(part[:, :, 2, :], oh[k])
                ins.then_inc(s_facts, 1)
                dve.wait_ge(s_rank, lay + 1)
                rank = bank[7][:, 0:128].rearrange("p (c n) -> p c n", c=C)
                for k in range(2):
                    ins = nc.vector.tensor_tensor(pick[k], rank, oh[k], ALU.mult)
                then(ins)
                for k in range(2):
                    ins = nc.vector.tensor_reduce(rpos[k], pick[k], X, ALU.add)
                then(ins)
                for k in range(2):
                    nc.vector.tensor_tensor(rank_hot[:, C * k:C * k + C, :],
                                                  cst[:, C_RANK:C_RANK + 128].unsqueeze(1).to_broadcast([128, C, 128]),
                                                  rpos[k].unsqueeze(2).to_broadcast([128, C, 128]), ALU.is_equal)\
                      .then_inc(s_facts, 1)
                dve.wait_ge(s_slots, 2 * lay + 1)
                found = bank[6][:, 0:96].rearrange("p (q e) -> p q e", q=3)
                then(nc.vector.tensor_scalar(pad, found[:, 2, :], -float(OOB), cst[:, C_OOB:C_OOB + 1],
                                             ALU.mult, ALU.add))
                nc.vector.tensor_tensor(gidx, found[:, 0, :], pad, ALU.add)
                nc.vector.tensor_tensor(sidx, found[:, 1, :], pad, ALU.add).then_inc(s_idx, 1)
                dve.wait_ge(s_rexp, 2 * lay + 2)
                then(nc.vector.tensor_reduce(gsum, gexp, X, ALU.add))
                nc.vector.tensor_scalar(esum, ed, 1.0, None, ALU.add)
                then(nc.vector.reciprocal(gw, gsum))
                then(nc.vector.reciprocal(einv, esum))
                then(nc.vector.tensor_tensor(wgt[:, 0, :], einv, gw, ALU.mult))
                then(nc.vector.tensor_tensor(wgt[:, 1, :], wgt[:, 0, :], ed, ALU.mult))
                recv = rec.rearrange("p (n w) -> p n w", w=4)
                ids = cst[:, C_TOK:C_TOK + 16].rearrange("p (w n) -> p n w", w=2)
                nc.vector.tensor_copy(recv[:, :, 0:2], ids)
                nc.vector.tensor_copy(recv.bitcast(f32)[:, :, 2:4],
                                      wgt.rearrange("p k c -> p (k c)").unsqueeze(2).to_broadcast([128, 8, 2]))
                for k in range(2):
                    ins = nc.vector.scalar_tensor_tensor(rslot[k], rpos[k], float(NE), emin[k], ALU.mult, ALU.add)
                then(ins)
                for k in range(2):
                    nc.vector.tensor_scalar(slot[:, 4 * k:4 * k + 4], rslot[k], 64.0, None, ALU.add)
                for k in range(2):
                    nc.vector.tensor_tensor(wfacts[:, C * k:C * k + C, :], oh[k],
                                            wgt[:, k, :].unsqueeze(2).to_broadcast([128, C, NE]), ALU.mult)
                    ins = nc.vector.tensor_tensor(rank_hot32[:, C * k:C * k + C, :],
                                                  cst[:, C_RANK:C_RANK + 128].unsqueeze(1).to_broadcast([128, C, 128]),
                                                  rpos[k].unsqueeze(2).to_broadcast([128, C, 128]), ALU.is_equal)
                ins.then_inc(s_facts, 1)

            def list_further_tiles(lay):
                dve.wait_ge(s_slots, 2 * lay + 2)
                nc.vector.tensor_copy(wtab, bank[7][:, 160:192])
                cnt = bank[7][0:1, 128:160]
                big = [ovbig[i].rearrange("p (a b) -> p a b", b=NE) for i in range(2)]
                b7 = ovbig[0][:, 0:224].rearrange("p (e t) -> p e t", t=7)
                then(nc.vector.tensor_copy(ends, cnt))
                then(nc.vector.tensor_tensor(b7, ends.unsqueeze(2).to_broadcast([1, NE, 7]),
                                             cst[0:1, C_THR:C_THR + 7].unsqueeze(1).to_broadcast([1, NE, 7]), ALU.is_gt))
                then(nc.vector.tensor_reduce(extra, b7, X, ALU.add))
                then(nc.vector.memset(ovbig[1][:, 0:NE], 0.0))
                then(nc.vector.tensor_tensor_scan(ends, extra, ovbig[1][:, 0:NE], 0.0, ALU.add, ALU.add))
                then(nc.vector.tensor_tensor(big[0], ends.unsqueeze(1).to_broadcast([1, MAXOV, NE]),
                                             cst[0:1, C_IOTA:C_IOTA + MAXOV].unsqueeze(2).to_broadcast([1, MAXOV, NE]),
                                             ALU.is_le))
                then(nc.vector.tensor_tensor(big[1], big[0], extra.unsqueeze(1).to_broadcast([1, MAXOV, NE]), ALU.mult))
                then(nc.vector.tensor_reduce(oe, big[0], X, ALU.add))
                then(nc.vector.tensor_reduce(ostart, big[1], X, ALU.add))
                then(nc.vector.tensor_tensor(ostart, cst[0:1, C_IOTA + 1:C_IOTA + 1 + MAXOV], ostart, ALU.subtract))
                nc.vector.tensor_copy(ncells[:, 0:1], ends[:, NE - 1:NE])
                nc.vector.tensor_copy(ncells[:, 1:1 + MAXOV], oe)
                nc.vector.tensor_copy(ncells[:, 1 + MAXOV:1 + 2 * MAXOV], ostart).then_inc(s_ncell, 1)

            def indices(gather_idx, scatter_idx, records, done):
                half = cst[:, C_OOB:C_OOB + 1]
                nc.vector.tensor_scalar(gather_idx, records[:, :, 0], half, -float(OOB), ALU.add, ALU.add)
                nc.vector.tensor_scalar(scatter_idx, records[:, :, 1], half, -float(OOB), ALU.add, ALU.add)\
                  .then_inc(done, 1)

            def hidden(e2, weight, done):
                nc.vector.scalar_tensor_tensor(hid[e2][64:128, :], bank[2 + e2][64:128, 0:256], weight,
                                               sil[e2][64:128, :], ALU.mult, ALU.mult).then_inc(done, 1)

            def experts(lay):
                base = NE * lay
                dve.wait_ge(s_xt, base + 1)
                nc.vector.tensor_copy(XT[0], bank[0][:, :]).then_inc(s_xte, 1)
                list_further_tiles(lay)

                def step(e, s, wcol, more, scattered):
                    e2 = s % 2
                    dve.wait_ge(s_sil, e + (base + 1))
                    hidden(e2, wtab[64:128, wcol], s_hid)
                    if more:
                        dve.wait_ge(s_xt, e + (base + 2))
                        nc.vector.tensor_copy(XT[1 - e2], bank[1 - e2][:, :]).then_inc(s_xte, 1)
                    dve.wait_ge(s_y, e + (base + 1))
                    if scattered is not None:
                        dve.wait_ge(s_sc[s], scattered)
                    nc.vector.tensor_copy(Y[s], bank[5 + e2][:, :]).then_inc(s_ye, 1)

                before = 16 * 8 * lay
                for e in range(4):
                    step(e, e, slice(e, e + 1), True, before if lay else None)
                with dve.Fori(4, NE - 4, 4) as e0:
                    for s in range(4):
                        e = dve.snap(e0 + s)
                        step(e, s, bass.ds(e, 1), True, e0 * 4 + before)
                for s in range(4):
                    e = NE - 4 + s
                    step(e, s, slice(e, e + 1), s < 3, 4 * (NE - 4) + before)

            def further_tiles(lay):
                o_ = ov[lay]
                n_over = dve.value_load(ncells[0:1, 0:1], min_val=0, max_val=MAXOV)
                with dve.If(n_over > 0):
                    dve.wait_ge(s_sc[0], 16 * 8 * (lay + 1))
                    with dve.Fori(0, n_over) as o:
                        dve.wait_ge(o_["records"], o * 32 + 32)
                        indices(oidx[:, 0:1], oidx[:, 1:2], orec.unsqueeze(1), o_["indices"])
                        dve.wait_ge(o_["xt"], o + 1)
                        nc.vector.tensor_copy(XT[0], bank[0][:, :]).then_inc(o_["xte"], 1)
                        dve.wait_ge(o_["sil"], o + 1)
                        hidden(0, orec.bitcast(f32)[64:128, 2:3], o_["hid"])
                        dve.wait_ge(o_["y"], o + 1)
                        nc.vector.tensor_copy(Y[0], bank[5][:, :]).then_inc(o_["ye"], 1)

            def add_expert_rows(lay):
                for c in range(C):
                    dve.wait_ge(s_yld[c], 16 * (lay + 1))
                    then(nc.vector.tensor_tensor(h[:, c, :], h[:, c, :], y_in[c][:, 0:DM], ALU.add))
                    if c == 0:
                        dve.wait_ge(s_yhalf, 16 * (lay + 1))
                    nc.vector.tensor_tensor(h[:, c, :], h[:, c, :], y_in[c][:, DM:2 * DM], ALU.add).then_inc(s_yadd, 1)
                    if c:
                        norm_chunk(2 * lay + 2, c - 1)
                    if c >= 2 and lay == 0:
                        norm_out(2, c - 2)
                norm_chunk(2 * lay + 2, C - 1)
                if lay == 0:
                    for c in range(C - 2, C):
                        norm_out(2, c)

            dve.wait_ge(s_const, 16)
            for c in range(C):
                norm_chunk(0, c)
                if c:
                    norm_out(0, c - 1)
            norm_out(0, C - 1)
            features_out(Q, -0.125, H)
            dve.wait_ge(s_heads, 32)
            nc.vector.tensor_scalar(sinks[:, H:2 * H], sinks[:, 0:H], -1.0, None, ALU.mult)
            dve.wait_ge(s_zf, 1)
            nc.vector.tensor_scalar(zf[0], bank[5][0:8, :], bf_sb[:, 0:1], None, ALU.add).then_inc(s_zfv, 1)
            dve.wait_ge(s_zfv, 1)
            nc.vector.scalar_tensor_tensor(zf[1], zf[0], -1.0, zf[0], ALU.mult, ALU.min).then_inc(s_zfv, 1)
            dve.wait_ge(s_zfa, 1)
            nc.vector.scalar_tensor_tensor(zf[0], zf[0], 0.0, zf[1], ALU.min, ALU.subtract).then_inc(s_zfv, 1)
            dve.wait_ge(s_zfv, 3)
            then(nc.vector.memset(zf[1], 0.0))
            nc.vector.tensor_tensor_scan(zf[2], zf[0], zf[1], 0.0, ALU.add, ALU.add).then_inc(s_zfv, 1)
            dve.wait_ge(s_zfv, 4)
            nc.vector.tensor_scalar(zf[3], zf[2], -1.0, None, ALU.mult).then_inc(s_zfv, 1)
            features_out(K, 1.0, H)
            dve.wait_ge(s_masks, 16)
            first_probs(DIL)
            rows_out()
            attention(DIL)
            features_out(Q, -0.125, H)
            features_out(K, 1.0, H)
            first_probs(FOX)
            rows_out()
            attention(FOX)
            mixer_add(0)
            routing(0)
            experts(0)
            further_tiles(0)
            add_expert_rows(0)
            for c in range(C):
                b = next_group()
                nc.vector.tensor_copy(cq_row[64:128, c, 0:512], b[64:128, :]).then_inc(s_pjV, 1)
            for c in (0, 2):
                b = next_group()
                nc.vector.tensor_copy(cq_row[64:128, c:c + 2, 512:672],
                                      b[64:128, 0:320].rearrange("p (c n) -> p c n", c=2)).then_inc(s_pjV, 1)
            dve.wait_ge(s_pjA, 30)
            dve.wait_ge(s_pjV, 30)
            dve.wait_ge(s_small, 128)
            t1, t2 = cq_row[:, :, 640:656], cq_row[:, :, 656:672]
            for a, (t, cs) in enumerate(((t1, 0), (t2, 1), (t1, 1), (t2, 0))):
                nc.vector.tensor_tensor(ktmp[:, a, :, :], t, krot[:, cs, :, :], ALU.mult)
            then(nc.vector.memset(kpe_pad[:, :, 0:64], 0.0))
            for at in (64, 96):
                nc.vector.tensor_tensor(kpe_pad[:, :, at:at + 16], ktmp[:, 0], ktmp[:, 1], ALU.subtract)
                nc.vector.tensor_tensor(kpe_pad[:, :, at + 16:at + 32], ktmp[:, 2], ktmp[:, 3], ALU.add)
            dve.wait_ge(s_lsq, 8)
            nc.vector.tensor_scalar(ssq[:, 0:4], ssq[:, 0:4], 1.0 / QR, 1e-6, ALU.mult, ALU.add)
            nc.vector.tensor_scalar(ssq[:, 4:8], ssq[:, 4:8], 1.0 / KVR, 1e-6, ALU.mult, ALU.add).then_inc(s_lms, 1)
            dve.wait_ge(s_lrt, 1)
            then(nc.vector.reciprocal(rstd[:, :], rstd[:, :]))
            for c in range(C):
                nc.vector.scalar_tensor_tensor(cq_row[:, c, 0:QR], cq_row[:, c, 0:QR], rstd[:, c:c + 1],
                                               qkv_gain[:, 0:QR], ALU.mult, ALU.mult)
                nc.vector.scalar_tensor_tensor(cq_row[:, c, QR:QR + KVR], cq_row[:, c, QR:QR + KVR], rstd[:, 4 + c:5 + c],
                                               qkv_gain[:, QR:QR + KVR], ALU.mult, ALU.mult).then_inc(s_lrow, 1)
            features_out(Q, -0.125, H)
            features_out(K, 1.0, 2)
            first_probs(SWA)
            b = next_group()
            nc.vector.tensor_copy(V[64:128, :, 0:128], b[64:128, :].rearrange("p (c n) -> p c n", c=C)).then_inc(s_pjV, 1)
            for c in range(C):
                dve.wait_ge(s_lt, 2 * c + 2)
                nc.vector.tensor_copy(hnT[:, 4, 128 * c:128 * c + 128], bank[4][:, 0:128])
                nc.vector.tensor_copy(kpe_T[:, 128 * c:128 * c + 128], bank[4][64:128, 128:256]).then_inc(s_ltV, 1)
            attention(SWA)
            dve.wait_ge(s_small, 144)
            for hh in range(H):
                b = next_group()
                nc.vector.tensor_tensor(Q[64:128, hh, :], b[64:128, :], qrot[64:128, :], ALU.mult).then_inc(s_pjV, 1)
            features_out(K, 1.0, H)
            first_probs(MLA)
            rows_out()
            attention(MLA)
            mixer_add(1)
            routing(1)
            experts(1)
            further_tiles(1)
            add_expert_rows(1)


_INS = ["x", "attn_norm", "ffn_norm", "final_norm", "e_w_in", "e_b_f", "e_w_out", "o_w_in", "o_q_norm", "o_kv_norm",
        "o_w_uq", "o_w_ukv", "o_sinks", "o_w_out", "moe_w_group", "moe_b_group", "moe_w_router", "moe_b_router",
        "moe_w_gate", "moe_w_up", "moe_w_down"]


def kernel(**inputs):
    import concourse.bacc as bacc
    from concourse.bass_utils import run_bass_kernel_spmd

    nc = bacc.Bacc("TRN2", target_bir_lowering=False, num_devices=1)
    arrays, args = {}, []
    consts = shape_constants()
    for name in _INS + list(consts):
        a = np.ascontiguousarray(inputs[name] if name in inputs else consts[name])
        arrays[f"in_{name}"] = a
        args.append(nc.dram_tensor(f"in_{name}", a.shape, mybir.dt.from_np(a.dtype), kind="ExternalInput").ap())
    args.append(nc.dram_tensor("out_0", (1, S, DM), mybir.dt.float32, kind="ExternalOutput").ap())
    trunk(nc, *args)
    return run_bass_kernel_spmd(nc, [arrays], core_ids=[0]).results[0]["out_0"]
```
